# Optimizing a Trainium2 kernel written in Bass

```python
import math
import jax, jax.numpy as jnp
from jax import lax
import numpy as np

D_MODEL = 1024
BATCH = 1
SEQ = 1024
DEPTH = 1

D_MIX = D_MODEL
CONV_GROUPS = 4
CONV_WIDTH = D_MIX // 4
CONV_K = 3
SB_HEADS = 6
SB_HEAD_DIM = 64
SB_WIDTH = SB_HEADS * SB_HEAD_DIM
SB_BLOCK = 128
GLA_HEADS = 4
GLA_WIDTH = D_MIX - CONV_WIDTH - SB_WIDTH
GLA_DV = GLA_WIDTH // GLA_HEADS
GLA_DK = GLA_DV // 2
GLA_KEY_WIDTH = GLA_HEADS * GLA_DK
GLA_GATE_RANK = 16
GLA_GATE_NORM = 16.0
GLA_CHUNK = 64
PROJ_SIZES = (CONV_WIDTH, CONV_WIDTH, CONV_WIDTH,
              SB_WIDTH, SB_WIDTH, SB_WIDTH,
              GLA_KEY_WIDTH, GLA_KEY_WIDTH, GLA_WIDTH, GLA_WIDTH, GLA_GATE_RANK)
D_PROJ = 3 * CONV_WIDTH + 3 * SB_WIDTH + 2 * GLA_KEY_WIDTH + 2 * GLA_WIDTH + GLA_GATE_RANK
N_EXPERTS = 16
N_GROUPS = 4
EXPERTS_PER_GROUP = N_EXPERTS // N_GROUPS
TOP_K = 2
D_EXPERT = 512
ALPHA = (2 * DEPTH) ** 0.25
BETA = (8 * DEPTH) ** -0.25
LN_EPS = 1e-5
RMS_EPS = 1e-6

kernel_name = "hybrid_conv_sb_gla_grouped_moe_deepnorm"

def layer_norm(x, g, b):
    xf = x.astype(jnp.float32)
    mu = jnp.mean(xf, axis=-1, keepdims=True)
    var = jnp.mean(jnp.square(xf - mu), axis=-1, keepdims=True)
    return ((xf - mu) * lax.rsqrt(var + LN_EPS) * g + b).astype(x.dtype)

def split_projection(proj):
    idx = []
    acc = 0
    for s in PROJ_SIZES[:-1]:
        acc += s
        idx.append(acc)
    return jnp.split(proj, idx, axis=-1)

def short_conv_mixer(h, b_gate, c_gate, conv_w, conv_b):
    u = c_gate * h
    S = u.shape[1]
    u_pad = jnp.pad(u, ((0, 0), (CONV_K - 1, 0), (0, 0)))
    y = conv_b
    for i in range(CONV_K):
        y = y + conv_w[i] * u_pad[:, CONV_K - 1 - i:CONV_K - 1 - i + S]
    return b_gate * y

def stick_breaking_attention(q, k, v):
    Bsz, S, H, Dh = q.shape
    q = q.transpose(0, 2, 1, 3)
    k = k.transpose(0, 2, 1, 3)
    v = v.transpose(0, 2, 1, 3)
    scale = Dh ** -0.5
    outs = []
    for blk in range(S // SB_BLOCK):
        q0 = blk * SB_BLOCK
        q1 = q0 + SB_BLOCK
        qb = q[:, :, q0:q1]
        kb = k[:, :, :q1]
        vb = v[:, :, :q1]
        z = jnp.einsum('bhqd,bhkd->bhqk', qb, kb).astype(jnp.float32) * scale
        t_idx = jnp.arange(q0, q1)[:, None]
        s_idx = jnp.arange(q1)[None, :]
        causal = s_idx < t_idx
        log_beta = jax.nn.log_sigmoid(z)
        log_1m_beta = jnp.where(causal, jax.nn.log_sigmoid(-z), 0.0)
        incl = jnp.cumsum(log_1m_beta, axis=-1)
        later = incl[..., -1:] - incl
        a = jnp.where(causal, jnp.exp(log_beta + later), 0.0)
        outs.append(jnp.einsum('bhqk,bhkd->bhqd', a.astype(v.dtype), vb))
    o = jnp.concatenate(outs, axis=2)
    return o.transpose(0, 2, 1, 3)

def gla_mixer(q, k, v, g, gate_lr, w_gate2, b_gate, norm_w):
    Bsz, S, H, DK = q.shape
    DV = v.shape[-1]
    C = GLA_CHUNK
    nC = S // C
    log_a = jax.nn.log_sigmoid((gate_lr @ w_gate2 + b_gate).astype(jnp.float32)) / GLA_GATE_NORM
    log_a = log_a.reshape(Bsz, S, H, DK)

    def chunk(t):
        return t.reshape(Bsz, nC, C, H, -1).transpose(0, 3, 1, 2, 4)

    qc = chunk(q).astype(jnp.float32) * (DK ** -0.5)
    kc = chunk(k).astype(jnp.float32)
    vc = chunk(v).astype(jnp.float32)
    bcum = jnp.cumsum(chunk(log_a), axis=3)
    b_last = bcum[:, :, :, -1:]
    q_in = qc * jnp.exp(bcum)
    k_in = kc * jnp.exp(-bcum)
    k_to_end = kc * jnp.exp(b_last - bcum)
    scores = jnp.einsum('bhcid,bhcjd->bhcij', q_in, k_in)
    tri = jnp.tril(jnp.ones((C, C), dtype=bool))
    scores = jnp.where(tri, scores, 0.0)
    o_intra = jnp.einsum('bhcij,bhcje->bhcie', scores, vc)
    kv = jnp.einsum('bhcjd,bhcje->bhcde', k_to_end, vc)
    decay = jnp.exp(b_last[:, :, :, 0])

    def step(state, inp):
        kv_c, dec_c = inp
        return dec_c[..., None] * state + kv_c, state

    init = jnp.zeros((Bsz, H, DK, DV), jnp.float32)
    _, s_prev = lax.scan(step, init, (jnp.moveaxis(kv, 2, 0), jnp.moveaxis(decay, 2, 0)))
    s_prev = jnp.moveaxis(s_prev, 0, 2)
    o_inter = jnp.einsum('bhcid,bhcde->bhcie', q_in, s_prev)
    o = (o_intra + o_inter).transpose(0, 2, 3, 1, 4).reshape(Bsz, S, H, DV)
    o_n = o * lax.rsqrt(jnp.mean(jnp.square(o), axis=-1, keepdims=True) + RMS_EPS) * norm_w
    out = o_n * jax.nn.silu(g.astype(jnp.float32))
    return out.reshape(Bsz, S, H * DV).astype(v.dtype)

def grouped_moe(x, router_w, router_bias, w1, w3, w2):
    Bsz, S, D = x.shape
    t = x.reshape(-1, D)
    T = t.shape[0]
    scores = jax.nn.sigmoid((t @ router_w).astype(jnp.float32))
    sel = scores + router_bias.astype(jnp.float32)
    grp = sel.reshape(T, N_GROUPS, EXPERTS_PER_GROUP)
    grp_score = jnp.sum(lax.top_k(grp, 2)[0], axis=-1)
    _, top_group = lax.top_k(grp_score, 1)
    group_mask = jax.nn.one_hot(top_group[:, 0], N_GROUPS, dtype=jnp.bool_)
    expert_mask = jnp.repeat(group_mask, EXPERTS_PER_GROUP, axis=1)
    masked_sel = jnp.where(expert_mask, sel, -jnp.inf)
    _, top_idx = lax.top_k(masked_sel, TOP_K)
    top_w = jnp.take_along_axis(scores, top_idx, axis=1)
    top_w = top_w / jnp.sum(top_w, axis=-1, keepdims=True)
    gate = jnp.sum(jax.nn.one_hot(top_idx, N_EXPERTS, dtype=jnp.float32) * top_w[..., None], axis=1)
    gate = gate.astype(t.dtype)
    y = jnp.zeros_like(t)
    for e in range(N_EXPERTS):
        h = jax.nn.silu(t @ w1[e]) * (t @ w3[e])
        y = y + gate[:, e:e + 1] * (h @ w2[e])
    return y.reshape(Bsz, S, D)

def setup_inputs(seed: int = 0) -> dict:
    key = jax.random.key(seed)
    ks = jax.random.split(key, 20)
    f32 = jnp.float32
    nrm = lambda k, shape, s: jax.random.normal(k, shape, f32) * s
    x = nrm(ks[0], (BATCH, SEQ, D_MODEL), 1.0)
    w_in = nrm(ks[1], (DEPTH, D_MODEL, D_PROJ), D_MODEL ** -0.5)
    conv_w = nrm(ks[2], (DEPTH, CONV_K, CONV_WIDTH), CONV_K ** -0.5)
    conv_b = nrm(ks[3], (DEPTH, CONV_WIDTH), 0.01)
    gla_w_gate2 = nrm(ks[4], (DEPTH, GLA_GATE_RANK, GLA_KEY_WIDTH), GLA_GATE_RANK ** -0.5)
    gla_b_gate = nrm(ks[5], (DEPTH, GLA_KEY_WIDTH), 0.01)
    gla_norm_w = 1.0 + nrm(ks[6], (DEPTH, GLA_DV), 0.01)
    w_out = nrm(ks[7], (DEPTH, D_MIX, D_MODEL), D_MIX ** -0.5 * BETA)
    ln1_g = 1.0 + nrm(ks[8], (DEPTH, D_MODEL), 0.01)
    ln1_b = nrm(ks[9], (DEPTH, D_MODEL), 0.01)
    router_w = nrm(ks[10], (D_MODEL, N_EXPERTS), D_MODEL ** -0.5)
    router_bias = nrm(ks[11], (N_EXPERTS,), 0.01)
    w1 = nrm(ks[12], (DEPTH, N_EXPERTS, D_MODEL, D_EXPERT), D_MODEL ** -0.5)
    w3 = nrm(ks[13], (DEPTH, N_EXPERTS, D_MODEL, D_EXPERT), D_MODEL ** -0.5)
    w2 = nrm(ks[14], (DEPTH, N_EXPERTS, D_EXPERT, D_MODEL), D_EXPERT ** -0.5 * BETA)
    ln2_g = 1.0 + nrm(ks[15], (DEPTH, D_MODEL), 0.01)
    ln2_b = nrm(ks[16], (DEPTH, D_MODEL), 0.01)
    return {"x": x, "w_in": w_in, "conv_w": conv_w, "conv_b": conv_b,
            "gla_w_gate2": gla_w_gate2, "gla_b_gate": gla_b_gate, "gla_norm_w": gla_norm_w,
            "w_out": w_out, "ln1_g": ln1_g, "ln1_b": ln1_b,
            "router_w": router_w, "router_bias": router_bias,
            "w1": w1, "w3": w3, "w2": w2, "ln2_g": ln2_g, "ln2_b": ln2_b}

def reference(x, w_in, conv_w, conv_b, gla_w_gate2, gla_b_gate, gla_norm_w, w_out,
              ln1_g, ln1_b, router_w, router_bias, w1, w3, w2, ln2_g, ln2_b):
    Bsz, S, D = x.shape
    for l in range(DEPTH):
        proj = x @ w_in[l]
        (c_h, c_b, c_c, sb_q, sb_k, sb_v,
         g_q, g_k, g_v, g_g, g_lr) = split_projection(proj)
        y_conv = short_conv_mixer(c_h, c_b, c_c, conv_w[l], conv_b[l])
        y_sb = stick_breaking_attention(
            sb_q.reshape(Bsz, S, SB_HEADS, SB_HEAD_DIM),
            sb_k.reshape(Bsz, S, SB_HEADS, SB_HEAD_DIM),
            sb_v.reshape(Bsz, S, SB_HEADS, SB_HEAD_DIM)).reshape(Bsz, S, SB_WIDTH)
        y_gla = gla_mixer(
            g_q.reshape(Bsz, S, GLA_HEADS, GLA_DK),
            g_k.reshape(Bsz, S, GLA_HEADS, GLA_DK),
            g_v.reshape(Bsz, S, GLA_HEADS, GLA_DV),
            g_g.reshape(Bsz, S, GLA_HEADS, GLA_DV),
            g_lr, gla_w_gate2[l], gla_b_gate[l], gla_norm_w[l])
        mix = jnp.concatenate([y_conv, y_sb, y_gla], axis=-1) @ w_out[l]
        x = layer_norm(ALPHA * x + mix, ln1_g[l], ln1_b[l])
        ffn = grouped_moe(x, router_w, router_bias, w1[l], w3[l], w2[l])
        x = layer_norm(ALPHA * x + ffn, ln2_g[l], ln2_b[l])
    return x


_drawn_inputs = setup_inputs


def setup_inputs(seed=0):
    import zlib

    import numpy as np

    out = dict(_drawn_inputs(seed))
    spreads = {}
    factors = {'conv_b': 6.544, 'gla_b_gate': 7.431, 'gla_norm_w': 5.377, 'ln2_g': 5.728, 'ln2_b': 5.715}
    for name, (base, spread) in spreads.items():
        noise = np.random.default_rng([zlib.crc32(name.encode()), seed]).standard_normal(out[name].shape)
        drawn = base * np.exp(spread * noise) if base else spread * noise
        out[name] = __import__('jax').numpy.asarray(drawn.astype(out[name].dtype))
    for name, factor in factors.items():
        out[name] = (out[name] * factor).astype(out[name].dtype)
    return out
```

```python
import math

import concourse.bass as bass
from concourse import mybir
from contextlib import ExitStack

F32, F32R, BF16 = mybir.dt.float32, mybir.dt.float32r, mybir.dt.bfloat16
I32, U32 = mybir.dt.int32, mybir.dt.uint32
ALU = mybir.AluOpType
ACT = mybir.ActivationFunctionType
AX = mybir.AxisListType

P = 128
D = 1024
T = 1024
NT = T // P
NK = D // P
CONV_W = D // 4
CONV_K = 3
SB_H, SB_D = 6, 64
SB_W = SB_H * SB_D
GLA_H, GLA_DV, GLA_DK, GLA_R, GLA_C = 4, 96, 48, 16, 64
GLA_W = GLA_H * GLA_DV
GLA_KW = GLA_H * GLA_DK
OFF = {}
_at = 0
for _n, _s in (("c_h", CONV_W), ("c_b", CONV_W), ("c_c", CONV_W), ("sb_q", SB_W), ("sb_k", SB_W), ("sb_v", SB_W),
               ("g_q", GLA_KW), ("g_k", GLA_KW), ("g_v", GLA_W), ("g_g", GLA_W), ("g_lr", GLA_R)):
    OFF[_n] = _at
    _at += _s
D_PROJ = _at
GATE_NORM = 16.0
CLAMP = 40.0
RMS_EPS = 1e-6
LN_EPS = 1e-5
ALPHA = 2 ** 0.25
NPAIR = SB_H // 2

T_FIRST = [("gq", 0), ("gk", 0), ("gq", 1), ("gk", 1), ("sq", 0), ("sk", 0)]
N_PIECES = ["g_v", "g_g", "sb_v"]
FILL = [("sq", 1), ("sk", 1), ("cc", 0), ("ch", 0), ("sq", 2), ("sk", 2), ("cb", 0), ("cc", 1), ("ch", 1), ("cb", 1)]
NCHUNK_T = len(T_FIRST)
CHUNK_N0 = NCHUNK_T
CHUNK_F0 = NCHUNK_T + 3 * len(N_PIECES)
NCHUNK = CHUNK_F0 + len(FILL)
FILL_T0 = 0
FILL_N0 = 2 * NCHUNK_T
FILL_F0 = FILL_N0 + NT * len(N_PIECES)
NFILL = FILL_F0 + 2 * len(FILL)
GG_FIRST, GG_LAST = FILL_N0 + NT, FILL_N0 + 2 * NT

UNITS = [(p, i, h) for p in range(NPAIR) for i in range(NT) for h in range(2)]
NU = len(UNITS)
HALVES = [0]
for _p, _i, _h in UNITS:
    HALVES.append(HALVES[-1] + (1 if _i < 4 else 2))
QUARTER = {}
_q = 0
for _u, (_p, _i, _h) in enumerate(UNITS):
    if _i >= 1 and _q < 4 * len(FILL):
        QUARTER[_u] = _q
        _q += 1
assert _q == 4 * len(FILL)


def ev_before(f):
    return f - max(0, min(f, GG_LAST) - GG_FIRST)


def gg_before(f):
    return max(0, min(f, GG_LAST) - GG_FIRST)

NE, NGRP = 16, 4
EPG = NE // NGRP
DE = 512
NF = DE // P
TW = 160
TR = TW - P
MAXPASS = -(-T // TW)
NROW = MAXPASS * NE * TW
NPIECE = 3 * NF
BIG = float(1 << 20)


def build(nc, I, out):
    ctx = ExitStack()
    with ctx:
        base = 16512

        def at(name, offset, shape, dt=F32):
            return nc.alloc_sbuf_tensor_at(name, shape, dt, offset=base + offset)

        def sem(name):
            return ctx.enter_context(nc.semaphore(name))

        K = 1024
        xT_hi = at("xT_hi", 0, [P, NK, T], F32R)
        xT_lo = at("xT_lo", 32 * K, [P, NK, T], F32R)
        w_raw = at("w_raw", 64 * K, [P, 2, D])
        w_hi = at("w_hi", 72 * K, [P, 3, D], F32R)
        w_lo = at("w_lo", 84 * K, [P, 3, D], F32R)
        mix = at("mix", 96 * K, [P, NK, T])
        kin = at("kin", 96 * K, [P, 2, T])
        tA = at("tA", 104 * K, [P, T])
        tB = at("tB", 108 * K, [P, T])
        tC = at("tC", 112 * K, [P, T])
        sv = at("sv", 128 * K, [P, NT, SB_W])
        qk0 = at("qk0", 140 * K, [P, 2, T])
        x_row = at("x_row", 140 * K, [P, 2, D])
        R = 148 * K
        gq = at("gq", R, [P, 2, T])
        gk = at("gk", R + 8 * K, [P, 2, T])
        gv = at("gv", R + 16 * K, [P, NT, GLA_W])
        gg = at("gg", R + 28 * K, [P, NT, GLA_W])
        w_rawg = at("w_rawg", R + 16 * K, [P, 4, NK, P])
        S_st = at("S_st", R + 40 * K, [P, 2, 4, 2 * GLA_DV])
        kteN = at("kteN", R + 46 * K, [P, 2, P])
        sT = at("sT", R + 47 * K, [P, 2, 2, P])
        gy = at("gy", R + 49 * K, [P, GLA_W])
        gsq = at("gsq", R + 50 * K + 512, [P, GLA_W])
        gms = at("gms", R + 52 * K, [P, 8])
        E = at("E", R, [P, 2, T])
        SP = at("SP", R + 8 * K, [P, 2, T])
        aT = at("aT", R + 16 * K, [P, 2, NT, P])
        conv_in = at("conv_in", R + 24 * K, [P, 3, T])
        qk1 = at("qk1", R + 36 * K, [P, 2, T])
        C0 = R + 53 * K
        ident = at("ident", C0, [P, P])
        trimask = at("trimask", C0 + 512, [P, P])
        wg2 = at("wg2", C0 + 1024, [64, 4, 64])
        nw = at("nw", C0 + 2048, [P, GLA_DV])
        cw = at("cw", C0 + 2432, [P, CONV_K, 2])
        cb = at("cb", C0 + 2464, [P, 2])
        bg = at("bg", C0 + 2496, [P, 2])
        dec = at("dec", C0 + 2528, [P, 2, T // GLA_C])
        zb = at("zb", C0 + 2656, [P, GLA_W], BF16)
        zeros = at("zeros", C0 + 3424, [P, GLA_C])

        pp = [ctx.enter_context(nc.psum_tensor(f"bank{i}", [P, 512], F32)) for i in range(2)]
        pz = [ctx.enter_context(nc.psum_tensor(f"pz{i}", [P, 1024], F32)) for i in range(2)]
        pa_ = ctx.enter_context(nc.psum_tensor("bank6", [P, 512], F32))
        po = ctx.enter_context(nc.psum_tensor("bank7", [P, 512], F32))
        xt_bank = [pp[0][:, :], pp[1][:, :], pz[0][:, 0:512], pz[0][:, 512:1024]]
        gate_bank = [pz[0][:, 0:512], pz[0][:, 512:1024], pz[1][:, 0:512], pz[1][:, 512:1024]]
        sc_banks = pz[0][:, :].rearrange("p (b x) -> p b x", b=2)[:, :, 0:2 * P].rearrange("p b (j t) -> p b j t", j=2)
        kt_bank = pz[1][:, 0:2 * P]
        kv_bank = [pz[1][:, 0:384], pz[1][:, 512:512 + 384]]

        wo_hi = at("wo_hi", 0, [P, NK, D], F32R)
        wo_lo = at("wo_lo", 32 * K, [P, NK, D], F32R)
        wo_raw = at("wo_raw", 64 * K, [P, 2, D])
        mixh = at("mixh", 72 * K, [P, 2, NK, P], F32R)
        mixl = at("mixl", 80 * K, [P, 2, NK, P], F32R)
        xres = at("xres", 88 * K, [P, 2, D])
        x1 = at("x1", 128 * K, [P, 2, D])
        x1T = at("x1T", 136 * K, [P, NK, P])
        lnp = at("lnp", 140 * K, [P, 2, D])
        SMALL = {F32: 4, U32: 4, I32: 4, BF16: 2}
        place = [R + 48 * K]

        def small(name, shape, dt=F32):
            place[0] += -place[0] % 32
            t = at(name, place[0], shape, dt)
            place[0] += math.prod(shape[1:]) * SMALL[dt]
            return t

        rw = small("rw", [P, NK, NE])
        rb = small("rb", [P, NE])
        rank0 = small("rank0", [P, EPG])
        ecol = small("ecol", [P, NE])
        tok = small("tok", [P, NT], U32)
        rows_u = small("rows_u", [P, 2, NT], U32)
        g12 = small("g12", [P, 2, NT])
        npi = small("npi", [P, 1], I32)
        bns = small("bns", [P, 2, 6])
        bna = small("bna", [P, 2])
        rst = small("rst", [P, 2])
        passes = small("passes", [P, MAXPASS - 1])
        pcmp = small("pcmp", [P, MAXPASS - 1])
        zidl = small("zidl", [P, NROW // P], U32)
        trib = small("trib", [P, P], BF16)
        oneb = small("oneb", [P, P], BF16)
        idxA = small("idxA", [P, 1], U32)
        idxB = small("idxB", [TR, 1], U32)
        M = 96 * K
        assert place[0] <= R + 53 * K
        rt = lambda n, o, s, dt=F32: at(n, M + o, s, dt)
        place[0] = M
        rs = small("rs", [P, NT, NE])
        rsel = small("rsel", [P, NT * NGRP, EPG])
        rpair = small("rpair", [P, NT * NGRP, 6])
        rgs = small("rgs", [P, NT, NGRP])
        rgk = small("rgk", [P, NT, NGRP])
        rge = small("rge", [P, NT * NGRP, 3])
        rek = small("rek", [P, NT * NGRP, EPG])
        rmask = small("rmask", [P, NT, NE])
        rgate = small("rgate", [P, NT, NE])
        rden = small("rden", [P, NT])
        rmb = small("rmb", [P, NT, NE], BF16)
        rpos = small("rpos", [P, NT + 1, NE])
        rrow = small("rrow", [P, NT, NE])
        rtmp = small("rtmp", [P, NT, NE])
        rr12 = small("rr12", [P, 2, NT])
        rmax = small("rmax", [P, 1])
        rnp = small("rnp", [P, 1])
        er = at("er", R, [P, NPIECE, D])
        eh = at("eh", 0, [P, NPIECE, D], F32R)
        el = at("el", 48 * K, [P, NPIECE, D], F32R)
        xgA = rt("xgA", 6 * K, [P, D])
        xgB = rt("xgB", 10 * K, [TR, D])
        xTh = rt("xTh", 14 * K, [P, NK, TW], F32R)
        xTl = rt("xTl", 19 * K, [P, NK, TW], F32R)
        sil = rt("sil", 24 * K, [P, 2, TW])
        hf = rt("hf", 24 * K + 1280, [P, NF, TW])
        hh = rt("hh", 24 * K + 3840, [P, NF, TW], F32R)
        hl = rt("hl", 24 * K + 6400, [P, NF, TW], F32R)
        yTs = rt("yTs", 33 * K, [P, NK, TW])
        yA = rt("yA", 38 * K, [P, D])
        yB = rt("yB", 42 * K, [TR, D])
        zrow = at("zrow", 144 * K, [P, D])
        cy1 = at("cy1", 0, [P, 2, D])
        cy2 = at("cy2", 8 * K, [P, 2, D])
        cx = at("cx", 16 * K, [P, 2, D])
        cr = at("cr", 24 * K, [P, 2, D])
        lnq = at("lnq", 32 * K, [P, 2, D])

        x1_dram = nc.dram_tensor("x1_scratch", [T, D], F32).ap()
        y_dram = nc.dram_tensor("y_scratch", [NROW, D], F32).ap()
        idl_dram = nc.dram_tensor("slot_tokens", [NROW, 1], U32).ap()
        ob = [[pp[0][:, :], pp[1][:, :]], [pz[0][:, 0:512], pz[0][:, 512:1024]]]
        h1b = [pp[0][:, 0:2 * TW], pp[1][:, 0:2 * TW]]
        h3b = [pz[0][:, 0:2 * TW], pz[0][:, 512:512 + 2 * TW]]
        xb = [pz[1][:, 0:2 * TW], pz[1][:, 512:512 + 2 * TW]]
        yb = [pa_[:, 0:2 * TW], po[:, 0:2 * TW]]
        names = ("x_in0 x_in1 xt_ps xt_hi xt_lo w_in0 w_in1 wg_in w_hi_ok w_lo_ok proj_ps proj_ev gg_ev "
                 "const_in const_ok gate_ps n_ok m_ok ge_ok gl_ok gsp_ok cs_ok gexp_ok gmul_ok dec_ok sc_ps kt_ps kteN_ok sT_ok "
                 "kv_ps st_ok o_ps gsq_ok gms_ok rstd_ok gy_ok gyT_ps gyT_ev gs_ok "
                 "z_ps zc_ok e_ok ln_ok sp_ok spm_ok sfx_ok arg_ok a_ok am_ok aT_ps aT_ev o_done o_ev conv_ok ggs_ok gge_ok stored").split()
        names += ("wo_in0 wo_in1 wo_hi_ok wo_lo_ok xr_in0 xr_in1 lnp_in mixh_ok mixl_ok ob_ps res_ok bn_ok lrs_ok x1_ok x1_st0 x1_st1 "
                  "x1t_ps x1t_ev lg_ps rexp_ok route_step mask_ok pos_ps route_ok tokc_ok idl_z idl_st idx_in pool_go zrow_ok y_zero xg_in "
                  "piece_done eh_ok el_ok sil_ok h_ok hh_ok hl_ok xtr_ps xTh_ok xTl_ok yT_ev ytr_ps yA_ev yB_ev y_out "
                  "cg_in0 cg_in1 cx_in0 cx_in1 lnq_in c1_ok c2_ok cres_ok cbn_ok clr_ok cnm_ok cnorm_ok cout_ok cfin_ok out_st0 out_st1").split()
        names += [f"e_in{p}" for p in range(NPIECE)]
        S = {n: sem(n) for n in names}

        block = ctx.enter_context(nc.Block())
        hs = [0, 64]

        def w_cols(n):
            if n < CHUNK_F0:
                m = n - CHUNK_N0
                return OFF[N_PIECES[m // 3]] + P * (m % 3)
            kind, j = FILL[n - CHUNK_F0]
            return OFF[{"sq": "sb_q", "sk": "sb_k", "cc": "c_c", "ch": "c_h", "cb": "c_b"}[kind]] + P * j

        def raw_chunk(n):
            return w_rawg[:, n, :, :].rearrange("p k c -> p (k c)") if n < 4 else w_raw[:, n % 2, :]

        w_k = I["w_in"][0].rearrange("(k p) n -> p k n", p=P)

        w1v = I["w1"][0].rearrange("e (k p) f -> p e k f", p=P)
        w3v = I["w3"][0].rearrange("e (k p) f -> p e k f", p=P)
        w2v = I["w2"][0].rearrange("e (f p) d -> p e f d", p=P)

        def load_expert(sp, j, e, first=False):
            b = NE * j + e
            for p in range(NPIECE):
                if not first:
                    sp.wait_ge(S["el_ok"], NPIECE * b - NPIECE + p + 1)
                if p < 2 * NF:
                    src = (w1v, w3v)[p % 2][:, bass.ds(e, 1), :, (p // 2) * P:(p // 2 + 1) * P]
                    dst = er[:, p:p + 1, :].rearrange("p e (k f) -> p e k f", k=NK)
                else:
                    m = p - 2 * NF
                    src = w2v[:, bass.ds(e, 1), :, m * 2 * P:(m + 1) * 2 * P]
                    dst = er[:, p:p + 1, :].rearrange("p e (f d) -> p e f d", f=NF)
                sp.dma_start(dst, src).then_inc(S[f"e_in{p}"], 16)

        def passes_of(eng, one_pass):
            one_pass(0)
            eng.wait_ge(S["route_ok"], 3)
            n = eng.value_load(npi[0:1, 0:1], min_val=1, max_val=MAXPASS)
            with eng.If(n > 1):
                with eng.Fori(1, n) as j:
                    one_pass(j)
            return n

        def experts_of(eng, j, block):
            block(NE * j, False, True)
            with eng.Fori(1, NE - 1) as e:
                block(NE * j + e, True, True)
            block(NE * j + NE - 1, True, False)

        def norm_stats(dve, buf, s, src, n, done, i, read):
            dve.wait_ge(S[src], n)
            for h in range(2):
                dve.bn_stats(bns[:, h, :], buf[:, s, h * 512:h * 512 + 512]).then_inc(S[done], 1)
            dve.wait_ge(S[done], 4 * i + 2)
            dve.bn_aggr(bna[:, :], bns[:, :, :].rearrange("p a b -> p (a b)")).then_inc(S[done], 1)
            dve.wait_ge(S[done], 4 * i + 3)
            dve.tensor_scalar(rst[:, 0:1], bna[:, 1:2], LN_EPS, None, ALU.add).then_inc(S[done], 1)

        def add_bias(pool, i):
            pool.wait_ge(S["cout_ok"], i + 1)
            pool.wait_ge(S["lnq_in"], 32)
            pool.tensor_tensor(cr[:, i % 2, :], cr[:, i % 2, :], lnq[:, 1, :], ALU.add).then_inc(S["cfin_ok"], 1)

        @block.sync
        def _(sp):
            for i in range(NT):
                if i >= 2:
                    sp.wait_ge(S["xt_ps"], 2 * (i - 1))
                sp.dma_start(x_row[:, i % 2, :], I["x"][0, i * P:(i + 1) * P, :]).then_inc(S[f"x_in{i % 2}"], 16)
                if i == 1:
                    sp.wait_ge(S["const_ok"], 5)
                    for n in range(4):
                        kind, hp = T_FIRST[n]
                        src = OFF["g_q"] if kind == "gq" else OFF["g_k"]
                        for h in range(2):
                            c0 = src + (2 * hp + h) * GLA_DK
                            sp.dma_start(w_rawg[:, n, :, hs[h]:hs[h] + GLA_DK], w_k[:, :, c0:c0 + GLA_DK]).then_inc(S["wg_in"], 16)
                    sp.dma_start(w_rawg[:, 1, :, GLA_DK:64], w_k[:, :, OFF["g_lr"]:OFF["g_lr"] + GLA_R]).then_inc(S["wg_in"], 16)
            for n in range(4, NCHUNK):
                if n >= 6:
                    sp.wait_ge(S["w_lo_ok"], n - 1)
                if n < 6:
                    kind, j = T_FIRST[n]
                    c0 = OFF["sb_q" if kind == "sq" else "sb_k"] + P * j
                else:
                    c0 = w_cols(n)
                sp.dma_start(w_raw[:, n % 2, :].rearrange("p (k c) -> p k c", k=NK), w_k[:, :, c0:c0 + P])\
                    .then_inc(S[f"w_in{n % 2}"], 16)
            w_o = I["w_out"][0].rearrange("(k p) n -> p k n", p=P)
            for k in range(NK):
                if k < 2:
                    sp.wait_ge(S["w_lo_ok"], NCHUNK)
                else:
                    sp.wait_ge(S["wo_lo_ok"], k - 1)
                sp.dma_start(wo_raw[:, k % 2, :], w_o[:, k, :]).then_inc(S[f"wo_in{k % 2}"], 16)
            sp.wait_ge(S["proj_ps"], NFILL)
            for i in range(NT):
                if i >= 2:
                    sp.wait_ge(S["res_ok"], 2 * (i - 1))
                sp.dma_start(xres[:, i % 2, :], I["x"][0, i * P:(i + 1) * P, :]).then_inc(S[f"xr_in{i % 2}"], 16)
                if i == 1:
                    sp.wait_ge(S["o_ev"], NPAIR * NT)
                    sp.wait_ge(S["arg_ok"], NU)
                    sp.wait_ge(S["aT_ev"], HALVES[NU])
                    sp.wait_ge(S["conv_ok"], 10)
                    load_expert(sp, 0, 0, first=True)
                if i >= 1:
                    sp.wait_ge(S["x1_ok"], 3 * i)
                    sp.dma_start(x1_dram[(i - 1) * P:i * P, :], x1[:, (i - 1) % 2, :]).then_inc(S[f"x1_st{(i - 1) % 2}"], 16)
            sp.wait_ge(S["x1_ok"], 3 * NT)
            sp.dma_start(x1_dram[(NT - 1) * P:NT * P, :], x1[:, (NT - 1) % 2, :]).then_inc(S[f"x1_st{(NT - 1) % 2}"], 16)
            with sp.Fori(1, NE) as e:
                load_expert(sp, 0, e)
            sp.wait_ge(S["route_ok"], 3)
            npass = sp.value_load(npi[0:1, 0:1], min_val=1, max_val=MAXPASS)
            with sp.If(npass > 1):
                with sp.Fori(1, npass) as j:
                    with sp.Fori(0, NE) as e:
                        load_expert(sp, j, e)
            sp.wait_ge(S["y_out"], npass * (32 * NE))
            for i in range(NT):
                if i >= 2:
                    sp.wait_ge(S["cres_ok"], i - 1)
                sp.dma_start(cx[:, i % 2, :], x1_dram[i * P:(i + 1) * P, :]).then_inc(S[f"cx_in{i % 2}"], 16)
                if i == 0:
                    for a, name in enumerate(("ln2_g", "ln2_b")):
                        sp.dma_start(lnq[:, a, :], I[name][0].partition_broadcast(P)).then_inc(S["lnq_in"], 16)
                if i >= 1:
                    sp.wait_ge(S["cfin_ok"], i)
                    sp.dma_start(out[0, (i - 1) * P:i * P, :], cr[:, (i - 1) % 2, :]).then_inc(S[f"out_st{(i - 1) % 2}"], 16)
            sp.wait_ge(S["cfin_ok"], NT)
            sp.dma_start(out[0, (NT - 1) * P:NT * P, :], cr[:, (NT - 1) % 2, :]).then_inc(S[f"out_st{(NT - 1) % 2}"], 16)
            for s in range(2):
                sp.wait_ge(S[f"out_st{s}"], 16 * (NT // 2))

        @block.gpsimd
        def _(pool):
            pool.memset(w_rawg[:, :, :, :], 0.0).then_inc(S["const_ok"], 1)
            pool.memset(wg2[:, :, :], 0.0).then_inc(S["const_ok"], 1)
            pool.memset(bg[:, :], 0.0).then_inc(S["const_ok"], 1)
            pool.memset(ident[:, :], 0.0).then_inc(S["const_ok"], 1)
            pool.memset(trimask[:, :], 1.0).then_inc(S["const_ok"], 1)
            pool.memset(zb[:, :], 0.0).then_inc(S["const_ok"], 1)
            pool.memset(zeros[:, :], 0.0).then_inc(S["const_ok"], 1)
            pool.memset(S_st[:, :, :, :], 0.0).then_inc(S["const_ok"], 1)
            pool.wait_ge(S["const_ok"], 8)
            pool.affine_select(ident[:, :], ident[:, :], [[-1, P]], ALU.not_equal, 1.0, base=0, channel_multiplier=1)\
                .then_inc(S["const_ok"], 1)
            pool.affine_select(trimask[:, :], trimask[:, :], [[1, P]], ALU.is_ge, 0.0, base=0, channel_multiplier=-1)\
                .then_inc(S["const_ok"], 1)
            pool.wait_ge(S["const_ok"], 10)
            pool.memset(trimask[0:64, 64:P], 0.0).then_inc(S["const_ok"], 1)
            for u, (p, i, h) in enumerate(UNITS):
                own = slice(i * P, (i + 1) * P)
                pool.wait_ge(S["sp_ok"], u + 1)
                pool.affine_select(SP[:, u % 2, own], SP[:, u % 2, own], [[-1, P]], ALU.is_gt, 0.0,
                                   base=0, channel_multiplier=1).then_inc(S["spm_ok"], 1)
                pool.wait_ge(S["a_ok"], u + 1)
                pool.affine_select(SP[:, u % 2, own], SP[:, u % 2, own], [[-1, P]], ALU.is_gt, 0.0,
                                   base=0, channel_multiplier=1).then_inc(S["am_ok"], 1)

            pool.wait_ge(S["aT_ev"], HALVES[NU])
            pool.memset(zidl[:, :], 0).then_inc(S["tokc_ok"], 1)
            pool.memset(trib[:, :], 1.0).then_inc(S["tokc_ok"], 1)
            pool.memset(oneb[:, :], 1.0).then_inc(S["tokc_ok"], 1)
            pool.iota(tok[:, :], [[P, NT]], base=0, channel_multiplier=1).then_inc(S["tokc_ok"], 1)
            pool.iota(ecol[:, :], [[TW, NE]], base=0, channel_multiplier=0, allow_small_or_imprecise_dtypes=True).then_inc(S["tokc_ok"], 1)
            pool.iota(rank0[:, :], [[-1, EPG]], base=EPG - 1, channel_multiplier=0, allow_small_or_imprecise_dtypes=True).then_inc(S["tokc_ok"], 1)
            pool.iota(passes[:, :], [[TW, MAXPASS - 1]], base=TW, channel_multiplier=0, allow_small_or_imprecise_dtypes=True).then_inc(S["tokc_ok"], 1)
            pool.wait_ge(S["tokc_ok"], 7)
            pool.affine_select(trib[:, :], trib[:, :], [[1, P]], ALU.is_gt, 0.0, base=0, channel_multiplier=-1).then_inc(S["tokc_ok"], 1)
            pool.dma_start(idl_dram.rearrange("(p c) o -> p (c o)", p=P), zidl[:, :]).then_inc(S["idl_z"], 16)
            pool.wait_ge(S["idl_z"], 16)
            pool.wait_ge(S["route_ok"], 3)
            for c in range(2):
                for i in range(NT):
                    pool.indirect_dma_start(idl_dram, bass.IndirectOffsetOnAxis(rows_u[:, c, i:i + 1], 0), tok[:, i:i + 1], None,
                                            bounds_check=NROW - 1, oob_is_err=True).then_inc(S["idl_st"], 16)
            pool.wait_ge(S["idl_st"], 16 * 2 * NT)
            for s in range(2):
                pool.wait_ge(S[f"x1_st{s}"], 16 * (NT // 2))

            def gather(b):
                pool.dma_start(idxA[:, :], idl_dram[bass.ds(b * TW, P), :]).then_inc(S["idx_in"], 16)
                pool.dma_start(idxB[:, :], idl_dram[bass.ds(b * TW + P, TR), :]).then_inc(S["idx_in"], 16)
                pool.wait_ge(S["idx_in"], 32 * b + 32)
                pool.wait_ge(S["xtr_ps"], NF * b)
                pool.sem_inc(S["pool_go"], 1)
                pool.indirect_dma_start(xgA[:, :], None, x1_dram, bass.IndirectOffsetOnAxis(idxA[:, 0:1], 0)).then_inc(S["xg_in"], 16)
                pool.indirect_dma_start(xgB[:, :], None, x1_dram, bass.IndirectOffsetOnAxis(idxB[:, 0:1], 0)).then_inc(S["xg_in"], 16)
                pool.wait_ge(S["xg_in"], 32 * b + 32)
                pool.sem_inc(S["pool_go"], 1)

            def store(b):
                pool.wait_ge(S["yB_ev"], b + 1)
                pool.dma_start(y_dram[bass.ds(b * TW, P), :], yA[:, :]).then_inc(S["y_out"], 16)
                pool.dma_start(y_dram[bass.ds(b * TW + P, TR), :], yB[:, :]).then_inc(S["y_out"], 16)

            def pool_pass(j):
                gather(NE * j)
                gather(NE * j + 1)
                with pool.Fori(2, NE) as e:
                    gather(NE * j + e)
                    store(NE * j + e - 2)
                store(NE * j + NE - 2)
                store(NE * j + NE - 1)
            pool_pass(0)
            npass = pool.value_load(npi[0:1, 0:1], min_val=1, max_val=MAXPASS)
            with pool.If(npass > 1):
                pool.memset(zrow[:, :], 0.0).then_inc(S["zrow_ok"], 1)
                pool.wait_ge(S["zrow_ok"], 1)
                with pool.Fori(NE * TW // P, NROW // P) as r:
                    pool.dma_start(y_dram[bass.ds(r * P, P), :], zrow[:, :]).then_inc(S["y_zero"], 16)
                pool.wait_ge(S["y_zero"], 16 * ((NROW - NE * TW) // P))
                with pool.Fori(1, npass) as j:
                    pool_pass(j)

            def token_rows(src):
                for i in range(NT):
                    if i >= 2:
                        pool.wait_ge(S["cres_ok"], i - 1)
                    for c, buf in ((0, cy1), (1, cy2)):
                        pool.indirect_dma_start(buf[:, i % 2, :], None, src, bass.IndirectOffsetOnAxis(rows_u[:, c, i:i + 1], 0))\
                            .then_inc(S[f"cg_in{i % 2}"], 16)
                    if i >= 1:
                        add_bias(pool, i - 1)
                add_bias(pool, NT - 1)
            pool.wait_ge(S["y_out"], npass * (32 * NE))
            pool.sem_inc(S["pool_go"], 1)
            with pool.If(npass < 2):
                token_rows(y_dram[0:NE * TW, :])
            with pool.If(npass > 1):
                token_rows(y_dram)

        def mm3(pe, dst, k_first, k_last, lhs, rhs, ks):
            for k in ks:
                lh, ll = lhs(k)
                rh, rl = rhs(k)
                pe.matmul(dst, lh, rh, start=(k == k_first), stop=False)
                pe.matmul(dst, lh, rl, start=False, stop=False)
                last = pe.matmul(dst, ll, rh, start=False, stop=(k == k_last))
            return last

        def qk_of(p):
            return qk0 if p % 2 == 0 else qk1

        @block.tensor
        def _(pe):
            def wait_bank(f):
                if f >= 2:
                    if GG_FIRST <= f - 2 < GG_LAST:
                        pe.wait_ge(S["gg_ev"], gg_before(f - 1))
                    else:
                        pe.wait_ge(S["proj_ev"], ev_before(f - 1))

            def t_fill(n, f, half, ks):
                s = n % 3
                ns = slice(half * 512, half * 512 + 512)
                if ks[0] == 0:
                    wait_bank(f)
                    if half == 0:
                        pe.wait_ge(S["w_lo_ok"], n + 1)
                last = mm3(pe, pp[f % 2][:, :], 0, NK - 1,
                           lambda k: (w_hi[:, s, k * P:(k + 1) * P], w_lo[:, s, k * P:(k + 1) * P]),
                           lambda k: (xT_hi[:, k, ns], xT_lo[:, k, ns]), ks)
                return last

            def t_piece(n, f0):
                for half in range(2):
                    last = t_fill(n, f0 + half, half, range(NK))
                    last.then_inc(S["proj_ps"], 1)

            def n_tile(m, t):
                f = FILL_N0 + NT * m + t
                wait_bank(f)
                if t == 0:
                    pe.wait_ge(S["w_lo_ok"], CHUNK_N0 + 3 * m + 3)
                ts = slice(t * P, (t + 1) * P)
                mm3(pe, pp[f % 2][:, 0:GLA_W], 0, NK - 1,
                    lambda k: (xT_hi[:, k, ts], xT_lo[:, k, ts]),
                    lambda k: (w_hi[:, :, k * P:(k + 1) * P], w_lo[:, :, k * P:(k + 1) * P]),
                    range(NK)).then_inc(S["proj_ps"], 1)

            pe.wait_ge(S["const_ok"], 11)
            for i in range(NT):
                pe.wait_ge(S[f"x_in{i % 2}"], 16 * (i // 2 + 1))
                for half in range(2):
                    c = 2 * i + half
                    if c >= 4:
                        pe.wait_ge(S["xt_lo"], c - 3)
                    for j in range(4):
                        k = 4 * half + j
                        last = pe.transpose(xt_bank[c % 4][:, j * P:(j + 1) * P], x_row[:, i % 2, k * P:(k + 1) * P], ident[:, :])
                    last.then_inc(S["xt_ps"], 1)
            pe.wait_ge(S["xt_lo"], 2 * NT)
            for n in range(NCHUNK_T):
                t_piece(n, 2 * n)
                if n == 1 or n == 3:
                    hp = n // 2
                    pe.wait_ge(S["const_in"], 16 * (CONV_K + 3 + GLA_H))
                    pe.wait_ge(S["proj_ev"], 2 * 2)
                    for half in range(2):
                        pe.matmul(gate_bank[2 * hp + half], wg2[:, 2 * hp:2 * hp + 2, :], gk[0:64, 0, half * 512:half * 512 + 512],
                                  start=True, stop=True).then_inc(S["gate_ps"], 1)
            for m in range(2):
                for t in range(NT):
                    n_tile(m, t)
            for t in range(NT + 2):
                if t < NT:
                    ts = slice(t * P, (t + 1) * P)
                    if t == 0:
                        pe.wait_ge(S["gmul_ok"], 6)
                    if t >= 1:
                        pe.wait_ge(S["sT_ok"], t)
                    for h in range(GLA_H):
                        r = slice(hs[h % 2], hs[h % 2] + GLA_DK)
                        last = pe.matmul(sc_banks[:, h % 2, h // 2, :], kin[r, h // 2, ts], gq[r, h // 2, ts], start=True, stop=True)
                    last.then_inc(S["sc_ps"], 1)
                    if t >= 1:
                        pe.wait_ge(S["st_ok"], 8 * t)
                    for hp in range(2):
                        last = pe.transpose(kt_bank[:, hp * P:(hp + 1) * P], gk[:, hp, ts], ident[:, :])
                    last.then_inc(S["kt_ps"], 1)
                if 1 <= t <= NT:
                    c = t - 1
                    ts = slice(c * P, (c + 1) * P)
                    pe.wait_ge(S["sT_ok"], c + 1)
                    if c >= 1:
                        pe.wait_ge(S["gs_ok"], c)
                        pe.wait_ge(S["st_ok"], 8 * (c - 1) + 8)
                    pe.matmul(pa_[:, 0:GLA_W], zb[:, 0:P], zb[:, :], start=True, stop=False, skip_group_check=True)
                    for h in range(GLA_H):
                        pe.matmul(pa_[:, h * GLA_DV:(h + 1) * GLA_DV], sT[:, h % 2, h // 2, :], gv[:, c, h * GLA_DV:(h + 1) * GLA_DV],
                                  start=False, stop=False, skip_group_check=True)
                    for cc in range(2):
                        ch = 2 * c + cc
                        if cc == 1:
                            pe.wait_ge(S["st_ok"], 8 * c + 4)
                        for hp in range(2):
                            last = pe.matmul(pa_[64 * cc:64 * cc + 64, hp * 192:hp * 192 + 192],
                                             gq[:, hp, ch * GLA_C:(ch + 1) * GLA_C], S_st[:, hp, ch % 4, :],
                                             start=False, stop=(hp == 1), skip_group_check=True)
                    last.then_inc(S["o_ps"], 1)
                if t >= 2:
                    c = t - 2
                    pe.wait_ge(S["gy_ok"], c + 1)
                    if c >= 1:
                        pe.wait_ge(S["gyT_ev"], c)
                    for j in range(3):
                        last = pe.transpose(po[:, j * P:(j + 1) * P], gy[:, j * P:(j + 1) * P], ident[:, :])
                    last.then_inc(S["gyT_ps"], 1)
                if t < NT:
                    n_tile(2, t)
                    pe.wait_ge(S["kteN_ok"], t + 1)
                    for cc in range(2):
                        for hp in range(2):
                            last = pe.matmul(kv_bank[cc][:, hp * 192:hp * 192 + 192], kteN[64 * cc:64 * cc + 64, hp, :],
                                             gv[64 * cc:64 * cc + 64, t, hp * 192:hp * 192 + 192], start=True, stop=True)
                    last.then_inc(S["kv_ps"], 1)

            def z_of(u):
                p, i, h = UNITS[u]
                q, r = qk_of(p), slice(64 * h, 64 * h + 64)
                if u == 0:
                    pe.wait_ge(S["gyT_ev"], NT)
                    pe.wait_ge(S["st_ok"], 8 * NT - 4)
                    pe.wait_ge(S["gs_ok"], NT)
                    pe.wait_ge(S["proj_ev"], ev_before(FILL_F0))
                if (i, h) == (0, 0) and p >= 1:
                    pe.wait_ge(S["proj_ev"], ev_before(FILL_F0 + 2 * (FILL.index(("sk", p)) + 1)))
                if u >= 2:
                    pe.wait_ge(S["arg_ok"], u - 1)
                W = (i + 1) * P
                for c in range(0, W, 512):
                    e = min(W, c + 512)
                    last = pe.matmul(pz[u % 2][:, c:e], q[r, 0, i * P:(i + 1) * P], q[r, 1, c:e], start=True, stop=True)
                last.then_inc(S["z_ps"], 1)

            def pv_of(u):
                p, i, h = UNITS[u]
                pe.wait_ge(S["aT_ev"], HALVES[u + 1])
                if h == 0 and u >= 2:
                    pe.wait_ge(S["o_ev"], (u // 2))
                for j in range(i + 1):
                    last = pe.matmul(po[64 * h:64 * h + 64, 0:P], sv[:, j, (2 * p + h) * SB_D:(2 * p + h + 1) * SB_D],
                                     aT[:, u % 2, j, :], start=(j == 0), stop=(j == i))
                last.then_inc(S["o_done"], 1)

            def t_of(u, half):
                p, i, h = UNITS[u]
                g = HALVES[u] + half
                if g >= 1:
                    pe.wait_ge(S["aT_ev"], g)
                if half == 0:
                    pe.wait_ge(S["am_ok"], u + 1)
                js = range(4 * half, min(i + 1, 4 * half + 4))
                for j in js:
                    last = pe.transpose(pa_[:, (j % 4) * P:(j % 4 + 1) * P], SP[:, u % 2, j * P:(j + 1) * P], ident[:, :])
                last.then_inc(S["aT_ps"], 1)

            z_of(0)
            for u, (p, i, h) in enumerate(UNITS):
                if u + 1 < NU:
                    z_of(u + 1)
                if u >= 1:
                    pv_of(u - 1)
                t_of(u, 0)
                if u in QUARTER:
                    q = QUARTER[u]
                    fi, half, kq = q // 4, (q // 2) % 2, q % 2
                    last = t_fill(CHUNK_F0 + fi, FILL_F0 + 2 * fi + half, half, range(4 * kq, 4 * kq + 4))
                    if kq == 1:
                        last.then_inc(S["proj_ps"], 1)
                if i >= 4:
                    t_of(u, 1)
            pv_of(NU - 1)
            pe.wait_ge(S["aT_ev"], HALVES[NU])
            pe.wait_ge(S["proj_ev"], ev_before(NFILL))
            pe.wait_ge(S["arg_ok"], NU)
            for i in range(NT + 2):
                if i >= 2:
                    c = i - 2
                    pe.wait_ge(S["x1_ok"], 3 * c + 3)
                    if c >= 1:
                        pe.wait_ge(S["x1t_ev"], c)
                    for k in range(NK):
                        last = pe.transpose(pz[1][:, k * P:(k + 1) * P], x1[:, c % 2, k * P:(k + 1) * P], ident[:, :])
                    last.then_inc(S["x1t_ps"], 1)
                if i < NT:
                    pe.wait_ge(S["mixl_ok"], i + 1)
                    for half in range(2):
                        if i >= 2:
                            pe.wait_ge(S["res_ok"], 2 * (i - 2) + half + 1)
                        ns = slice(half * 512, half * 512 + 512)
                        for k in range(NK):
                            if i == 0 and half == 0:
                                pe.wait_ge(S["wo_lo_ok"], k + 1)
                            last = mm3(pe, ob[i % 2][half], 0, NK - 1,
                                       lambda k: (mixh[:, i % 2, k, :], mixl[:, i % 2, k, :]),
                                       lambda k: (wo_hi[:, k, ns], wo_lo[:, k, ns]), [k])
                        last.then_inc(S["ob_ps"], 1)
                if i >= 2:
                    c = i - 2
                    if c == 0:
                        pe.wait_ge(S["lnp_in"], 16 * 4)
                    pe.wait_ge(S["x1t_ev"], c + 1)
                    for k in range(NK):
                        last = pe.matmul(pa_[:, c * NE:(c + 1) * NE], x1T[:, k, :], rw[:, k, :], start=(k == 0), stop=(k == NK - 1))
                    last.then_inc(S["lg_ps"], 1)
            pe.wait_ge(S["tokc_ok"], 8)
            pe.wait_ge(S["mask_ok"], 1)
            rk = po[:, 0:(NT + 1) * NE]
            pe.matmul(rk, zb[:, 0:P], zb[:, 0:(NT + 1) * NE], start=True, stop=False, skip_group_check=True)
            pe.matmul(po[:, 0:NT * NE], trib[:, :], rmb[:, :, :], start=False, stop=False, skip_group_check=True)
            for j in range(NT):
                last = pe.matmul(po[:, (j + 1) * NE:(NT + 1) * NE], oneb[:, :], rmb[:, j:j + 1, :].to_broadcast([P, NT - j, NE]),
                                 start=False, stop=(j == NT - 1), skip_group_check=True)
            last.then_inc(S["pos_ps"], 1)

            def x_transposes(b, before):
                pe.wait_ge(S["xg_in"], 32 * b + 32)
                if before:
                    pe.wait_ge(S["yB_ev"], b - 1)
                for r in range(4):
                    if r >= 2:
                        pe.wait_ge(S["xTl_ok"], 4 * b + r - 1)
                    for dd in range(2):
                        d = 2 * r + dd
                        pe.transpose(xb[r % 2][:, dd * TW:dd * TW + P], xgA[:, d * P:(d + 1) * P], ident[:, :])
                        last = pe.transpose(xb[r % 2][:, dd * TW + P:(dd + 1) * TW], xgB[:, d * P:(d + 1) * P], ident[0:TR, 0:TR])
                    last.then_inc(S["xtr_ps"], 1)

            def y_transposes(b, rest):
                if not rest:
                    pe.wait_ge(S["yT_ev"], 4 * b + 4)
                else:
                    pe.wait_ge(S["yA_ev"], b + 1)
                for d in range(NK):
                    if rest:
                        last = pe.transpose(pz[1][0:TR, d * P:(d + 1) * P], yTs[:, d, P:TW], ident[:, :])
                    else:
                        last = pe.transpose(pz[1][:, d * P:(d + 1) * P], yTs[:, d, 0:P], ident[:, :])
                last.then_inc(S["ytr_ps"], 1)

            def pe_block(b, prev, nxt):
                pe.wait_ge(S["xTl_ok"], 4 * b + 4)
                for f in range(NF):
                    if f % 2 == 0 and not (prev is False and isinstance(b, int) and b == 0):
                        pe.wait_ge(S["h_ok"], 2 * b + f // 2 - 1)
                    for w, bank in ((0, h1b), (1, h3b)):
                        p = 2 * f + w
                        pe.wait_ge(S["el_ok"], NPIECE * b + p + 1)
                        mm3(pe, bank[f // 2][:, (f % 2) * TW:(f % 2 + 1) * TW], 0, NK - 1,
                            lambda k: (eh[:, p, k * P:(k + 1) * P], el[:, p, k * P:(k + 1) * P]),
                            lambda k: (xTh[:, k, :], xTl[:, k, :]), range(NK)).then_inc(S["piece_done"], 1)
                    if prev and f == 0:
                        pe.wait_ge(S["xTl_ok"], 4 * b + 4)
                        y_transposes(b - 1, False)
                    if prev and f == 1:
                        y_transposes(b - 1, True)
                if nxt:
                    x_transposes(b + 1, prev)
                pe.wait_ge(S["hl_ok"], 2 * b + 2)
                for m in range(4):
                    if m >= 2 or not (prev is False and isinstance(b, int) and b == 0):
                        pe.wait_ge(S["yT_ev"], 4 * b + m - 1)
                    p = 2 * NF + m
                    pe.wait_ge(S["el_ok"], NPIECE * b + p + 1)
                    for dd in range(2):
                        last = mm3(pe, yb[m % 2][:, dd * TW:(dd + 1) * TW], 0, NF - 1,
                                   lambda f: (eh[:, p, f * 2 * P + dd * P:f * 2 * P + (dd + 1) * P],
                                              el[:, p, f * 2 * P + dd * P:f * 2 * P + (dd + 1) * P]),
                                   lambda f: (hh[:, f, :], hl[:, f, :]), range(NF))
                    last.then_inc(S["piece_done"], 1)
                if not nxt:
                    y_transposes(b, False)
                    y_transposes(b, True)

            def pe_pass(j):
                if isinstance(j, int):
                    x_transposes(0, False)
                else:
                    pe.wait_ge(S["yB_ev"], NE * j)
                    x_transposes(NE * j, False)
                experts_of(pe, j, pe_block)
            passes_of(pe, pe_pass)

        def last_fill(n):
            if n < CHUNK_N0:
                return 2 * n + 2
            if n < CHUNK_F0:
                return FILL_N0 + NT * ((n - CHUNK_N0) // 3 + 1)
            return FILL_F0 + 2 * (n - CHUNK_F0) + 2

        def wait_raw(eng, n):
            if n < 4:
                eng.wait_ge(S["wg_in"], 16 * 9)
            else:
                eng.wait_ge(S[f"w_in{n % 2}"], 16 * ((n - 4) // 2 + 1))

        @block.scalar
        def _(act):
            act.preload_act_table_set("natural_log_exp_and_others")
            with nc.allow_non_contiguous_dma(reason="a few hundred parameters"):
                for i in range(CONV_K):
                    act.dma_start(cw[:, i, :], I["conv_w"][0, i, :].rearrange("(c p) -> p c", p=P)).then_inc(S["const_in"], 16)
                act.dma_start(cb[:, :], I["conv_b"][0].rearrange("(c p) -> p c", p=P)).then_inc(S["const_in"], 16)
                act.dma_start(nw[:, :], I["gla_norm_w"][0].partition_broadcast(P))\
                    .then_inc(S["const_in"], 16)
                act.wait_ge(S["const_ok"], 8)
                act.dma_start(wg2[GLA_DK:64, :, 0:GLA_DK], I["gla_w_gate2"][0].rearrange("r (h d) -> r h d", h=GLA_H))\
                    .then_inc(S["const_in"], 16)
                for h in range(GLA_H):
                    act.dma_start(bg[hs[h % 2]:hs[h % 2] + GLA_DK, h // 2:h // 2 + 1],
                                  I["gla_b_gate"][0, h * GLA_DK:(h + 1) * GLA_DK].rearrange("(d o) -> d o", o=1))\
                        .then_inc(S["const_in"], 16)

            def split_hi(n):
                wait_raw(act, n)
                if n >= 3:
                    act.wait_ge(S["proj_ps"], last_fill(n - 3))
                    act.wait_ge(S["w_lo_ok"], n - 2)
                act.activation(w_hi[:, n % 3, :], raw_chunk(n), ACT.Copy).then_inc(S["w_hi_ok"], 1)

            def evac(f, dst, scale=1.0, cols=512):
                act.wait_ge(S["proj_ps"], f + 1)
                act.activation(dst, pp[f % 2][:, 0:cols], ACT.Copy, scale=scale).then_inc(S["proj_ev"], 1)

            for c in range(2 * NT):
                i, half = c // 2, c % 2
                act.wait_ge(S["xt_ps"], c + 1)
                act.activation(xT_hi[:, 4 * half:4 * half + 4, i * P:(i + 1) * P],
                               xt_bank[c % 4].rearrange("p (k t) -> p k t", k=4), ACT.Copy).then_inc(S["xt_hi"], 1)
            split_hi(0)
            split_hi(1)
            for n in range(NCHUNK_T):
                split_hi(n + 2)
                kind, j = T_FIRST[n]
                for half in range(2):
                    hsl = slice(half * 512, half * 512 + 512)
                    dst = {"gq": gq[:, j, hsl], "gk": gk[:, j, hsl], "sq": qk0[:, 0, hsl], "sk": qk0[:, 1, hsl]}[kind]
                    evac(2 * n + half, dst, {"gq": GLA_DK ** -0.5, "sq": SB_D ** -0.5}.get(kind, 1.0))
            split_hi(NCHUNK_T + 2)

            def gate_steps(hp):
                act.wait_ge(S["m_ok"], hp + 1)
                act.activation(tB[:, :], tB[:, :], ACT.Exp).then_inc(S["ge_ok"], 1)
                act.wait_ge(S["ge_ok"], hp + 1)
                act.activation(tB[:, :], tB[:, :], ACT.Ln, bias=1.0).then_inc(S["gl_ok"], 1)
                yield
                act.wait_ge(S["cs_ok"], 17 * hp + 16)
                act.activation(tB[:, :], tA[:, :], ACT.Exp, scale=-1.0 / GATE_NORM).then_inc(S["gexp_ok"], 1)
                act.activation(tC[:, :], tA[:, :], ACT.Exp, scale=1.0 / GATE_NORM).then_inc(S["gexp_ok"], 1)
                yield
                act.wait_ge(S["cs_ok"], 17 * hp + 17)
                act.activation(tB[:, :], tB[:, :], ACT.Exp, scale=1.0 / GATE_NORM).then_inc(S["gexp_ok"], 1)
                act.activation(dec[:, hp, :], tA[:, :].rearrange("p (c t) -> p c t", t=GLA_C)[:, :, GLA_C - 1],
                               ACT.Exp, scale=-1.0 / GATE_NORM).then_inc(S["dec_ok"], 1)
                yield

            steps = [s for hp in range(2) for s in [gate_steps(hp)] * 3]
            for t in range(NT):
                evac(FILL_N0 + t, gv[:, t, :], cols=GLA_W)
                if t < 6:
                    next(steps[t])
            for n in range(CHUNK_N0 + 3, CHUNK_N0 + 6):
                split_hi(n)
            for t in range(NT):
                f = FILL_N0 + NT + t
                act.wait_ge(S["proj_ps"], f + 1)
                act.activation(gg[:, t, :], pp[f % 2][:, 0:GLA_W], ACT.Exp, scale=-1.0).then_inc(S["gge_ok"], 1)
            for n in range(CHUNK_N0 + 6, CHUNK_N0 + 9):
                split_hi(n)
            for t in range(NT + 2):
                if t < NT:
                    act.wait_ge(S["kt_ps"], t + 1)
                    if t >= 1:
                        act.wait_ge(S["kv_ps"], t)
                    act.activation(kteN[:, :, :], kt_bank.rearrange("p (h c) -> p h c", h=2), ACT.Copy).then_inc(S["kteN_ok"], 1)
                if 1 <= t <= NT:
                    act.wait_ge(S["o_ps"], t)
                    if t >= 2:
                        act.wait_ge(S["gms_ok"], 2 * (t - 1))
                    act.activation(gsq[:, :], pa_[:, 0:GLA_W], ACT.Square).then_inc(S["gsq_ok"], 1)
                if t >= 2:
                    act.wait_ge(S["gyT_ps"], t - 1)
                    act.activation(mix[:, 5:8, (t - 2) * P:(t - 1) * P], po[:, 0:3 * P].rearrange("p (j t) -> p j t", j=3),
                                   ACT.Copy).then_inc(S["gyT_ev"], 1)
                if 1 <= t <= NT:
                    act.wait_ge(S["gms_ok"], 2 * t)
                    act.activation(gms[:, 0:4], gms[:, 0:4], ACT.Ln).then_inc(S["rstd_ok"], 1)
                    act.wait_ge(S["rstd_ok"], 2 * t - 1)
                    act.activation(gms[:, 4:8], gms[:, 0:4], ACT.Exp, scale=-0.5).then_inc(S["rstd_ok"], 1)
                if t < NT:
                    evac(FILL_N0 + 2 * NT + t, sv[:, t, :], cols=SB_W)
            split_hi(CHUNK_F0)

            def softplus_of(u):
                W = (UNITS[u][1] + 1) * P
                act.wait_ge(S["zc_ok"], u + 1)
                act.activation(E[:, u % 2, 0:W], E[:, u % 2, 0:W], ACT.Exp).then_inc(S["e_ok"], 1)
                act.wait_ge(S["e_ok"], u + 1)
                act.activation(E[:, u % 2, 0:W], E[:, u % 2, 0:W], ACT.Ln, bias=1.0).then_inc(S["ln_ok"], 1)

            def split_wo_hi(k):
                if k == 0:
                    act.wait_ge(S["proj_ps"], NFILL)
                act.wait_ge(S[f"wo_in{k % 2}"], 16 * (k // 2 + 1))
                act.activation(wo_hi[:, k, :], wo_raw[:, k % 2, :], ACT.Copy).then_inc(S["wo_hi_ok"], 1)

            softplus_of(0)
            for u, (p, i, h) in enumerate(UNITS):
                W = (i + 1) * P
                if u + 1 < NU:
                    softplus_of(u + 1)
                q = QUARTER.get(u)
                if q is not None and q % 4 == 0 and q // 4 + 1 < len(FILL):
                    split_hi(CHUNK_F0 + q // 4 + 1)
                if u >= NU - 2:
                    for k in range(4 * (u - NU + 2), 4 * (u - NU + 3)):
                        split_wo_hi(k)
                act.wait_ge(S["arg_ok"], u + 1)
                act.activation(SP[:, u % 2, 0:W], SP[:, u % 2, 0:W], ACT.Exp).then_inc(S["a_ok"], 1)
                if h == 0 and u >= 2:
                    pp_, ii = UNITS[u - 1][0], UNITS[u - 1][1]
                    act.wait_ge(S["o_done"], u)
                    act.activation(mix[:, 2 + pp_, ii * P:(ii + 1) * P], po[:, 0:P], ACT.Copy).then_inc(S["o_ev"], 1)
                for half in range(1 if i < 4 else 2):
                    lo, hi = 4 * half, min(i + 1, 4 * half + 4)
                    act.wait_ge(S["aT_ps"], HALVES[u] + half + 1)
                    if half == 0 and u >= 2:
                        act.wait_ge(S["o_done"], u - 1)
                    act.activation(aT[:, u % 2, lo:hi, :], pa_[:, 0:(hi - lo) * P].rearrange("p (j t) -> p j t", t=P),
                                   ACT.Copy).then_inc(S["aT_ev"], 1)
                if q is not None and q % 2 == 1:
                    f = q // 2
                    kind, j = FILL[f // 2]
                    hsl = slice((f % 2) * 512, (f % 2) * 512 + 512)
                    if kind in ("sq", "sk"):
                        dst = qk_of(j)[:, 0 if kind == "sq" else 1, hsl]
                        if j == 2:
                            act.wait_ge(S["z_ps"], 2 * NT)
                    else:
                        dst = conv_in[:, {"cc": 0, "ch": 1, "cb": 2}[kind], hsl]
                        if j == 1:
                            act.wait_ge(S["conv_ok"], 5 if kind == "cb" else 4)
                    evac(FILL_F0 + f, dst, SB_D ** -0.5 if kind == "sq" else 1.0)
            act.wait_ge(S["o_done"], NU)
            act.activation(mix[:, 2 + NPAIR - 1, (NT - 1) * P:NT * P], po[:, 0:P], ACT.Copy).then_inc(S["o_ev"], 1)

            act.wait_ge(S["am_ok"], NU)
            act.dma_start(lnp[:, 0, :], I["ln1_g"][0].partition_broadcast(P)).then_inc(S["lnp_in"], 16)
            act.dma_start(lnp[:, 1, :], I["ln1_b"][0].partition_broadcast(P)).then_inc(S["lnp_in"], 16)
            act.dma_start(rw[:, :, :], I["router_w"].rearrange("(k p) e -> p k e", p=P)).then_inc(S["lnp_in"], 16)
            act.dma_start(rb[:, :], I["router_bias"].partition_broadcast(P)).then_inc(S["lnp_in"], 16)

            def mix_hi(i):
                if i == 0:
                    act.wait_ge(S["conv_ok"], 10)
                    act.wait_ge(S["o_ev"], NPAIR * NT)
                    act.wait_ge(S["gyT_ev"], NT)
                if i >= 2:
                    act.wait_ge(S["ob_ps"], 2 * (i - 1))
                act.activation(mixh[:, i % 2, :, :], mix[:, :, i * P:(i + 1) * P], ACT.Copy).then_inc(S["mixh_ok"], 1)
            mix_hi(0)
            for i in range(NT + 2):
                if i + 1 < NT:
                    mix_hi(i + 1)
                if i >= 2:
                    act.wait_ge(S["x1t_ps"], i - 1)
                    if i >= 3:
                        act.wait_ge(S["lg_ps"], i - 2)
                    act.activation(x1T[:, :, :], pz[1][:, :].rearrange("p (k t) -> p k t", k=NK), ACT.Copy).then_inc(S["x1t_ev"], 1)
                if i < NT:
                    act.wait_ge(S["bn_ok"], 4 * i + 4)
                    act.activation(rst[:, 0:1], rst[:, 0:1], ACT.Ln).then_inc(S["lrs_ok"], 1)
                    act.wait_ge(S["lrs_ok"], 2 * i + 1)
                    act.activation(rst[:, 1:2], rst[:, 0:1], ACT.Exp, scale=-0.5).then_inc(S["lrs_ok"], 1)
            act.wait_ge(S["lg_ps"], NT)
            act.activation(rs[:, :, :], pa_[:, 0:NT * NE].rearrange("p (i e) -> p i e", e=NE), ACT.Exp, scale=-1.0).then_inc(S["rexp_ok"], 1)

            def piece_hi(b, p):
                act.wait_ge(S[f"e_in{p}"], 16 * b + 16)
                if not (isinstance(b, int) and b == 0):
                    act.wait_ge(S["piece_done"], NPIECE * b - NPIECE + p + 1)
                act.activation(eh[:, p, :], er[:, p, :], ACT.Copy).then_inc(S["eh_ok"], 1)

            def x_hi(b):
                for r in range(4):
                    act.wait_ge(S["xtr_ps"], 4 * b + r + 1)
                    act.activation(xTh[:, 2 * r:2 * r + 2, :], xb[r % 2].rearrange("p (d t) -> p d t", d=2), ACT.Copy).then_inc(S["xTh_ok"], 1)

            def act_block(b, prev, nxt):
                if nxt:
                    for p in range(4):
                        piece_hi(b + 1, p)
                for fp in range(2):
                    act.wait_ge(S["piece_done"], NPIECE * b + 4 * fp + 4)
                    if fp or not (prev is False and isinstance(b, int) and b == 0):
                        act.wait_ge(S["h_ok"], 2 * b + fp)
                    act.activation(sil[:, :, :], h1b[fp].rearrange("p (f t) -> p f t", f=2), ACT.Silu).then_inc(S["sil_ok"], 1)
                    act.wait_ge(S["h_ok"], 2 * b + fp + 1)
                    act.activation(hh[:, 2 * fp:2 * fp + 2, :], hf[:, 2 * fp:2 * fp + 2, :], ACT.Copy).then_inc(S["hh_ok"], 1)
                    if nxt and fp == 0:
                        piece_hi(b + 1, 4)
                        piece_hi(b + 1, 5)
                if nxt:
                    x_hi(b + 1)
                    piece_hi(b + 1, 6)
                    piece_hi(b + 1, 7)
                for m in range(4):
                    act.wait_ge(S["piece_done"], NPIECE * b + 2 * NF + m + 1)
                    if m == 0 and not (prev is False and isinstance(b, int) and b == 0):
                        act.wait_ge(S["ytr_ps"], 2 * b)
                    act.activation(yTs[:, 2 * m:2 * m + 2, :], yb[m % 2].rearrange("p (d t) -> p d t", d=2), ACT.Copy).then_inc(S["yT_ev"], 1)
                    if nxt:
                        piece_hi(b + 1, 2 * NF + m)

            def act_pass(j):
                b0 = NE * j
                if isinstance(j, int):
                    act.wait_ge(S["ob_ps"], 2 * NT)
                    act.wait_ge(S["res_ok"], 2 * NT)
                for p in range(NPIECE):
                    piece_hi(b0, p)
                    if p == 5:
                        x_hi(b0)
                experts_of(act, j, act_block)
            passes_of(act, act_pass)

            for i in range(NT):
                act.wait_ge(S[f"cg_in{i % 2}"], 32 * (i // 2 + 1))
                act.activation(cy1[:, i % 2, :], cy1[:, i % 2, :], ACT.Copy, scale=g12[:, 0, i:i + 1]).then_inc(S["c1_ok"], 1)
                act.wait_ge(S["cbn_ok"], 4 * i + 4)
                act.activation(rst[:, 0:1], rst[:, 0:1], ACT.Ln).then_inc(S["clr_ok"], 1)
                act.wait_ge(S["clr_ok"], 2 * i + 1)
                act.activation(rst[:, 1:2], rst[:, 0:1], ACT.Exp, scale=-0.5).then_inc(S["clr_ok"], 1)

        @block.vector
        def _(dve):
            def split_lo(n):
                dve.wait_ge(S["w_hi_ok"], n + 1)
                dve.tensor_tensor(w_lo[:, n % 3, :], raw_chunk(n), w_hi[:, n % 3, :].bitcast(F32), ALU.subtract)\
                    .then_inc(S["w_lo_ok"], 1)

            for c in range(2 * NT):
                i, half = c // 2, c % 2
                dve.wait_ge(S["xt_hi"], c + 1)
                ts = slice(i * P, (i + 1) * P)
                dve.tensor_tensor(xT_lo[:, 4 * half:4 * half + 4, ts], xt_bank[c % 4].rearrange("p (k t) -> p k t", k=4),
                                  xT_hi[:, 4 * half:4 * half + 4, ts].bitcast(F32), ALU.subtract).then_inc(S["xt_lo"], 1)
            for n in range(CHUNK_N0 + 3):
                split_lo(n)

            dve.wait_ge(S["const_in"], 16 * (CONV_K + 3 + GLA_H))
            for hp in range(2):
                if hp == 1:
                    dve.wait_ge(S["dec_ok"], 1)
                for half in range(2):
                    dve.wait_ge(S["gate_ps"], 2 * hp + half + 1)
                    dve.tensor_scalar(tA[:, half * 512:half * 512 + 512], gate_bank[2 * hp + half], bg[:, hp:hp + 1], -1.0,
                                      ALU.add, ALU.mult).then_inc(S["n_ok"], 1)
                dve.wait_ge(S["n_ok"], 2 * hp + 2)
                dve.tensor_scalar(tB[:, :], tA[:, :], CLAMP, None, ALU.min).then_inc(S["m_ok"], 1)
                dve.wait_ge(S["gl_ok"], hp + 1)
                dve.tensor_tensor(tB[:, :], tB[:, :], tA[:, :], ALU.max).then_inc(S["gsp_ok"], 1)
                dve.wait_ge(S["gsp_ok"], hp + 1)
                for c in range(T // GLA_C):
                    cs = slice(c * GLA_C, (c + 1) * GLA_C)
                    dve.tensor_tensor_scan(tA[:, cs], tB[:, cs], zeros[:, :], 0.0, ALU.add, ALU.add).then_inc(S["cs_ok"], 1)
                dve.wait_ge(S["gate_ps"], 4)
                dve.wait_ge(S["gexp_ok"], 3 * hp + 1)
                dve.tensor_tensor(gq[:, hp, :], gq[:, hp, :], tB[:, :], ALU.mult).then_inc(S["gmul_ok"], 1)
                dve.wait_ge(S["gexp_ok"], 3 * hp + 2)
                dve.tensor_tensor(kin[:, hp, :], gk[:, hp, :], tC[:, :], ALU.mult).then_inc(S["gmul_ok"], 1)
                csv = tA[:, :].rearrange("p (c t) -> p c t", t=GLA_C)
                dve.wait_ge(S["gmul_ok"], 3 * hp + 1)
                dve.tensor_tensor(tB[:, :].rearrange("p (c t) -> p c t", t=GLA_C), csv,
                                  csv[:, :, GLA_C - 1:GLA_C].to_broadcast([P, T // GLA_C, GLA_C]), ALU.subtract)\
                    .then_inc(S["cs_ok"], 1)
                dve.wait_ge(S["gexp_ok"], 3 * hp + 3)
                dve.tensor_tensor(gk[:, hp, :], gk[:, hp, :], tB[:, :], ALU.mult).then_inc(S["gmul_ok"], 1)

            for n in range(CHUNK_N0 + 3, CHUNK_N0 + 6):
                split_lo(n)
            for t in range(NT):
                f = FILL_N0 + NT + t
                dve.wait_ge(S["gge_ok"], t + 1)
                dve.tensor_scalar(gg[:, t, :], gg[:, t, :], 1.0, None, ALU.add).then_inc(S["ggs_ok"], 1)
                dve.wait_ge(S["ggs_ok"], 3 * t + 1)
                dve.reciprocal(gg[:, t, :], gg[:, t, :]).then_inc(S["ggs_ok"], 1)
                dve.wait_ge(S["ggs_ok"], 3 * t + 2)
                dve.tensor_tensor(gg[:, t, :], pp[f % 2][:, 0:GLA_W], gg[:, t, :], ALU.mult).then_inc(S["gg_ev"], 1)
                dve.wait_ge(S["gg_ev"], t + 1)
                dve.tensor_tensor(gg[:, t, :].rearrange("p (h d) -> p h d", h=GLA_H), gg[:, t, :].rearrange("p (h d) -> p h d", h=GLA_H),
                                  nw[:, :].unsqueeze(1).to_broadcast([P, GLA_H, GLA_DV]), ALU.mult).then_inc(S["ggs_ok"], 1)
            for n in range(CHUNK_N0 + 6, CHUNK_N0 + 9):
                split_lo(n)

            for t in range(NT + 1):
                if t < NT:
                    dve.wait_ge(S["sc_ps"], t + 1)
                    if t >= 1:
                        dve.wait_ge(S["o_ps"], t)
                    dve.tensor_tensor(sT[:, :, :, :], sc_banks,
                                      trimask[:, :].unsqueeze(1).unsqueeze(1).to_broadcast([P, 2, 2, P]), ALU.mult).then_inc(S["sT_ok"], 1)
                if t >= 1:
                    c = t - 1
                    dve.wait_ge(S["gsq_ok"], c + 1)
                    dve.tensor_reduce(gms[:, 0:4], gsq[:, :].rearrange("p (h d) -> p h d", h=GLA_H), AX.X, ALU.add)\
                        .then_inc(S["gms_ok"], 1)
                    dve.wait_ge(S["gms_ok"], 2 * c + 1)
                    dve.tensor_scalar(gms[:, 0:4], gms[:, 0:4], 1.0 / GLA_DV, RMS_EPS, ALU.mult, ALU.add).then_inc(S["gms_ok"], 1)
                    dve.wait_ge(S["rstd_ok"], 2 * c + 2)
                    if c >= 1:
                        dve.wait_ge(S["gyT_ps"], c)
                    dve.tensor_tensor(gy[:, :].rearrange("p (h d) -> p h d", h=GLA_H), pa_[:, 0:GLA_W].rearrange("p (h d) -> p h d", h=GLA_H),
                                      gms[:, 4:8].unsqueeze(2).to_broadcast([P, GLA_H, GLA_DV]), ALU.mult).then_inc(S["gs_ok"], 1)
                    dve.wait_ge(S["gs_ok"], c + 1)
                    dve.tensor_tensor(gy[:, :], gy[:, :], gg[:, c, :], ALU.mult).then_inc(S["gy_ok"], 1)
                if t < NT:
                    dve.wait_ge(S["kv_ps"], t + 1)
                    for cc in range(2):
                        ch = 2 * t + cc
                        if ch == T // GLA_C - 1:
                            continue
                        if ch >= 3:
                            dve.wait_ge(S["o_ps"], (ch - 3) // 2 + 1)
                        if ch >= 1:
                            dve.wait_ge(S["st_ok"], 4 * ch)
                        for hp in range(2):
                            for h in range(2):
                                r = slice(hs[h], hs[h] + 64)
                                c_ = slice(h * GLA_DV, (h + 1) * GLA_DV)
                                dve.scalar_tensor_tensor(S_st[r, hp, (ch + 1) % 4, c_], S_st[r, hp, ch % 4, c_],
                                                         dec[r, hp, ch:ch + 1],
                                                         kv_bank[cc][r, hp * 192 + h * GLA_DV:hp * 192 + (h + 1) * GLA_DV],
                                                         ALU.mult, ALU.add).then_inc(S["st_ok"], 1)
            split_lo(CHUNK_F0)

            def clamp_of(u):
                W = (UNITS[u][1] + 1) * P
                dve.wait_ge(S["z_ps"], u + 1)
                dve.tensor_scalar(E[:, u % 2, 0:W], pz[u % 2][:, 0:W], CLAMP, None, ALU.min).then_inc(S["zc_ok"], 1)

            def conv_steps(ct, first):
                y = mix[:, ct, :]
                u_ = conv_in[:, 0, :]
                k = 5 * ct
                if first:
                    dve.tensor_tensor(u_, u_, conv_in[:, 1, :], ALU.mult).then_inc(S["conv_ok"], 1)
                    dve.wait_ge(S["conv_ok"], k + 1)
                    dve.tensor_scalar(y, u_, cw[:, 0, ct:ct + 1], cb[:, ct:ct + 1], ALU.mult, ALU.add).then_inc(S["conv_ok"], 1)
                    for i in range(1, CONV_K):
                        dve.wait_ge(S["conv_ok"], k + 1 + i)
                        dve.scalar_tensor_tensor(y[:, i:], u_[:, :T - i], cw[:, i, ct:ct + 1], y[:, i:], ALU.mult, ALU.add)\
                            .then_inc(S["conv_ok"], 1)
                else:
                    dve.wait_ge(S["conv_ok"], k + 4)
                    dve.tensor_tensor(y, y, conv_in[:, 2, :], ALU.mult).then_inc(S["conv_ok"], 1)

            def split_wo_lo(k):
                dve.wait_ge(S["wo_hi_ok"], k + 1)
                dve.tensor_tensor(wo_lo[:, k, :], wo_raw[:, k % 2, :], wo_hi[:, k, :].bitcast(F32), ALU.subtract).then_inc(S["wo_lo_ok"], 1)

            clamp_of(0)
            ready = []
            for u, (p, i, h) in enumerate(UNITS):
                W = (i + 1) * P
                if u + 1 < NU:
                    clamp_of(u + 1)
                q = QUARTER.get(u)
                if q is not None and q % 4 == 0 and q // 4 + 1 < len(FILL):
                    split_lo(CHUNK_F0 + q // 4 + 1)
                if u >= NU - 2:
                    for k in range(4 * (u - NU + 2), 4 * (u - NU + 3)):
                        split_wo_lo(k)
                dve.wait_ge(S["ln_ok"], u + 1)
                if u >= 2:
                    dve.wait_ge(S["aT_ps"], HALVES[u - 1])
                dve.tensor_tensor(SP[:, u % 2, 0:W], pz[u % 2][:, 0:W], E[:, u % 2, 0:W], ALU.max).then_inc(S["sp_ok"], 1)
                dve.wait_ge(S["spm_ok"], u + 1)
                dve.tensor_tensor_scan(E[:, u % 2, 0:W][:, ::-1], SP[:, u % 2, 0:W][:, ::-1], SP[:, u % 2, 0:W][:, ::-1], 0.0,
                                       ALU.add, ALU.max).then_inc(S["sfx_ok"], 1)
                dve.wait_ge(S["sfx_ok"], u + 1)
                dve.tensor_tensor(SP[:, u % 2, 0:W], pz[u % 2][:, 0:W], E[:, u % 2, 0:W], ALU.subtract).then_inc(S["arg_ok"], 1)
                for what, at_u in list(ready):
                    if at_u < u:
                        kind, j = what
                        dve.wait_ge(S["proj_ev"], ev_before(FILL_F0 + 2 * (FILL.index(what) + 1)))
                        conv_steps(j, kind == "ch")
                        ready.remove((what, at_u))
                if q is not None and q % 4 == 3 and FILL[q // 4][0] in ("ch", "cb"):
                    ready.append((FILL[q // 4], u))
            for kind, j in [w for w, _ in ready]:
                dve.wait_ge(S["proj_ev"], ev_before(FILL_F0 + 2 * (FILL.index((kind, j)) + 1)))
                conv_steps(j, kind == "ch")
            def mix_lo(i):
                dve.wait_ge(S["mixh_ok"], i + 1)
                dve.tensor_tensor(mixl[:, i % 2, :, :], mix[:, :, i * P:(i + 1) * P], mixh[:, i % 2, :, :].bitcast(F32), ALU.subtract)\
                    .then_inc(S["mixl_ok"], 1)
            mix_lo(0)
            for i in range(NT):
                if i + 1 < NT:
                    mix_lo(i + 1)
                s = i % 2
                dve.wait_ge(S[f"xr_in{s}"], 16 * (i // 2 + 1))
                if i >= 2:
                    dve.wait_ge(S[f"x1_st{s}"], 16 * (i // 2))
                    dve.wait_ge(S["x1t_ps"], i - 1)
                for half in range(2):
                    hsl = slice(half * 512, half * 512 + 512)
                    dve.wait_ge(S["ob_ps"], 2 * i + half + 1)
                    dve.scalar_tensor_tensor(x1[:, s, hsl], xres[:, s, hsl], ALPHA, ob[s][half], ALU.mult, ALU.add).then_inc(S["res_ok"], 1)
                norm_stats(dve, x1, s, "res_ok", 2 * i + 2, "bn_ok", i, "lrs_ok")
                dve.wait_ge(S["lrs_ok"], 2 * i + 2)
                dve.tensor_scalar(x1[:, s, :], x1[:, s, :], bna[:, 0:1], rst[:, 1:2], ALU.subtract, ALU.mult).then_inc(S["x1_ok"], 1)
                if i == 0:
                    dve.wait_ge(S["lnp_in"], 16 * 4)
                for a, op in ((0, ALU.mult), (1, ALU.add)):
                    dve.wait_ge(S["x1_ok"], 3 * i + a + 1)
                    dve.tensor_tensor(x1[:, s, :], x1[:, s, :], lnp[:, a, :], op).then_inc(S["x1_ok"], 1)

            step = [0]

            def link(ins):
                step[0] += 1
                ins.then_inc(S["route_step"], 1)
                dve.wait_ge(S["route_step"], step[0])

            def grp(t_):
                return t_[:, :, :].rearrange("p i (g j) -> p (i g) j", j=EPG)

            bc = lambda t_, n: t_.unsqueeze(1).to_broadcast([P, n, t_.shape[-1]])
            dve.wait_ge(S["rexp_ok"], 1)
            dve.wait_ge(S["tokc_ok"], 8)
            dve.wait_ge(S["mixl_ok"], NT)
            link(dve.tensor_scalar(rs[:, :, :], rs[:, :, :], 1.0, None, ALU.add))
            link(dve.reciprocal(rs[:, :, :], rs[:, :, :]))
            link(dve.tensor_tensor(rsel[:, :, :].rearrange("p (i g) j -> p i (g j)", g=NGRP), rs[:, :, :], bc(rb[:, :], NT), ALU.add))
            dve.tensor_tensor(rpair[:, :, 0:3], rsel[:, :, 0:3], rsel[:, :, 1:4], ALU.add).then_inc(S["route_step"], 1)
            dve.tensor_tensor(rpair[:, :, 3:5], rsel[:, :, 0:2], rsel[:, :, 2:4], ALU.add).then_inc(S["route_step"], 1)
            step[0] += 2
            link(dve.tensor_tensor(rpair[:, :, 5:6], rsel[:, :, 0:1], rsel[:, :, 3:4], ALU.add))
            link(dve.tensor_reduce(rgs[:, :, :].rearrange("p i g -> p (i g)"), rpair[:, :, :], AX.X, ALU.max))

            def ranks(v, r, n):
                link(dve.tensor_copy(r, bc(rank0[:, :], n)))
                for d in range(1, EPG):
                    m = EPG - d
                    ge = rge[:, 0:n, 0:m]
                    link(dve.tensor_tensor(ge, v[:, :, 0:m], v[:, :, d:EPG], ALU.is_ge))
                    link(dve.tensor_tensor(r[:, :, d:EPG], r[:, :, d:EPG], ge, ALU.add))
                    link(dve.tensor_tensor(r[:, :, 0:m], r[:, :, 0:m], ge, ALU.subtract))
            ranks(rgs[:, :, :], rgk[:, :, :], NT)
            ranks(rsel[:, :, :], rek[:, :, :], NT * NGRP)
            link(dve.tensor_scalar(rgk[:, :, :], rgk[:, :, :], 0.0, None, ALU.is_equal))
            link(dve.scalar_tensor_tensor(grp(rmask), rek[:, :, :], 2.0,
                                          rgk[:, :, :].rearrange("p i g -> p (i g)").unsqueeze(2).to_broadcast([P, NT * NGRP, EPG]),
                                          ALU.is_lt, ALU.mult))
            dve.tensor_copy(rmb[:, :, :], rmask[:, :, :]).then_inc(S["mask_ok"], 1)
            link(dve.tensor_tensor(rgate[:, :, :], rs[:, :, :], rmask[:, :, :], ALU.mult))
            link(dve.tensor_reduce(rden[:, :], rgate[:, :, :], AX.X, ALU.add))
            link(dve.reciprocal(rden[:, :], rden[:, :]))
            link(dve.tensor_tensor(rgate[:, :, :], rgate[:, :, :], rden[:, :].unsqueeze(2).to_broadcast([P, NT, NE]), ALU.mult))
            dve.wait_ge(S["pos_ps"], 1)
            link(dve.tensor_copy(rpos[:, :, :], po[:, 0:(NT + 1) * NE].rearrange("p (i e) -> p i e", e=NE)))
            link(dve.tensor_reduce(rmax[:, :], rpos[:, NT, :], AX.X, ALU.max))
            link(dve.tensor_scalar(pcmp[:, :], passes[:, :], rmax[:, 0:1], None, ALU.is_lt))
            link(dve.tensor_reduce(rnp[:, :], pcmp[:, :], AX.X, ALU.add))
            dve.tensor_scalar(npi[:, :], rnp[:, :], 1.0, None, ALU.add).then_inc(S["route_ok"], 1)
            link(dve.tensor_tensor(rrow[:, :, :], rpos[:, 0:NT, :], bc(ecol[:, :], NT), ALU.add))
            for j in range(1, MAXPASS):
                link(dve.tensor_scalar(rtmp[:, :, :], rpos[:, 0:NT, :], float(j * TW), float((NE - 1) * TW), ALU.is_ge, ALU.mult))
                link(dve.tensor_tensor(rrow[:, :, :], rrow[:, :, :], rtmp[:, :, :], ALU.add))
            link(dve.scalar_tensor_tensor(rtmp[:, :, :], rrow[:, :, :], -BIG, rmask[:, :, :], ALU.add, ALU.mult))
            link(dve.tensor_reduce(rr12[:, 0, :], rtmp[:, :, :], AX.X, ALU.min))
            link(dve.scalar_tensor_tensor(rtmp[:, :, :], rrow[:, :, :], 1.0, rmask[:, :, :], ALU.add, ALU.mult))
            link(dve.tensor_reduce(rr12[:, 1, :], rtmp[:, :, :], AX.X, ALU.max))
            link(dve.tensor_scalar(rr12[:, 0, :], rr12[:, 0, :], BIG, None, ALU.add))
            link(dve.tensor_scalar(rr12[:, 1, :], rr12[:, 1, :], -1.0, None, ALU.add))
            dve.tensor_copy(rows_u[:, 0, :], rr12[:, 0, :]).then_inc(S["route_ok"], 1)
            dve.tensor_copy(rows_u[:, 1, :], rr12[:, 1, :]).then_inc(S["route_ok"], 1)
            for c in range(2):
                link(dve.tensor_tensor(rtmp[:, :, :], rrow[:, :, :], rr12[:, c, :].unsqueeze(2).to_broadcast([P, NT, NE]), ALU.is_equal))
                link(dve.tensor_tensor(rtmp[:, :, :], rtmp[:, :, :], rgate[:, :, :], ALU.mult))
                link(dve.tensor_reduce(g12[:, c, :], rtmp[:, :, :], AX.X, ALU.add))

            def piece_lo(b, p):
                dve.wait_ge(S["eh_ok"], NPIECE * b + p + 1)
                dve.tensor_tensor(el[:, p, :], er[:, p, :], eh[:, p, :].bitcast(F32), ALU.subtract).then_inc(S["el_ok"], 1)

            def x_lo(b):
                for r in range(4):
                    dve.wait_ge(S["xTh_ok"], 4 * b + r + 1)
                    dve.tensor_tensor(xTl[:, 2 * r:2 * r + 2, :], xb[r % 2].rearrange("p (d t) -> p d t", d=2),
                                      xTh[:, 2 * r:2 * r + 2, :].bitcast(F32), ALU.subtract).then_inc(S["xTl_ok"], 1)

            def rows_a(b):
                dve.wait_ge(S["ytr_ps"], 2 * b + 1)
                dve.wait_ge(S["y_out"], 32 * b)
                dve.tensor_copy(yA[:, :], pz[1][:, :]).then_inc(S["yA_ev"], 1)

            def rows_b(b):
                dve.wait_ge(S["ytr_ps"], 2 * b + 2)
                dve.tensor_copy(yB[:, :], pz[1][0:TR, :]).then_inc(S["yB_ev"], 1)

            def dve_block(b, prev, nxt):
                if nxt:
                    piece_lo(b + 1, 0)
                    piece_lo(b + 1, 1)
                if prev:
                    rows_a(b - 1)
                if nxt:
                    piece_lo(b + 1, 2)
                    piece_lo(b + 1, 3)
                if prev:
                    rows_b(b - 1)
                for fp in range(2):
                    dve.wait_ge(S["sil_ok"], 2 * b + fp + 1)
                    if not (prev is False and isinstance(b, int) and b == 0):
                        dve.wait_ge(S["hl_ok"], 2 * b + fp - 1)
                    dve.tensor_tensor(hf[:, 2 * fp:2 * fp + 2, :], sil[:, :, :], h3b[fp].rearrange("p (f t) -> p f t", f=2), ALU.mult).then_inc(S["h_ok"], 1)
                    dve.wait_ge(S["hh_ok"], 2 * b + fp + 1)
                    dve.tensor_tensor(hl[:, 2 * fp:2 * fp + 2, :], hf[:, 2 * fp:2 * fp + 2, :], hh[:, 2 * fp:2 * fp + 2, :].bitcast(F32), ALU.subtract)\
                        .then_inc(S["hl_ok"], 1)
                    if nxt and fp == 0:
                        piece_lo(b + 1, 4)
                        piece_lo(b + 1, 5)
                if nxt:
                    x_lo(b + 1)
                    for p in range(6, NPIECE):
                        piece_lo(b + 1, p)
                else:
                    rows_a(b)
                    rows_b(b)

            def dve_pass(j):
                b0 = NE * j
                for p in range(NPIECE):
                    piece_lo(b0, p)
                    if p == 5:
                        x_lo(b0)
                experts_of(dve, j, dve_block)
            npass = passes_of(dve, dve_pass)

            for i in range(NT):
                s = i % 2
                if i == 0:
                    dve.wait_ge(S["y_out"], npass * (32 * NE))
                dve.wait_ge(S["c1_ok"], i + 1)
                dve.scalar_tensor_tensor(cy1[:, s, :], cy2[:, s, :], g12[:, 1, i:i + 1], cy1[:, s, :], ALU.mult, ALU.add).then_inc(S["c2_ok"], 1)
                dve.wait_ge(S["c2_ok"], i + 1)
                dve.wait_ge(S[f"cx_in{s}"], 16 * (i // 2 + 1))
                if i >= 2:
                    dve.wait_ge(S[f"out_st{s}"], 16 * (i // 2))
                dve.scalar_tensor_tensor(cr[:, s, :], cx[:, s, :], ALPHA, cy1[:, s, :], ALU.mult, ALU.add).then_inc(S["cres_ok"], 1)
                norm_stats(dve, cr, s, "cres_ok", i + 1, "cbn_ok", i, "clr_ok")
                dve.wait_ge(S["clr_ok"], 2 * i + 2)
                dve.tensor_scalar(cr[:, s, :], cr[:, s, :], bna[:, 0:1], rst[:, 1:2], ALU.subtract, ALU.mult).then_inc(S["cnorm_ok"], 1)
                if i == 0:
                    dve.wait_ge(S["lnq_in"], 32)
                dve.wait_ge(S["cnorm_ok"], i + 1)
                dve.tensor_tensor(cr[:, s, :], cr[:, s, :], lnq[:, 0, :], ALU.mult).then_inc(S["cout_ok"], 1)


_INS = ["x", "w_in", "conv_w", "conv_b", "gla_w_gate2", "gla_b_gate", "gla_norm_w", "w_out", "ln1_g", "ln1_b",
        "router_w", "router_bias", "w1", "w3", "w2", "ln2_g", "ln2_b"]


def kernel(**inputs):
    import numpy as np
    import concourse.bacc as bacc
    from concourse.bass_utils import run_bass_kernel_spmd

    nc = bacc.Bacc("TRN2", target_bir_lowering=False, num_devices=1)
    arrays, aps = {}, {}
    for name in _INS:
        a = np.ascontiguousarray(inputs[name])
        arrays[f"in_{name}_dram"] = a
        aps[name] = nc.dram_tensor(f"in_{name}_dram", a.shape, mybir.dt.from_np(a.dtype), kind="ExternalInput").ap()
    out = nc.dram_tensor("out_0_dram", (1, T, D), F32, kind="ExternalOutput").ap()
    build(nc, aps, out)
    r = run_bass_kernel_spmd(nc, [arrays], core_ids=[0])
    return r.results[0]["out_0_dram"]
```

```python
import math

import concourse.bass as bass
from concourse import mybir
from contextlib import ExitStack

F32, F32R, BF16 = mybir.dt.float32, mybir.dt.float32r, mybir.dt.bfloat16
I32, U32 = mybir.dt.int32, mybir.dt.uint32
ALU = mybir.AluOpType
ACT = mybir.ActivationFunctionType
AX = mybir.AxisListType

P = 128
D = 1024
T = 1024
NT = T // P
NK = D // P
CONV_W = D // 4
CONV_K = 3
SB_H, SB_D = 6, 64
SB_W = SB_H * SB_D
GLA_H, GLA_DV, GLA_DK, GLA_R, GLA_C = 4, 96, 48, 16, 64
GLA_W = GLA_H * GLA_DV
GLA_KW = GLA_H * GLA_DK
OFF = {}
_at = 0
for _n, _s in (("c_h", CONV_W), ("c_b", CONV_W), ("c_c", CONV_W), ("sb_q", SB_W), ("sb_k", SB_W), ("sb_v", SB_W),
               ("g_q", GLA_KW), ("g_k", GLA_KW), ("g_v", GLA_W), ("g_g", GLA_W), ("g_lr", GLA_R)):
    OFF[_n] = _at
    _at += _s
D_PROJ = _at
GATE_NORM = 16.0
CLAMP = 40.0
RMS_EPS = 1e-6
LN_EPS = 1e-5
ALPHA = 2 ** 0.25
NPAIR = SB_H // 2

T_FIRST = [("gq", 0), ("gk", 0), ("gq", 1), ("gk", 1), ("sq", 0), ("sk", 0)]
N_PIECES = ["g_v", "g_g", "sb_v"]
FILL = [("sq", 1), ("sk", 1), ("cc", 0), ("ch", 0), ("sq", 2), ("sk", 2), ("cb", 0), ("cc", 1), ("ch", 1), ("cb", 1)]
NCHUNK_T = len(T_FIRST)
CHUNK_N0 = NCHUNK_T
CHUNK_F0 = NCHUNK_T + 3 * len(N_PIECES)
NCHUNK = CHUNK_F0 + len(FILL)
FILL_T0 = 0
FILL_N0 = 2 * NCHUNK_T
FILL_F0 = FILL_N0 + NT * len(N_PIECES)
NFILL = FILL_F0 + 2 * len(FILL)
GG_FIRST, GG_LAST = FILL_N0 + NT, FILL_N0 + 2 * NT

UNITS = [(p, i, h) for p in range(NPAIR) for i in range(NT) for h in range(2)]
NU = len(UNITS)
HALVES = [0]
for _p, _i, _h in UNITS:
    HALVES.append(HALVES[-1] + (1 if _i < 4 else 2))
QUARTER = {}
_q = 0
for _u, (_p, _i, _h) in enumerate(UNITS):
    if _i >= 1 and _q < 4 * len(FILL):
        QUARTER[_u] = _q
        _q += 1
assert _q == 4 * len(FILL)


def ev_before(f):
    return f - max(0, min(f, GG_LAST) - GG_FIRST)


def gg_before(f):
    return max(0, min(f, GG_LAST) - GG_FIRST)

NE, NGRP = 16, 4
EPG = NE // NGRP
DE = 512
NF = DE // P
TW = 160
TR = TW - P
MAXPASS = -(-T // TW)
NROW = MAXPASS * NE * TW
NPIECE = 3 * NF
BIG = float(1 << 20)


def build(nc, I, out):
    ctx = ExitStack()
    with ctx:
        base = 16512

        def at(name, offset, shape, dt=F32):
            return nc.alloc_sbuf_tensor_at(name, shape, dt, offset=base + offset)

        def sem(name):
            return ctx.enter_context(nc.semaphore(name))

        K = 1024
        xT_hi = at("xT_hi", 0, [P, NK, T], F32R)
        xT_lo = at("xT_lo", 32 * K, [P, NK, T], F32R)
        w_raw = at("w_raw", 64 * K, [P, 2, D])
        w_hi = at("w_hi", 72 * K, [P, 3, D], F32R)
        w_lo = at("w_lo", 84 * K, [P, 3, D], F32R)
        mix = at("mix", 96 * K, [P, NK, T])
        kin = at("kin", 96 * K, [P, 2, T])
        tA = at("tA", 104 * K, [P, T])
        tB = at("tB", 108 * K, [P, T])
        tC = at("tC", 112 * K, [P, T])
        sv = at("sv", 128 * K, [P, NT, SB_W])
        qk0 = at("qk0", 140 * K, [P, 2, T])
        x_row = at("x_row", 140 * K, [P, 2, D])
        R = 148 * K
        gq = at("gq", R, [P, 2, T])
        gk = at("gk", R + 8 * K, [P, 2, T])
        gv = at("gv", R + 16 * K, [P, NT, GLA_W])
        gg = at("gg", R + 28 * K, [P, NT, GLA_W])
        w_rawg = at("w_rawg", R + 16 * K, [P, 4, NK, P])
        S_st = at("S_st", R + 40 * K, [P, 2, 4, 2 * GLA_DV])
        kteN = at("kteN", R + 46 * K, [P, 2, P])
        sT = at("sT", R + 47 * K, [P, 2, 2, P])
        gy = at("gy", R + 49 * K, [P, GLA_W])
        gsq = at("gsq", R + 50 * K + 512, [P, GLA_W])
        gms = at("gms", R + 52 * K, [P, 8])
        E = at("E", R, [P, 2, T])
        SP = at("SP", R + 8 * K, [P, 2, T])
        aT = at("aT", R + 16 * K, [P, 2, NT, P])
        conv_in = at("conv_in", R + 24 * K, [P, 3, T])
        qk1 = at("qk1", R + 36 * K, [P, 2, T])
        C0 = R + 53 * K
        ident = at("ident", C0, [P, P])
        trimask = at("trimask", C0 + 512, [P, P])
        wg2 = at("wg2", C0 + 1024, [64, 4, 64])
        nw = at("nw", C0 + 2048, [P, GLA_DV])
        cw = at("cw", C0 + 2432, [P, CONV_K, 2])
        cb = at("cb", C0 + 2464, [P, 2])
        bg = at("bg", C0 + 2496, [P, 2])
        dec = at("dec", C0 + 2528, [P, 2, T // GLA_C])
        zb = at("zb", C0 + 2656, [P, GLA_W], BF16)
        zeros = at("zeros", C0 + 3424, [P, GLA_C])

        pp = [ctx.enter_context(nc.psum_tensor(f"bank{i}", [P, 512], F32)) for i in range(2)]
        pz = [ctx.enter_context(nc.psum_tensor(f"pz{i}", [P, 1024], F32)) for i in range(2)]
        pa_ = ctx.enter_context(nc.psum_tensor("bank6", [P, 512], F32))
        po = ctx.enter_context(nc.psum_tensor("bank7", [P, 512], F32))
        xt_bank = [pp[0][:, :], pp[1][:, :], pz[0][:, 0:512], pz[0][:, 512:1024]]
        gate_bank = [pz[0][:, 0:512], pz[0][:, 512:1024], pz[1][:, 0:512], pz[1][:, 512:1024]]
        sc_banks = pz[0][:, :].rearrange("p (b x) -> p b x", b=2)[:, :, 0:2 * P].rearrange("p b (j t) -> p b j t", j=2)
        kt_bank = pz[1][:, 0:2 * P]
        kv_bank = [pz[1][:, 0:384], pz[1][:, 512:512 + 384]]

        wo_hi = at("wo_hi", 0, [P, NK, D], F32R)
        wo_lo = at("wo_lo", 32 * K, [P, NK, D], F32R)
        wo_raw = at("wo_raw", 64 * K, [P, 2, D])
        mixh = at("mixh", 72 * K, [P, 2, NK, P], F32R)
        mixl = at("mixl", 80 * K, [P, 2, NK, P], F32R)
        xres = at("xres", 88 * K, [P, 2, D])
        x1 = at("x1", 128 * K, [P, 2, D])
        x1T = at("x1T", 136 * K, [P, NK, P])
        lnp = at("lnp", 140 * K, [P, 2, D])
        SMALL = {F32: 4, U32: 4, I32: 4, BF16: 2}
        place = [R + 48 * K]

        def small(name, shape, dt=F32):
            place[0] += -place[0] % 32
            t = at(name, place[0], shape, dt)
            place[0] += math.prod(shape[1:]) * SMALL[dt]
            return t

        rw = small("rw", [P, NK, NE])
        rb = small("rb", [P, NE])
        rank0 = small("rank0", [P, EPG])
        ecol = small("ecol", [P, NE])
        tok = small("tok", [P, NT], U32)
        rows_u = small("rows_u", [P, 2, NT], U32)
        g12 = small("g12", [P, 2, NT])
        npi = small("npi", [P, 1], I32)
        bns = small("bns", [P, 2, 6])
        bna = small("bna", [P, 2])
        rst = small("rst", [P, 2])
        passes = small("passes", [P, MAXPASS - 1])
        pcmp = small("pcmp", [P, MAXPASS - 1])
        zidl = small("zidl", [P, NROW // P], U32)
        trib = small("trib", [P, P], BF16)
        oneb = small("oneb", [P, P], BF16)
        idxA = small("idxA", [P, 1], U32)
        idxB = small("idxB", [TR, 1], U32)
        M = 96 * K
        assert place[0] <= R + 53 * K
        rt = lambda n, o, s, dt=F32: at(n, M + o, s, dt)
        place[0] = M
        rs = small("rs", [P, NT, NE])
        rsel = small("rsel", [P, NT * NGRP, EPG])
        rpair = small("rpair", [P, NT * NGRP, 6])
        rgs = small("rgs", [P, NT, NGRP])
        rgk = small("rgk", [P, NT, NGRP])
        rge = small("rge", [P, NT * NGRP, 3])
        rek = small("rek", [P, NT * NGRP, EPG])
        rmask = small("rmask", [P, NT, NE])
        rgate = small("rgate", [P, NT, NE])
        rden = small("rden", [P, NT])
        rmb = small("rmb", [P, NT, NE], BF16)
        rpos = small("rpos", [P, NT + 1, NE])
        rrow = small("rrow", [P, NT, NE])
        rtmp = small("rtmp", [P, NT, NE])
        rr12 = small("rr12", [P, 2, NT])
        rmax = small("rmax", [P, 1])
        rnp = small("rnp", [P, 1])
        er = at("er", R, [P, NPIECE, D])
        eh = at("eh", 0, [P, NPIECE, D], F32R)
        el = at("el", 48 * K, [P, NPIECE, D], F32R)
        xgA = rt("xgA", 6 * K, [P, D])
        xgB = rt("xgB", 10 * K, [TR, D])
        xT2 = rt("xT2", 14 * K, [P, NK, 2, TW], F32R)
        cross = rt("cross", 24 * K, [P, 2, 2, TW])
        gu = rt("gu", 24 * K + 2560, [P, 2, 2, TW])
        sil = rt("sil", 24 * K + 5120, [P, 2, TW])
        hf = rt("hf", 24 * K + 6400, [P, NF, TW])
        hh = rt("hh", 24 * K + 8960, [P, NF, TW], F32R)
        hl = rt("hl", 24 * K + 11520, [P, NF, TW], F32R)
        yA = rt("yA", 38 * K, [P, D])
        yB = rt("yB", 42 * K, [TR, D])
        zrow = at("zrow", 144 * K, [P, D])
        cy1 = at("cy1", 0, [P, 2, D])
        cy2 = at("cy2", 8 * K, [P, 2, D])
        cx = at("cx", 16 * K, [P, 2, D])
        cr = at("cr", 24 * K, [P, 2, D])
        lnq = at("lnq", 32 * K, [P, 2, D])

        x1_dram = nc.dram_tensor("x1_scratch", [T, D], F32).ap()
        y_dram = nc.dram_tensor("y_scratch", [NROW, D], F32).ap()
        idl_dram = nc.dram_tensor("slot_tokens", [NROW, 1], U32).ap()
        ob = [[pp[0][:, :], pp[1][:, :]], [pz[0][:, 0:512], pz[0][:, 512:1024]]]
        xb = [pa_[:, 0:2 * TW], po[:, 0:2 * TW]]
        names = ("x_in0 x_in1 xt_ps xt_hi xt_lo w_in0 w_in1 wg_in w_hi_ok w_lo_ok proj_ps proj_ev gg_ev "
                 "const_in const_ok gate_ps n_ok m_ok ge_ok gl_ok gsp_ok cs_ok gexp_ok gmul_ok dec_ok sc_ps kt_ps kteN_ok sT_ok "
                 "kv_ps st_ok o_ps gsq_ok gms_ok rstd_ok gy_ok gyT_ps gyT_ev gs_ok "
                 "z_ps zc_ok e_ok ln_ok sp_ok spm_ok sfx_ok arg_ok a_ok am_ok aT_ps aT_ev o_done o_ev conv_ok ggs_ok gge_ok stored").split()
        names += ("wo_in0 wo_in1 wo_hi_ok wo_lo_ok xr_in0 xr_in1 lnp_in mixh_ok mixl_ok ob_ps res_ok bn_ok lrs_ok x1_ok x1_st0 x1_st1 "
                  "x1t_ps x1t_ev lg_ps rexp_ok route_step mask_ok pos_ps route_ok tokc_ok idl_z idl_st idx_in pool_go zrow_ok y_zero xg_in "
                  "piece_done eh_ok el_ok cross_ok sum_ok sil_ok h_ok hh_ok hl_ok xtr_ps xTh_ok xTl_ok rowsA_ps yA0_ev yA1_ev yB0_ev yB1_ev y_out "
                  "cg_in0 cg_in1 cx_in0 cx_in1 lnq_in c1_ok c2_ok cres_ok cbn_ok clr_ok cnm_ok cnorm_ok cout_ok cfin_ok out_st0 out_st1").split()
        names += [f"e_in{p}" for p in range(NPIECE)]
        S = {n: sem(n) for n in names}

        block = ctx.enter_context(nc.Block())
        hs = [0, 64]

        def w_cols(n):
            if n < CHUNK_F0:
                m = n - CHUNK_N0
                return OFF[N_PIECES[m // 3]] + P * (m % 3)
            kind, j = FILL[n - CHUNK_F0]
            return OFF[{"sq": "sb_q", "sk": "sb_k", "cc": "c_c", "ch": "c_h", "cb": "c_b"}[kind]] + P * j

        def raw_chunk(n):
            return w_rawg[:, n, :, :].rearrange("p k c -> p (k c)") if n < 4 else w_raw[:, n % 2, :]

        w_k = I["w_in"][0].rearrange("(k p) n -> p k n", p=P)

        w1v = I["w1"][0].rearrange("e (k p) f -> p e k f", p=P)
        w3v = I["w3"][0].rearrange("e (k p) f -> p e k f", p=P)
        w2v = I["w2"][0].rearrange("e (f p) d -> p e f d", p=P)

        def load_expert(sp, j, e, first=False):
            b = NE * j + e
            for p in range(NPIECE):
                if not first:
                    sp.wait_ge(S["el_ok"], NPIECE * b - NPIECE + p + 1)
                if p < 2 * NF:
                    src = (w1v, w3v)[p % 2][:, bass.ds(e, 1), :, (p // 2) * P:(p // 2 + 1) * P]
                    dst = er[:, p:p + 1, :].rearrange("p e (k f) -> p e k f", k=NK)
                else:
                    src = w2v[:, bass.ds(e, 1), p - 2 * NF, :]
                    dst = er[:, p:p + 1, :]
                sp.dma_start(dst, src).then_inc(S[f"e_in{p}"], 16)

        def passes_of(eng, one_pass):
            one_pass(0)
            eng.wait_ge(S["route_ok"], 3)
            n = eng.value_load(npi[0:1, 0:1], min_val=1, max_val=MAXPASS)
            with eng.If(n > 1):
                with eng.Fori(1, n) as j:
                    one_pass(j)
            return n

        def experts_of(eng, j, block):
            block(NE * j, True)
            with eng.Fori(1, NE - 1) as e:
                block(NE * j + e, True)
            block(NE * j + NE - 1, False)

        def first_block(b):
            return isinstance(b, int) and b == 0

        def norm_stats(dve, buf, s, src, n, done, i, read):
            dve.wait_ge(S[src], n)
            for h in range(2):
                dve.bn_stats(bns[:, h, :], buf[:, s, h * 512:h * 512 + 512]).then_inc(S[done], 1)
            dve.wait_ge(S[done], 4 * i + 2)
            dve.bn_aggr(bna[:, :], bns[:, :, :].rearrange("p a b -> p (a b)")).then_inc(S[done], 1)
            dve.wait_ge(S[done], 4 * i + 3)
            dve.tensor_scalar(rst[:, 0:1], bna[:, 1:2], LN_EPS, None, ALU.add).then_inc(S[done], 1)

        def add_bias(pool, i):
            pool.wait_ge(S["cout_ok"], i + 1)
            pool.wait_ge(S["lnq_in"], 32)
            pool.tensor_tensor(cr[:, i % 2, :], cr[:, i % 2, :], lnq[:, 1, :], ALU.add).then_inc(S["cfin_ok"], 1)

        @block.sync
        def _(sp):
            for i in range(NT):
                if i >= 2:
                    sp.wait_ge(S["xt_ps"], 2 * (i - 1))
                sp.dma_start(x_row[:, i % 2, :], I["x"][0, i * P:(i + 1) * P, :]).then_inc(S[f"x_in{i % 2}"], 16)
                if i == 1:
                    sp.wait_ge(S["const_ok"], 5)
                    for n in range(4):
                        kind, hp = T_FIRST[n]
                        src = OFF["g_q"] if kind == "gq" else OFF["g_k"]
                        for h in range(2):
                            c0 = src + (2 * hp + h) * GLA_DK
                            sp.dma_start(w_rawg[:, n, :, hs[h]:hs[h] + GLA_DK], w_k[:, :, c0:c0 + GLA_DK]).then_inc(S["wg_in"], 16)
                    sp.dma_start(w_rawg[:, 1, :, GLA_DK:64], w_k[:, :, OFF["g_lr"]:OFF["g_lr"] + GLA_R]).then_inc(S["wg_in"], 16)
            for n in range(4, NCHUNK):
                if n >= 6:
                    sp.wait_ge(S["w_lo_ok"], n - 1)
                if n < 6:
                    kind, j = T_FIRST[n]
                    c0 = OFF["sb_q" if kind == "sq" else "sb_k"] + P * j
                else:
                    c0 = w_cols(n)
                sp.dma_start(w_raw[:, n % 2, :].rearrange("p (k c) -> p k c", k=NK), w_k[:, :, c0:c0 + P])\
                    .then_inc(S[f"w_in{n % 2}"], 16)
            w_o = I["w_out"][0].rearrange("(k p) n -> p k n", p=P)
            for k in range(NK):
                if k < 2:
                    sp.wait_ge(S["w_lo_ok"], NCHUNK)
                else:
                    sp.wait_ge(S["wo_lo_ok"], k - 1)
                sp.dma_start(wo_raw[:, k % 2, :], w_o[:, k, :]).then_inc(S[f"wo_in{k % 2}"], 16)
            sp.wait_ge(S["proj_ps"], NFILL)
            for i in range(NT):
                if i >= 2:
                    sp.wait_ge(S["res_ok"], 2 * (i - 1))
                sp.dma_start(xres[:, i % 2, :], I["x"][0, i * P:(i + 1) * P, :]).then_inc(S[f"xr_in{i % 2}"], 16)
                if i == 1:
                    sp.wait_ge(S["o_ev"], NPAIR * NT)
                    sp.wait_ge(S["arg_ok"], NU)
                    sp.wait_ge(S["aT_ev"], HALVES[NU])
                    sp.wait_ge(S["conv_ok"], 10)
                    load_expert(sp, 0, 0, first=True)
                if i >= 1:
                    sp.wait_ge(S["x1_ok"], 3 * i)
                    sp.dma_start(x1_dram[(i - 1) * P:i * P, :], x1[:, (i - 1) % 2, :]).then_inc(S[f"x1_st{(i - 1) % 2}"], 16)
            sp.wait_ge(S["x1_ok"], 3 * NT)
            sp.dma_start(x1_dram[(NT - 1) * P:NT * P, :], x1[:, (NT - 1) % 2, :]).then_inc(S[f"x1_st{(NT - 1) % 2}"], 16)
            with sp.Fori(1, NE) as e:
                load_expert(sp, 0, e)
            sp.wait_ge(S["route_ok"], 3)
            npass = sp.value_load(npi[0:1, 0:1], min_val=1, max_val=MAXPASS)
            with sp.If(npass > 1):
                with sp.Fori(1, npass) as j:
                    with sp.Fori(0, NE) as e:
                        load_expert(sp, j, e)
            sp.wait_ge(S["y_out"], npass * (32 * NE))
            for i in range(NT):
                if i >= 2:
                    sp.wait_ge(S["cres_ok"], i - 1)
                sp.dma_start(cx[:, i % 2, :], x1_dram[i * P:(i + 1) * P, :]).then_inc(S[f"cx_in{i % 2}"], 16)
                if i == 0:
                    for a, name in enumerate(("ln2_g", "ln2_b")):
                        sp.dma_start(lnq[:, a, :], I[name][0].partition_broadcast(P)).then_inc(S["lnq_in"], 16)
                if i >= 1:
                    sp.wait_ge(S["cfin_ok"], i)
                    sp.dma_start(out[0, (i - 1) * P:i * P, :], cr[:, (i - 1) % 2, :]).then_inc(S[f"out_st{(i - 1) % 2}"], 16)
            sp.wait_ge(S["cfin_ok"], NT)
            sp.dma_start(out[0, (NT - 1) * P:NT * P, :], cr[:, (NT - 1) % 2, :]).then_inc(S[f"out_st{(NT - 1) % 2}"], 16)
            for s in range(2):
                sp.wait_ge(S[f"out_st{s}"], 16 * (NT // 2))

        @block.gpsimd
        def _(pool):
            pool.memset(w_rawg[:, :, :, :], 0.0).then_inc(S["const_ok"], 1)
            pool.memset(wg2[:, :, :], 0.0).then_inc(S["const_ok"], 1)
            pool.memset(bg[:, :], 0.0).then_inc(S["const_ok"], 1)
            pool.memset(ident[:, :], 0.0).then_inc(S["const_ok"], 1)
            pool.memset(trimask[:, :], 1.0).then_inc(S["const_ok"], 1)
            pool.memset(zb[:, :], 0.0).then_inc(S["const_ok"], 1)
            pool.memset(zeros[:, :], 0.0).then_inc(S["const_ok"], 1)
            pool.memset(S_st[:, :, :, :], 0.0).then_inc(S["const_ok"], 1)
            pool.wait_ge(S["const_ok"], 8)
            pool.affine_select(ident[:, :], ident[:, :], [[-1, P]], ALU.not_equal, 1.0, base=0, channel_multiplier=1)\
                .then_inc(S["const_ok"], 1)
            pool.affine_select(trimask[:, :], trimask[:, :], [[1, P]], ALU.is_ge, 0.0, base=0, channel_multiplier=-1)\
                .then_inc(S["const_ok"], 1)
            pool.wait_ge(S["const_ok"], 10)
            pool.memset(trimask[0:64, 64:P], 0.0).then_inc(S["const_ok"], 1)
            for u, (p, i, h) in enumerate(UNITS):
                own = slice(i * P, (i + 1) * P)
                pool.wait_ge(S["sp_ok"], u + 1)
                pool.affine_select(SP[:, u % 2, own], SP[:, u % 2, own], [[-1, P]], ALU.is_gt, 0.0,
                                   base=0, channel_multiplier=1).then_inc(S["spm_ok"], 1)
                pool.wait_ge(S["a_ok"], u + 1)
                pool.affine_select(SP[:, u % 2, own], SP[:, u % 2, own], [[-1, P]], ALU.is_gt, 0.0,
                                   base=0, channel_multiplier=1).then_inc(S["am_ok"], 1)

            pool.wait_ge(S["aT_ev"], HALVES[NU])
            pool.memset(zidl[:, :], 0).then_inc(S["tokc_ok"], 1)
            pool.memset(trib[:, :], 1.0).then_inc(S["tokc_ok"], 1)
            pool.memset(oneb[:, :], 1.0).then_inc(S["tokc_ok"], 1)
            pool.iota(tok[:, :], [[P, NT]], base=0, channel_multiplier=1).then_inc(S["tokc_ok"], 1)
            pool.iota(ecol[:, :], [[TW, NE]], base=0, channel_multiplier=0, allow_small_or_imprecise_dtypes=True).then_inc(S["tokc_ok"], 1)
            pool.iota(rank0[:, :], [[-1, EPG]], base=EPG - 1, channel_multiplier=0, allow_small_or_imprecise_dtypes=True).then_inc(S["tokc_ok"], 1)
            pool.iota(passes[:, :], [[TW, MAXPASS - 1]], base=TW, channel_multiplier=0, allow_small_or_imprecise_dtypes=True).then_inc(S["tokc_ok"], 1)
            pool.wait_ge(S["tokc_ok"], 7)
            pool.affine_select(trib[:, :], trib[:, :], [[1, P]], ALU.is_gt, 0.0, base=0, channel_multiplier=-1).then_inc(S["tokc_ok"], 1)
            pool.dma_start(idl_dram.rearrange("(p c) o -> p (c o)", p=P), zidl[:, :]).then_inc(S["idl_z"], 16)
            pool.wait_ge(S["idl_z"], 16)
            pool.wait_ge(S["route_ok"], 3)
            for c in range(2):
                for i in range(NT):
                    pool.indirect_dma_start(idl_dram, bass.IndirectOffsetOnAxis(rows_u[:, c, i:i + 1], 0), tok[:, i:i + 1], None,
                                            bounds_check=NROW - 1, oob_is_err=True).then_inc(S["idl_st"], 16)
            pool.wait_ge(S["idl_st"], 16 * 2 * NT)
            for s in range(2):
                pool.wait_ge(S[f"x1_st{s}"], 16 * (NT // 2))

            def gather(b):
                pool.dma_start(idxA[:, :], idl_dram[bass.ds(b * TW, P), :]).then_inc(S["idx_in"], 16)
                pool.dma_start(idxB[:, :], idl_dram[bass.ds(b * TW + P, TR), :]).then_inc(S["idx_in"], 16)
                pool.wait_ge(S["idx_in"], 32 * b + 32)
                pool.wait_ge(S["xtr_ps"], NF * b)
                pool.sem_inc(S["pool_go"], 1)
                pool.indirect_dma_start(xgA[:, :], None, x1_dram, bass.IndirectOffsetOnAxis(idxA[:, 0:1], 0)).then_inc(S["xg_in"], 16)
                pool.indirect_dma_start(xgB[:, :], None, x1_dram, bass.IndirectOffsetOnAxis(idxB[:, 0:1], 0)).then_inc(S["xg_in"], 16)
                pool.wait_ge(S["xg_in"], 32 * b + 32)
                pool.sem_inc(S["pool_go"], 1)

            def store(b):
                pool.wait_ge(S["yA0_ev"], b + 1)
                pool.wait_ge(S["yA1_ev"], b + 1)
                pool.dma_start(y_dram[bass.ds(b * TW, P), :], yA[:, :]).then_inc(S["y_out"], 16)
                pool.wait_ge(S["yB0_ev"], b + 1)
                pool.wait_ge(S["yB1_ev"], b + 1)
                pool.dma_start(y_dram[bass.ds(b * TW + P, TR), :], yB[:, :]).then_inc(S["y_out"], 16)

            def pool_pass(j):
                gather(NE * j)
                gather(NE * j + 1)
                with pool.Fori(2, NE) as e:
                    gather(NE * j + e)
                    store(NE * j + e - 2)
                store(NE * j + NE - 2)
                store(NE * j + NE - 1)
            pool_pass(0)
            npass = pool.value_load(npi[0:1, 0:1], min_val=1, max_val=MAXPASS)
            with pool.If(npass > 1):
                pool.memset(zrow[:, :], 0.0).then_inc(S["zrow_ok"], 1)
                pool.wait_ge(S["zrow_ok"], 1)
                with pool.Fori(NE * TW // P, NROW // P) as r:
                    pool.dma_start(y_dram[bass.ds(r * P, P), :], zrow[:, :]).then_inc(S["y_zero"], 16)
                pool.wait_ge(S["y_zero"], 16 * ((NROW - NE * TW) // P))
                with pool.Fori(1, npass) as j:
                    pool_pass(j)

            def token_rows(src):
                for i in range(NT):
                    if i >= 2:
                        pool.wait_ge(S["cres_ok"], i - 1)
                    for c, buf in ((0, cy1), (1, cy2)):
                        pool.indirect_dma_start(buf[:, i % 2, :], None, src, bass.IndirectOffsetOnAxis(rows_u[:, c, i:i + 1], 0))\
                            .then_inc(S[f"cg_in{i % 2}"], 16)
                    if i >= 1:
                        add_bias(pool, i - 1)
                add_bias(pool, NT - 1)
            pool.wait_ge(S["y_out"], npass * (32 * NE))
            pool.sem_inc(S["pool_go"], 1)
            with pool.If(npass < 2):
                token_rows(y_dram[0:NE * TW, :])
            with pool.If(npass > 1):
                token_rows(y_dram)

        def mm3(pe, dst, k_first, k_last, lhs, rhs, ks):
            for k in ks:
                lh, ll = lhs(k)
                rh, rl = rhs(k)
                pe.matmul(dst, lh, rh, start=(k == k_first), stop=False)
                pe.matmul(dst, lh, rl, start=False, stop=False)
                last = pe.matmul(dst, ll, rh, start=False, stop=(k == k_last))
            return last

        def qk_of(p):
            return qk0 if p % 2 == 0 else qk1

        @block.tensor
        def _(pe):
            def wait_bank(f):
                if f >= 2:
                    if GG_FIRST <= f - 2 < GG_LAST:
                        pe.wait_ge(S["gg_ev"], gg_before(f - 1))
                    else:
                        pe.wait_ge(S["proj_ev"], ev_before(f - 1))

            def t_fill(n, f, half, ks):
                s = n % 3
                ns = slice(half * 512, half * 512 + 512)
                if ks[0] == 0:
                    wait_bank(f)
                    if half == 0:
                        pe.wait_ge(S["w_lo_ok"], n + 1)
                last = mm3(pe, pp[f % 2][:, :], 0, NK - 1,
                           lambda k: (w_hi[:, s, k * P:(k + 1) * P], w_lo[:, s, k * P:(k + 1) * P]),
                           lambda k: (xT_hi[:, k, ns], xT_lo[:, k, ns]), ks)
                return last

            def t_piece(n, f0):
                for half in range(2):
                    last = t_fill(n, f0 + half, half, range(NK))
                    last.then_inc(S["proj_ps"], 1)

            def n_tile(m, t):
                f = FILL_N0 + NT * m + t
                wait_bank(f)
                if t == 0:
                    pe.wait_ge(S["w_lo_ok"], CHUNK_N0 + 3 * m + 3)
                ts = slice(t * P, (t + 1) * P)
                mm3(pe, pp[f % 2][:, 0:GLA_W], 0, NK - 1,
                    lambda k: (xT_hi[:, k, ts], xT_lo[:, k, ts]),
                    lambda k: (w_hi[:, :, k * P:(k + 1) * P], w_lo[:, :, k * P:(k + 1) * P]),
                    range(NK)).then_inc(S["proj_ps"], 1)

            pe.wait_ge(S["const_ok"], 11)
            for i in range(NT):
                pe.wait_ge(S[f"x_in{i % 2}"], 16 * (i // 2 + 1))
                for half in range(2):
                    c = 2 * i + half
                    if c >= 4:
                        pe.wait_ge(S["xt_lo"], c - 3)
                    for j in range(4):
                        k = 4 * half + j
                        last = pe.transpose(xt_bank[c % 4][:, j * P:(j + 1) * P], x_row[:, i % 2, k * P:(k + 1) * P], ident[:, :])
                    last.then_inc(S["xt_ps"], 1)
            pe.wait_ge(S["xt_lo"], 2 * NT)
            for n in range(NCHUNK_T):
                t_piece(n, 2 * n)
                if n == 1 or n == 3:
                    hp = n // 2
                    pe.wait_ge(S["const_in"], 16 * (CONV_K + 3 + GLA_H))
                    pe.wait_ge(S["proj_ev"], 2 * 2)
                    for half in range(2):
                        pe.matmul(gate_bank[2 * hp + half], wg2[:, 2 * hp:2 * hp + 2, :], gk[0:64, 0, half * 512:half * 512 + 512],
                                  start=True, stop=True).then_inc(S["gate_ps"], 1)
            for m in range(2):
                for t in range(NT):
                    n_tile(m, t)
            for t in range(NT + 2):
                if t < NT:
                    ts = slice(t * P, (t + 1) * P)
                    if t == 0:
                        pe.wait_ge(S["gmul_ok"], 6)
                    if t >= 1:
                        pe.wait_ge(S["sT_ok"], t)
                    for h in range(GLA_H):
                        r = slice(hs[h % 2], hs[h % 2] + GLA_DK)
                        last = pe.matmul(sc_banks[:, h % 2, h // 2, :], kin[r, h // 2, ts], gq[r, h // 2, ts], start=True, stop=True)
                    last.then_inc(S["sc_ps"], 1)
                    if t >= 1:
                        pe.wait_ge(S["st_ok"], 8 * t)
                    for hp in range(2):
                        last = pe.transpose(kt_bank[:, hp * P:(hp + 1) * P], gk[:, hp, ts], ident[:, :])
                    last.then_inc(S["kt_ps"], 1)
                if 1 <= t <= NT:
                    c = t - 1
                    ts = slice(c * P, (c + 1) * P)
                    pe.wait_ge(S["sT_ok"], c + 1)
                    if c >= 1:
                        pe.wait_ge(S["gs_ok"], c)
                        pe.wait_ge(S["st_ok"], 8 * (c - 1) + 8)
                    pe.matmul(pa_[:, 0:GLA_W], zb[:, 0:P], zb[:, :], start=True, stop=False, skip_group_check=True)
                    for h in range(GLA_H):
                        pe.matmul(pa_[:, h * GLA_DV:(h + 1) * GLA_DV], sT[:, h % 2, h // 2, :], gv[:, c, h * GLA_DV:(h + 1) * GLA_DV],
                                  start=False, stop=False, skip_group_check=True)
                    for cc in range(2):
                        ch = 2 * c + cc
                        if cc == 1:
                            pe.wait_ge(S["st_ok"], 8 * c + 4)
                        for hp in range(2):
                            last = pe.matmul(pa_[64 * cc:64 * cc + 64, hp * 192:hp * 192 + 192],
                                             gq[:, hp, ch * GLA_C:(ch + 1) * GLA_C], S_st[:, hp, ch % 4, :],
                                             start=False, stop=(hp == 1), skip_group_check=True)
                    last.then_inc(S["o_ps"], 1)
                if t >= 2:
                    c = t - 2
                    pe.wait_ge(S["gy_ok"], c + 1)
                    if c >= 1:
                        pe.wait_ge(S["gyT_ev"], c)
                    for j in range(3):
                        last = pe.transpose(po[:, j * P:(j + 1) * P], gy[:, j * P:(j + 1) * P], ident[:, :])
                    last.then_inc(S["gyT_ps"], 1)
                if t < NT:
                    n_tile(2, t)
                    pe.wait_ge(S["kteN_ok"], t + 1)
                    for cc in range(2):
                        for hp in range(2):
                            last = pe.matmul(kv_bank[cc][:, hp * 192:hp * 192 + 192], kteN[64 * cc:64 * cc + 64, hp, :],
                                             gv[64 * cc:64 * cc + 64, t, hp * 192:hp * 192 + 192], start=True, stop=True)
                    last.then_inc(S["kv_ps"], 1)

            def z_of(u):
                p, i, h = UNITS[u]
                q, r = qk_of(p), slice(64 * h, 64 * h + 64)
                if u == 0:
                    pe.wait_ge(S["gyT_ev"], NT)
                    pe.wait_ge(S["st_ok"], 8 * NT - 4)
                    pe.wait_ge(S["gs_ok"], NT)
                    pe.wait_ge(S["proj_ev"], ev_before(FILL_F0))
                if (i, h) == (0, 0) and p >= 1:
                    pe.wait_ge(S["proj_ev"], ev_before(FILL_F0 + 2 * (FILL.index(("sk", p)) + 1)))
                if u >= 2:
                    pe.wait_ge(S["arg_ok"], u - 1)
                W = (i + 1) * P
                for c in range(0, W, 512):
                    e = min(W, c + 512)
                    last = pe.matmul(pz[u % 2][:, c:e], q[r, 0, i * P:(i + 1) * P], q[r, 1, c:e], start=True, stop=True)
                last.then_inc(S["z_ps"], 1)

            def pv_of(u):
                p, i, h = UNITS[u]
                pe.wait_ge(S["aT_ev"], HALVES[u + 1])
                if h == 0 and u >= 2:
                    pe.wait_ge(S["o_ev"], (u // 2))
                for j in range(i + 1):
                    last = pe.matmul(po[64 * h:64 * h + 64, 0:P], sv[:, j, (2 * p + h) * SB_D:(2 * p + h + 1) * SB_D],
                                     aT[:, u % 2, j, :], start=(j == 0), stop=(j == i))
                last.then_inc(S["o_done"], 1)

            def t_of(u, half):
                p, i, h = UNITS[u]
                g = HALVES[u] + half
                if g >= 1:
                    pe.wait_ge(S["aT_ev"], g)
                if half == 0:
                    pe.wait_ge(S["am_ok"], u + 1)
                js = range(4 * half, min(i + 1, 4 * half + 4))
                for j in js:
                    last = pe.transpose(pa_[:, (j % 4) * P:(j % 4 + 1) * P], SP[:, u % 2, j * P:(j + 1) * P], ident[:, :])
                last.then_inc(S["aT_ps"], 1)

            z_of(0)
            z_of(1)
            for u, (p, i, h) in enumerate(UNITS):
                if u + 2 < NU:
                    z_of(u + 2)
                if u >= 1:
                    pv_of(u - 1)
                t_of(u, 0)
                if u in QUARTER:
                    q = QUARTER[u]
                    fi, half, kq = q // 4, (q // 2) % 2, q % 2
                    last = t_fill(CHUNK_F0 + fi, FILL_F0 + 2 * fi + half, half, range(4 * kq, 4 * kq + 4))
                    if kq == 1:
                        last.then_inc(S["proj_ps"], 1)
                if i >= 4:
                    t_of(u, 1)
            pv_of(NU - 1)
            pe.wait_ge(S["aT_ev"], HALVES[NU])
            pe.wait_ge(S["proj_ev"], ev_before(NFILL))
            pe.wait_ge(S["arg_ok"], NU)
            for i in range(NT + 2):
                if i >= 2:
                    c = i - 2
                    pe.wait_ge(S["x1_ok"], 3 * c + 3)
                    if c >= 1:
                        pe.wait_ge(S["x1t_ev"], c)
                    for k in range(NK):
                        last = pe.transpose(pz[1][:, k * P:(k + 1) * P], x1[:, c % 2, k * P:(k + 1) * P], ident[:, :])
                    last.then_inc(S["x1t_ps"], 1)
                if i < NT:
                    pe.wait_ge(S["mixl_ok"], i + 1)
                    for half in range(2):
                        if i >= 2:
                            pe.wait_ge(S["res_ok"], 2 * (i - 2) + half + 1)
                        ns = slice(half * 512, half * 512 + 512)
                        for k in range(NK):
                            if i == 0 and half == 0:
                                pe.wait_ge(S["wo_lo_ok"], k + 1)
                            last = mm3(pe, ob[i % 2][half], 0, NK - 1,
                                       lambda k: (mixh[:, i % 2, k, :], mixl[:, i % 2, k, :]),
                                       lambda k: (wo_hi[:, k, ns], wo_lo[:, k, ns]), [k])
                        last.then_inc(S["ob_ps"], 1)
                if i >= 2:
                    c = i - 2
                    if c == 0:
                        pe.wait_ge(S["lnp_in"], 16 * 4)
                    pe.wait_ge(S["x1t_ev"], c + 1)
                    for k in range(NK):
                        last = pe.matmul(pa_[:, c * NE:(c + 1) * NE], x1T[:, k, :], rw[:, k, :], start=(k == 0), stop=(k == NK - 1))
                    last.then_inc(S["lg_ps"], 1)
            pe.wait_ge(S["tokc_ok"], 8)
            pe.wait_ge(S["mask_ok"], 1)
            rk = po[:, 0:(NT + 1) * NE]
            pe.matmul(rk, zb[:, 0:P], zb[:, 0:(NT + 1) * NE], start=True, stop=False, skip_group_check=True)
            pe.matmul(po[:, 0:NT * NE], trib[:, :], rmb[:, :, :], start=False, stop=False, skip_group_check=True)
            for j in range(NT):
                last = pe.matmul(po[:, (j + 1) * NE:(NT + 1) * NE], oneb[:, :], rmb[:, j:j + 1, :].to_broadcast([P, NT - j, NE]),
                                 start=False, stop=(j == NT - 1), skip_group_check=True)
            last.then_inc(S["pos_ps"], 1)

            def x_transposes(b):
                pe.wait_ge(S["xg_in"], 32 * b + 32)
                for r in range(4):
                    if r >= 2:
                        pe.wait_ge(S["xTl_ok"], 4 * b + r - 1)
                    for dd in range(2):
                        d = 2 * r + dd
                        pe.transpose(xb[r % 2][:, dd * TW:dd * TW + P], xgA[:, d * P:(d + 1) * P], ident[:, :])
                        last = pe.transpose(xb[r % 2][:, dd * TW + P:(dd + 1) * TW], xgB[:, d * P:(d + 1) * P], ident[0:TR, 0:TR])
                    last.then_inc(S["xtr_ps"], 1)

            def down(f, rows, banks):
                for half in range(2):
                    w = slice(half * 512, half * 512 + 512)
                    last = mm3(pe, banks[half], 0, NF - 1, lambda f: (hh[:, f, rows], hl[:, f, rows]),
                               lambda f: (eh[:, 2 * NF + f, w], el[:, 2 * NF + f, w]), [f])
                    yield last

            def pe_block(b, nxt):
                pe.wait_ge(S["xTl_ok"], 4 * b + 4)
                for f in range(NF):
                    if f >= 2 or not first_block(b):
                        pe.wait_ge(S["sum_ok"], 4 * b + f - 1)
                    for w in range(2):
                        p = 2 * f + w
                        bank = pz[f % 2][:, w * 512:w * 512 + 2 * TW]
                        pe.wait_ge(S["el_ok"], NPIECE * b + p + 1)
                        for k in range(NK):
                            ks = slice(k * P, (k + 1) * P)
                            pe.matmul(bank, eh[:, p, ks], xT2[:, k, :, :].rearrange("p a t -> p (a t)"),
                                      start=(k == 0), stop=False, skip_group_check=True)
                            last = pe.matmul(bank[:, 0:TW], el[:, p, ks], xT2[:, k, 0, :], start=False, stop=(k == NK - 1),
                                             skip_group_check=True)
                        last.then_inc(S["piece_done"], 1)
                if not first_block(b):
                    pe.wait_ge(S["yB0_ev"], b)
                    pe.wait_ge(S["yB1_ev"], b)
                if nxt:
                    x_transposes(b + 1)
                if not first_block(b):
                    pe.wait_ge(S["yA0_ev"], b)
                    pe.wait_ge(S["yA1_ev"], b)
                for f in range(NF):
                    pe.wait_ge(S["hl_ok"], 4 * b + f + 1)
                    pe.wait_ge(S["el_ok"], NPIECE * b + 2 * NF + f + 1)
                    for last in down(f, slice(0, P), [pp[0][:, :], pp[1][:, :]]):
                        if f == NF - 1:
                            last.then_inc(S["rowsA_ps"], 1)
                if nxt:
                    pe.wait_ge(S["xTl_ok"], 4 * b + 8)
                for f in range(NF):
                    for last in down(f, slice(P, TW), [pa_[0:TR, :], po[0:TR, :]]):
                        pass
                    last.then_inc(S["piece_done"], 1)

            def pe_pass(j):
                if not isinstance(j, int):
                    pe.wait_ge(S["yB0_ev"], NE * j)
                    pe.wait_ge(S["yB1_ev"], NE * j)
                x_transposes(NE * j)
                experts_of(pe, j, pe_block)
            passes_of(pe, pe_pass)

        def last_fill(n):
            if n < CHUNK_N0:
                return 2 * n + 2
            if n < CHUNK_F0:
                return FILL_N0 + NT * ((n - CHUNK_N0) // 3 + 1)
            return FILL_F0 + 2 * (n - CHUNK_F0) + 2

        def wait_raw(eng, n):
            if n < 4:
                eng.wait_ge(S["wg_in"], 16 * 9)
            else:
                eng.wait_ge(S[f"w_in{n % 2}"], 16 * ((n - 4) // 2 + 1))

        @block.scalar
        def _(act):
            act.preload_act_table_set("natural_log_exp_and_others")
            with nc.allow_non_contiguous_dma(reason="a few hundred parameters"):
                for i in range(CONV_K):
                    act.dma_start(cw[:, i, :], I["conv_w"][0, i, :].rearrange("(c p) -> p c", p=P)).then_inc(S["const_in"], 16)
                act.dma_start(cb[:, :], I["conv_b"][0].rearrange("(c p) -> p c", p=P)).then_inc(S["const_in"], 16)
                act.dma_start(nw[:, :], I["gla_norm_w"][0].partition_broadcast(P))\
                    .then_inc(S["const_in"], 16)
                act.wait_ge(S["const_ok"], 8)
                act.dma_start(wg2[GLA_DK:64, :, 0:GLA_DK], I["gla_w_gate2"][0].rearrange("r (h d) -> r h d", h=GLA_H))\
                    .then_inc(S["const_in"], 16)
                for h in range(GLA_H):
                    act.dma_start(bg[hs[h % 2]:hs[h % 2] + GLA_DK, h // 2:h // 2 + 1],
                                  I["gla_b_gate"][0, h * GLA_DK:(h + 1) * GLA_DK].rearrange("(d o) -> d o", o=1))\
                        .then_inc(S["const_in"], 16)

            def split_hi(n):
                wait_raw(act, n)
                if n >= 3:
                    act.wait_ge(S["proj_ps"], last_fill(n - 3))
                    act.wait_ge(S["w_lo_ok"], n - 2)
                act.activation(w_hi[:, n % 3, :], raw_chunk(n), ACT.Copy).then_inc(S["w_hi_ok"], 1)

            def evac(f, dst, scale=1.0, cols=512):
                act.wait_ge(S["proj_ps"], f + 1)
                act.activation(dst, pp[f % 2][:, 0:cols], ACT.Copy, scale=scale).then_inc(S["proj_ev"], 1)

            for c in range(2 * NT):
                i, half = c // 2, c % 2
                act.wait_ge(S["xt_ps"], c + 1)
                act.activation(xT_hi[:, 4 * half:4 * half + 4, i * P:(i + 1) * P],
                               xt_bank[c % 4].rearrange("p (k t) -> p k t", k=4), ACT.Copy).then_inc(S["xt_hi"], 1)
            split_hi(0)
            split_hi(1)
            for n in range(NCHUNK_T):
                split_hi(n + 2)
                kind, j = T_FIRST[n]
                for half in range(2):
                    hsl = slice(half * 512, half * 512 + 512)
                    dst = {"gq": gq[:, j, hsl], "gk": gk[:, j, hsl], "sq": qk0[:, 0, hsl], "sk": qk0[:, 1, hsl]}[kind]
                    evac(2 * n + half, dst, {"gq": GLA_DK ** -0.5, "sq": SB_D ** -0.5}.get(kind, 1.0))
            split_hi(NCHUNK_T + 2)

            def gate_steps(hp):
                act.wait_ge(S["m_ok"], hp + 1)
                act.activation(tB[:, :], tB[:, :], ACT.Exp).then_inc(S["ge_ok"], 1)
                act.wait_ge(S["ge_ok"], hp + 1)
                act.activation(tB[:, :], tB[:, :], ACT.Ln, bias=1.0).then_inc(S["gl_ok"], 1)
                yield
                act.wait_ge(S["cs_ok"], 17 * hp + 16)
                act.activation(tB[:, :], tA[:, :], ACT.Exp, scale=-1.0 / GATE_NORM).then_inc(S["gexp_ok"], 1)
                act.activation(tC[:, :], tA[:, :], ACT.Exp, scale=1.0 / GATE_NORM).then_inc(S["gexp_ok"], 1)
                yield
                act.wait_ge(S["cs_ok"], 17 * hp + 17)
                act.activation(tB[:, :], tB[:, :], ACT.Exp, scale=1.0 / GATE_NORM).then_inc(S["gexp_ok"], 1)
                act.activation(dec[:, hp, :], tA[:, :].rearrange("p (c t) -> p c t", t=GLA_C)[:, :, GLA_C - 1],
                               ACT.Exp, scale=-1.0 / GATE_NORM).then_inc(S["dec_ok"], 1)
                yield

            steps = [s for hp in range(2) for s in [gate_steps(hp)] * 3]
            for t in range(NT):
                evac(FILL_N0 + t, gv[:, t, :], cols=GLA_W)
                if t < 6:
                    next(steps[t])
            for n in range(CHUNK_N0 + 3, CHUNK_N0 + 6):
                split_hi(n)
            for t in range(NT):
                f = FILL_N0 + NT + t
                act.wait_ge(S["proj_ps"], f + 1)
                act.activation(gg[:, t, :], pp[f % 2][:, 0:GLA_W], ACT.Exp, scale=-1.0).then_inc(S["gge_ok"], 1)
            for n in range(CHUNK_N0 + 6, CHUNK_N0 + 9):
                split_hi(n)
            for t in range(NT + 2):
                if t < NT:
                    act.wait_ge(S["kt_ps"], t + 1)
                    if t >= 1:
                        act.wait_ge(S["kv_ps"], t)
                    act.activation(kteN[:, :, :], kt_bank.rearrange("p (h c) -> p h c", h=2), ACT.Copy).then_inc(S["kteN_ok"], 1)
                if 1 <= t <= NT:
                    act.wait_ge(S["o_ps"], t)
                    if t >= 2:
                        act.wait_ge(S["gms_ok"], 2 * (t - 1))
                    act.activation(gsq[:, :], pa_[:, 0:GLA_W], ACT.Square).then_inc(S["gsq_ok"], 1)
                if t >= 2:
                    act.wait_ge(S["gyT_ps"], t - 1)
                    act.activation(mix[:, 5:8, (t - 2) * P:(t - 1) * P], po[:, 0:3 * P].rearrange("p (j t) -> p j t", j=3),
                                   ACT.Copy).then_inc(S["gyT_ev"], 1)
                if 1 <= t <= NT:
                    act.wait_ge(S["gms_ok"], 2 * t)
                    act.activation(gms[:, 0:4], gms[:, 0:4], ACT.Ln).then_inc(S["rstd_ok"], 1)
                    act.wait_ge(S["rstd_ok"], 2 * t - 1)
                    act.activation(gms[:, 4:8], gms[:, 0:4], ACT.Exp, scale=-0.5).then_inc(S["rstd_ok"], 1)
                if t < NT:
                    evac(FILL_N0 + 2 * NT + t, sv[:, t, :], cols=SB_W)
            split_hi(CHUNK_F0)

            def softplus_of(u):
                W = (UNITS[u][1] + 1) * P
                act.wait_ge(S["zc_ok"], u + 1)
                act.activation(E[:, u % 2, 0:W], E[:, u % 2, 0:W], ACT.Exp).then_inc(S["e_ok"], 1)
                act.wait_ge(S["e_ok"], u + 1)
                act.activation(E[:, u % 2, 0:W], E[:, u % 2, 0:W], ACT.Ln, bias=1.0).then_inc(S["ln_ok"], 1)

            def weights_of(u):
                W = (UNITS[u][1] + 1) * P
                act.wait_ge(S["arg_ok"], u + 1)
                act.activation(SP[:, u % 2, 0:W], SP[:, u % 2, 0:W], ACT.Exp).then_inc(S["a_ok"], 1)

            def evac_fill(f):
                kind, j = FILL[f // 2]
                hsl = slice((f % 2) * 512, (f % 2) * 512 + 512)
                if kind in ("sq", "sk"):
                    dst = qk_of(j)[:, 0 if kind == "sq" else 1, hsl]
                    if j == 2:
                        act.wait_ge(S["z_ps"], 2 * NT)
                else:
                    dst = conv_in[:, {"cc": 0, "ch": 1, "cb": 2}[kind], hsl]
                    if j == 1:
                        act.wait_ge(S["conv_ok"], 5 if kind == "cb" else 4)
                evac(FILL_F0 + f, dst, SB_D ** -0.5 if kind == "sq" else 1.0)

            def split_wo_hi(k):
                if k == 0:
                    act.wait_ge(S["proj_ps"], NFILL)
                act.wait_ge(S[f"wo_in{k % 2}"], 16 * (k // 2 + 1))
                act.activation(wo_hi[:, k, :], wo_raw[:, k % 2, :], ACT.Copy).then_inc(S["wo_hi_ok"], 1)

            softplus_of(0)
            softplus_of(1)
            weights_of(0)
            for u, (p, i, h) in enumerate(UNITS):
                if u + 2 < NU:
                    softplus_of(u + 2)
                q = QUARTER.get(u)
                if q is not None and q % 4 == 0 and q // 4 + 1 < len(FILL):
                    split_hi(CHUNK_F0 + q // 4 + 1)
                if u >= 1 and QUARTER.get(u - 1, 0) % 2 == 1:
                    evac_fill(QUARTER[u - 1] // 2)
                if u >= NU - 2:
                    for k in range(4 * (u - NU + 2), 4 * (u - NU + 3)):
                        split_wo_hi(k)
                if h == 0 and u >= 2:
                    pp_, ii = UNITS[u - 1][0], UNITS[u - 1][1]
                    act.wait_ge(S["o_done"], u)
                    act.activation(mix[:, 2 + pp_, ii * P:(ii + 1) * P], po[:, 0:P], ACT.Copy).then_inc(S["o_ev"], 1)
                for half in range(1 if i < 4 else 2):
                    lo, hi = 4 * half, min(i + 1, 4 * half + 4)
                    act.wait_ge(S["aT_ps"], HALVES[u] + half + 1)
                    if half == 0 and u >= 2:
                        act.wait_ge(S["o_done"], u - 1)
                    act.activation(aT[:, u % 2, lo:hi, :], pa_[:, 0:(hi - lo) * P].rearrange("p (j t) -> p j t", t=P),
                                   ACT.Copy).then_inc(S["aT_ev"], 1)
                    if half == 0 and u + 1 < NU:
                        weights_of(u + 1)
            act.wait_ge(S["o_done"], NU)
            act.activation(mix[:, 2 + NPAIR - 1, (NT - 1) * P:NT * P], po[:, 0:P], ACT.Copy).then_inc(S["o_ev"], 1)

            act.wait_ge(S["am_ok"], NU)
            act.dma_start(lnp[:, 0, :], I["ln1_g"][0].partition_broadcast(P)).then_inc(S["lnp_in"], 16)
            act.dma_start(lnp[:, 1, :], I["ln1_b"][0].partition_broadcast(P)).then_inc(S["lnp_in"], 16)
            act.dma_start(rw[:, :, :], I["router_w"].rearrange("(k p) e -> p k e", p=P)).then_inc(S["lnp_in"], 16)
            act.dma_start(rb[:, :], I["router_bias"].partition_broadcast(P)).then_inc(S["lnp_in"], 16)

            def mix_hi(i):
                if i == 0:
                    act.wait_ge(S["conv_ok"], 10)
                    act.wait_ge(S["o_ev"], NPAIR * NT)
                    act.wait_ge(S["gyT_ev"], NT)
                if i >= 2:
                    act.wait_ge(S["ob_ps"], 2 * (i - 1))
                act.activation(mixh[:, i % 2, :, :], mix[:, :, i * P:(i + 1) * P], ACT.Copy).then_inc(S["mixh_ok"], 1)
            mix_hi(0)
            for i in range(NT + 2):
                if i + 1 < NT:
                    mix_hi(i + 1)
                if i >= 2:
                    act.wait_ge(S["x1t_ps"], i - 1)
                    if i >= 3:
                        act.wait_ge(S["lg_ps"], i - 2)
                    act.activation(x1T[:, :, :], pz[1][:, :].rearrange("p (k t) -> p k t", k=NK), ACT.Copy).then_inc(S["x1t_ev"], 1)
                if i < NT:
                    act.wait_ge(S["bn_ok"], 4 * i + 4)
                    act.activation(rst[:, 0:1], rst[:, 0:1], ACT.Ln).then_inc(S["lrs_ok"], 1)
                    act.wait_ge(S["lrs_ok"], 2 * i + 1)
                    act.activation(rst[:, 1:2], rst[:, 0:1], ACT.Exp, scale=-0.5).then_inc(S["lrs_ok"], 1)
            act.wait_ge(S["lg_ps"], NT)
            act.activation(rs[:, :, :], pa_[:, 0:NT * NE].rearrange("p (i e) -> p i e", e=NE), ACT.Exp, scale=-1.0).then_inc(S["rexp_ok"], 1)

            def piece_hi(b, p):
                act.wait_ge(S[f"e_in{p}"], 16 * b + 16)
                if not (isinstance(b, int) and b == 0):
                    act.wait_ge(S["piece_done"], NPIECE * b - NPIECE + p + 1)
                act.activation(eh[:, p, :], er[:, p, :], ACT.Copy).then_inc(S["eh_ok"], 1)

            def x_hi(b):
                for r in range(4):
                    act.wait_ge(S["xtr_ps"], 4 * b + r + 1)
                    act.activation(xT2[:, 2 * r:2 * r + 2, 0, :], xb[r % 2].rearrange("p (d t) -> p d t", d=2), ACT.Copy).then_inc(S["xTh_ok"], 1)

            def act_block(b, nxt):
                for f in range(NF):
                    act.wait_ge(S["piece_done"], NPIECE * b + 2 * f + 2)
                    act.activation(cross[:, f % 2, :, :], pz[f % 2][:, :].rearrange("p (w c) -> p w c", w=2)[:, :, TW:2 * TW],
                                   ACT.Copy).then_inc(S["cross_ok"], 1)
                    if nxt:
                        piece_hi(b + 1, 2 * f)
                    act.wait_ge(S["sum_ok"], 4 * b + f + 1)
                    act.activation(sil[:, f % 2, :], gu[:, f % 2, 0, :], ACT.Silu).then_inc(S["sil_ok"], 1)
                    if nxt:
                        piece_hi(b + 1, 2 * f + 1)
                    act.wait_ge(S["h_ok"], 4 * b + f + 1)
                    act.activation(hh[:, f, :], hf[:, f, :], ACT.Copy).then_inc(S["hh_ok"], 1)
                if nxt:
                    x_hi(b + 1)
                act.wait_ge(S["rowsA_ps"], 2 * b + 2)
                if not first_block(b):
                    act.wait_ge(S["y_out"], 32 * b)
                act.activation(yA[:, 512:], pp[1][:, :], ACT.Copy).then_inc(S["yA1_ev"], 1)
                if nxt:
                    for p in range(2 * NF, NPIECE - 1):
                        piece_hi(b + 1, p)
                act.wait_ge(S["piece_done"], NPIECE * b + NPIECE)
                act.activation(yB[:, 512:], po[0:TR, :], ACT.Copy).then_inc(S["yB1_ev"], 1)
                if nxt:
                    piece_hi(b + 1, NPIECE - 1)

            def act_pass(j):
                b0 = NE * j
                if isinstance(j, int):
                    act.wait_ge(S["ob_ps"], 2 * NT)
                    act.wait_ge(S["res_ok"], 2 * NT)
                for p in range(NPIECE):
                    piece_hi(b0, p)
                    if p == 5:
                        x_hi(b0)
                experts_of(act, j, act_block)
            passes_of(act, act_pass)

            for i in range(NT):
                act.wait_ge(S[f"cg_in{i % 2}"], 32 * (i // 2 + 1))
                act.activation(cy1[:, i % 2, :], cy1[:, i % 2, :], ACT.Copy, scale=g12[:, 0, i:i + 1]).then_inc(S["c1_ok"], 1)
                act.wait_ge(S["cbn_ok"], 4 * i + 4)
                act.activation(rst[:, 0:1], rst[:, 0:1], ACT.Ln).then_inc(S["clr_ok"], 1)
                act.wait_ge(S["clr_ok"], 2 * i + 1)
                act.activation(rst[:, 1:2], rst[:, 0:1], ACT.Exp, scale=-0.5).then_inc(S["clr_ok"], 1)

        @block.vector
        def _(dve):
            def split_lo(n):
                dve.wait_ge(S["w_hi_ok"], n + 1)
                dve.tensor_tensor(w_lo[:, n % 3, :], raw_chunk(n), w_hi[:, n % 3, :].bitcast(F32), ALU.subtract)\
                    .then_inc(S["w_lo_ok"], 1)

            for c in range(2 * NT):
                i, half = c // 2, c % 2
                dve.wait_ge(S["xt_hi"], c + 1)
                ts = slice(i * P, (i + 1) * P)
                dve.tensor_tensor(xT_lo[:, 4 * half:4 * half + 4, ts], xt_bank[c % 4].rearrange("p (k t) -> p k t", k=4),
                                  xT_hi[:, 4 * half:4 * half + 4, ts].bitcast(F32), ALU.subtract).then_inc(S["xt_lo"], 1)
            for n in range(CHUNK_N0 + 3):
                split_lo(n)

            dve.wait_ge(S["const_in"], 16 * (CONV_K + 3 + GLA_H))
            for hp in range(2):
                if hp == 1:
                    dve.wait_ge(S["dec_ok"], 1)
                for half in range(2):
                    dve.wait_ge(S["gate_ps"], 2 * hp + half + 1)
                    dve.tensor_scalar(tA[:, half * 512:half * 512 + 512], gate_bank[2 * hp + half], bg[:, hp:hp + 1], -1.0,
                                      ALU.add, ALU.mult).then_inc(S["n_ok"], 1)
                dve.wait_ge(S["n_ok"], 2 * hp + 2)
                dve.tensor_scalar(tB[:, :], tA[:, :], CLAMP, None, ALU.min).then_inc(S["m_ok"], 1)
                dve.wait_ge(S["gl_ok"], hp + 1)
                dve.tensor_tensor(tB[:, :], tB[:, :], tA[:, :], ALU.max).then_inc(S["gsp_ok"], 1)
                dve.wait_ge(S["gsp_ok"], hp + 1)
                for c in range(T // GLA_C):
                    cs = slice(c * GLA_C, (c + 1) * GLA_C)
                    dve.tensor_tensor_scan(tA[:, cs], tB[:, cs], zeros[:, :], 0.0, ALU.add, ALU.add).then_inc(S["cs_ok"], 1)
                dve.wait_ge(S["gate_ps"], 4)
                dve.wait_ge(S["gexp_ok"], 3 * hp + 1)
                dve.tensor_tensor(gq[:, hp, :], gq[:, hp, :], tB[:, :], ALU.mult).then_inc(S["gmul_ok"], 1)
                dve.wait_ge(S["gexp_ok"], 3 * hp + 2)
                dve.tensor_tensor(kin[:, hp, :], gk[:, hp, :], tC[:, :], ALU.mult).then_inc(S["gmul_ok"], 1)
                csv = tA[:, :].rearrange("p (c t) -> p c t", t=GLA_C)
                dve.wait_ge(S["gmul_ok"], 3 * hp + 1)
                dve.tensor_tensor(tB[:, :].rearrange("p (c t) -> p c t", t=GLA_C), csv,
                                  csv[:, :, GLA_C - 1:GLA_C].to_broadcast([P, T // GLA_C, GLA_C]), ALU.subtract)\
                    .then_inc(S["cs_ok"], 1)
                dve.wait_ge(S["gexp_ok"], 3 * hp + 3)
                dve.tensor_tensor(gk[:, hp, :], gk[:, hp, :], tB[:, :], ALU.mult).then_inc(S["gmul_ok"], 1)

            for n in range(CHUNK_N0 + 3, CHUNK_N0 + 6):
                split_lo(n)
            for t in range(NT):
                f = FILL_N0 + NT + t
                dve.wait_ge(S["gge_ok"], t + 1)
                dve.tensor_scalar(gg[:, t, :], gg[:, t, :], 1.0, None, ALU.add).then_inc(S["ggs_ok"], 1)
                dve.wait_ge(S["ggs_ok"], 3 * t + 1)
                dve.reciprocal(gg[:, t, :], gg[:, t, :]).then_inc(S["ggs_ok"], 1)
                dve.wait_ge(S["ggs_ok"], 3 * t + 2)
                dve.tensor_tensor(gg[:, t, :], pp[f % 2][:, 0:GLA_W], gg[:, t, :], ALU.mult).then_inc(S["gg_ev"], 1)
                dve.wait_ge(S["gg_ev"], t + 1)
                dve.tensor_tensor(gg[:, t, :].rearrange("p (h d) -> p h d", h=GLA_H), gg[:, t, :].rearrange("p (h d) -> p h d", h=GLA_H),
                                  nw[:, :].unsqueeze(1).to_broadcast([P, GLA_H, GLA_DV]), ALU.mult).then_inc(S["ggs_ok"], 1)
            for n in range(CHUNK_N0 + 6, CHUNK_N0 + 9):
                split_lo(n)

            for t in range(NT + 1):
                if t < NT:
                    dve.wait_ge(S["sc_ps"], t + 1)
                    if t >= 1:
                        dve.wait_ge(S["o_ps"], t)
                    dve.tensor_tensor(sT[:, :, :, :], sc_banks,
                                      trimask[:, :].unsqueeze(1).unsqueeze(1).to_broadcast([P, 2, 2, P]), ALU.mult).then_inc(S["sT_ok"], 1)
                if t >= 1:
                    c = t - 1
                    dve.wait_ge(S["gsq_ok"], c + 1)
                    dve.tensor_reduce(gms[:, 0:4], gsq[:, :].rearrange("p (h d) -> p h d", h=GLA_H), AX.X, ALU.add)\
                        .then_inc(S["gms_ok"], 1)
                    dve.wait_ge(S["gms_ok"], 2 * c + 1)
                    dve.tensor_scalar(gms[:, 0:4], gms[:, 0:4], 1.0 / GLA_DV, RMS_EPS, ALU.mult, ALU.add).then_inc(S["gms_ok"], 1)
                    dve.wait_ge(S["rstd_ok"], 2 * c + 2)
                    if c >= 1:
                        dve.wait_ge(S["gyT_ps"], c)
                    dve.tensor_tensor(gy[:, :].rearrange("p (h d) -> p h d", h=GLA_H), pa_[:, 0:GLA_W].rearrange("p (h d) -> p h d", h=GLA_H),
                                      gms[:, 4:8].unsqueeze(2).to_broadcast([P, GLA_H, GLA_DV]), ALU.mult).then_inc(S["gs_ok"], 1)
                    dve.wait_ge(S["gs_ok"], c + 1)
                    dve.tensor_tensor(gy[:, :], gy[:, :], gg[:, c, :], ALU.mult).then_inc(S["gy_ok"], 1)
                if t < NT:
                    dve.wait_ge(S["kv_ps"], t + 1)
                    for cc in range(2):
                        ch = 2 * t + cc
                        if ch == T // GLA_C - 1:
                            continue
                        if ch >= 3:
                            dve.wait_ge(S["o_ps"], (ch - 3) // 2 + 1)
                        if ch >= 1:
                            dve.wait_ge(S["st_ok"], 4 * ch)
                        for hp in range(2):
                            for h in range(2):
                                r = slice(hs[h], hs[h] + 64)
                                c_ = slice(h * GLA_DV, (h + 1) * GLA_DV)
                                dve.scalar_tensor_tensor(S_st[r, hp, (ch + 1) % 4, c_], S_st[r, hp, ch % 4, c_],
                                                         dec[r, hp, ch:ch + 1],
                                                         kv_bank[cc][r, hp * 192 + h * GLA_DV:hp * 192 + (h + 1) * GLA_DV],
                                                         ALU.mult, ALU.add).then_inc(S["st_ok"], 1)
            split_lo(CHUNK_F0)

            def clamp_of(u):
                W = (UNITS[u][1] + 1) * P
                dve.wait_ge(S["z_ps"], u + 1)
                dve.tensor_scalar(E[:, u % 2, 0:W], pz[u % 2][:, 0:W], CLAMP, None, ALU.min).then_inc(S["zc_ok"], 1)

            def conv_steps(ct, first):
                y = mix[:, ct, :]
                u_ = conv_in[:, 0, :]
                k = 5 * ct
                if first:
                    dve.tensor_tensor(u_, u_, conv_in[:, 1, :], ALU.mult).then_inc(S["conv_ok"], 1)
                    dve.wait_ge(S["conv_ok"], k + 1)
                    dve.tensor_scalar(y, u_, cw[:, 0, ct:ct + 1], cb[:, ct:ct + 1], ALU.mult, ALU.add).then_inc(S["conv_ok"], 1)
                    for i in range(1, CONV_K):
                        dve.wait_ge(S["conv_ok"], k + 1 + i)
                        dve.scalar_tensor_tensor(y[:, i:], u_[:, :T - i], cw[:, i, ct:ct + 1], y[:, i:], ALU.mult, ALU.add)\
                            .then_inc(S["conv_ok"], 1)
                else:
                    dve.wait_ge(S["conv_ok"], k + 4)
                    dve.tensor_tensor(y, y, conv_in[:, 2, :], ALU.mult).then_inc(S["conv_ok"], 1)

            def arg_of(u):
                W = (UNITS[u][1] + 1) * P
                dve.wait_ge(S["ln_ok"], u + 1)
                if u >= 2:
                    dve.wait_ge(S["aT_ps"], HALVES[u - 1])
                dve.tensor_tensor(SP[:, u % 2, 0:W], pz[u % 2][:, 0:W], E[:, u % 2, 0:W], ALU.max).then_inc(S["sp_ok"], 1)
                dve.wait_ge(S["spm_ok"], u + 1)
                dve.tensor_tensor_scan(E[:, u % 2, 0:W][:, ::-1], SP[:, u % 2, 0:W][:, ::-1], SP[:, u % 2, 0:W][:, ::-1], 0.0,
                                       ALU.add, ALU.max).then_inc(S["sfx_ok"], 1)
                dve.wait_ge(S["sfx_ok"], u + 1)
                dve.tensor_tensor(SP[:, u % 2, 0:W], pz[u % 2][:, 0:W], E[:, u % 2, 0:W], ALU.subtract).then_inc(S["arg_ok"], 1)

            def split_wo_lo(k):
                dve.wait_ge(S["wo_hi_ok"], k + 1)
                dve.tensor_tensor(wo_lo[:, k, :], wo_raw[:, k % 2, :], wo_hi[:, k, :].bitcast(F32), ALU.subtract).then_inc(S["wo_lo_ok"], 1)

            clamp_of(0)
            clamp_of(1)
            arg_of(0)
            ready = []
            for u, (p, i, h) in enumerate(UNITS):
                if u + 2 < NU:
                    clamp_of(u + 2)
                q = QUARTER.get(u)
                if q is not None and q % 4 == 0 and q // 4 + 1 < len(FILL):
                    split_lo(CHUNK_F0 + q // 4 + 1)
                if u >= NU - 2:
                    for k in range(4 * (u - NU + 2), 4 * (u - NU + 3)):
                        split_wo_lo(k)
                if u + 1 < NU:
                    arg_of(u + 1)
                for what, at_u in list(ready):
                    if at_u < u:
                        kind, j = what
                        dve.wait_ge(S["proj_ev"], ev_before(FILL_F0 + 2 * (FILL.index(what) + 1)))
                        conv_steps(j, kind == "ch")
                        ready.remove((what, at_u))
                if q is not None and q % 4 == 3 and FILL[q // 4][0] in ("ch", "cb"):
                    ready.append((FILL[q // 4], u))
            for kind, j in [w for w, _ in ready]:
                dve.wait_ge(S["proj_ev"], ev_before(FILL_F0 + 2 * (FILL.index((kind, j)) + 1)))
                conv_steps(j, kind == "ch")
            def mix_lo(i):
                dve.wait_ge(S["mixh_ok"], i + 1)
                dve.tensor_tensor(mixl[:, i % 2, :, :], mix[:, :, i * P:(i + 1) * P], mixh[:, i % 2, :, :].bitcast(F32), ALU.subtract)\
                    .then_inc(S["mixl_ok"], 1)
            mix_lo(0)
            for i in range(NT):
                if i + 1 < NT:
                    mix_lo(i + 1)
                s = i % 2
                dve.wait_ge(S[f"xr_in{s}"], 16 * (i // 2 + 1))
                if i >= 2:
                    dve.wait_ge(S[f"x1_st{s}"], 16 * (i // 2))
                    dve.wait_ge(S["x1t_ps"], i - 1)
                for half in range(2):
                    hsl = slice(half * 512, half * 512 + 512)
                    dve.wait_ge(S["ob_ps"], 2 * i + half + 1)
                    dve.scalar_tensor_tensor(x1[:, s, hsl], xres[:, s, hsl], ALPHA, ob[s][half], ALU.mult, ALU.add).then_inc(S["res_ok"], 1)
                norm_stats(dve, x1, s, "res_ok", 2 * i + 2, "bn_ok", i, "lrs_ok")
                dve.wait_ge(S["lrs_ok"], 2 * i + 2)
                dve.tensor_scalar(x1[:, s, :], x1[:, s, :], bna[:, 0:1], rst[:, 1:2], ALU.subtract, ALU.mult).then_inc(S["x1_ok"], 1)
                if i == 0:
                    dve.wait_ge(S["lnp_in"], 16 * 4)
                for a, op in ((0, ALU.mult), (1, ALU.add)):
                    dve.wait_ge(S["x1_ok"], 3 * i + a + 1)
                    dve.tensor_tensor(x1[:, s, :], x1[:, s, :], lnp[:, a, :], op).then_inc(S["x1_ok"], 1)

            step = [0]

            def link(ins):
                step[0] += 1
                ins.then_inc(S["route_step"], 1)
                dve.wait_ge(S["route_step"], step[0])

            def grp(t_):
                return t_[:, :, :].rearrange("p i (g j) -> p (i g) j", j=EPG)

            bc = lambda t_, n: t_.unsqueeze(1).to_broadcast([P, n, t_.shape[-1]])
            dve.wait_ge(S["rexp_ok"], 1)
            dve.wait_ge(S["tokc_ok"], 8)
            dve.wait_ge(S["mixl_ok"], NT)
            link(dve.tensor_scalar(rs[:, :, :], rs[:, :, :], 1.0, None, ALU.add))
            link(dve.reciprocal(rs[:, :, :], rs[:, :, :]))
            link(dve.tensor_tensor(rsel[:, :, :].rearrange("p (i g) j -> p i (g j)", g=NGRP), rs[:, :, :], bc(rb[:, :], NT), ALU.add))
            dve.tensor_tensor(rpair[:, :, 0:3], rsel[:, :, 0:3], rsel[:, :, 1:4], ALU.add).then_inc(S["route_step"], 1)
            dve.tensor_tensor(rpair[:, :, 3:5], rsel[:, :, 0:2], rsel[:, :, 2:4], ALU.add).then_inc(S["route_step"], 1)
            step[0] += 2
            link(dve.tensor_tensor(rpair[:, :, 5:6], rsel[:, :, 0:1], rsel[:, :, 3:4], ALU.add))
            link(dve.tensor_reduce(rgs[:, :, :].rearrange("p i g -> p (i g)"), rpair[:, :, :], AX.X, ALU.max))

            def ranks(v, r, n):
                link(dve.tensor_copy(r, bc(rank0[:, :], n)))
                for d in range(1, EPG):
                    m = EPG - d
                    ge = rge[:, 0:n, 0:m]
                    link(dve.tensor_tensor(ge, v[:, :, 0:m], v[:, :, d:EPG], ALU.is_ge))
                    link(dve.tensor_tensor(r[:, :, d:EPG], r[:, :, d:EPG], ge, ALU.add))
                    link(dve.tensor_tensor(r[:, :, 0:m], r[:, :, 0:m], ge, ALU.subtract))
            ranks(rgs[:, :, :], rgk[:, :, :], NT)
            ranks(rsel[:, :, :], rek[:, :, :], NT * NGRP)
            link(dve.tensor_scalar(rgk[:, :, :], rgk[:, :, :], 0.0, None, ALU.is_equal))
            link(dve.scalar_tensor_tensor(grp(rmask), rek[:, :, :], 2.0,
                                          rgk[:, :, :].rearrange("p i g -> p (i g)").unsqueeze(2).to_broadcast([P, NT * NGRP, EPG]),
                                          ALU.is_lt, ALU.mult))
            dve.tensor_copy(rmb[:, :, :], rmask[:, :, :]).then_inc(S["mask_ok"], 1)
            link(dve.tensor_tensor(rgate[:, :, :], rs[:, :, :], rmask[:, :, :], ALU.mult))
            link(dve.tensor_reduce(rden[:, :], rgate[:, :, :], AX.X, ALU.add))
            link(dve.reciprocal(rden[:, :], rden[:, :]))
            link(dve.tensor_tensor(rgate[:, :, :], rgate[:, :, :], rden[:, :].unsqueeze(2).to_broadcast([P, NT, NE]), ALU.mult))
            dve.wait_ge(S["pos_ps"], 1)
            link(dve.tensor_copy(rpos[:, :, :], po[:, 0:(NT + 1) * NE].rearrange("p (i e) -> p i e", e=NE)))
            link(dve.tensor_reduce(rmax[:, :], rpos[:, NT, :], AX.X, ALU.max))
            link(dve.tensor_scalar(pcmp[:, :], passes[:, :], rmax[:, 0:1], None, ALU.is_lt))
            link(dve.tensor_reduce(rnp[:, :], pcmp[:, :], AX.X, ALU.add))
            dve.tensor_scalar(npi[:, :], rnp[:, :], 1.0, None, ALU.add).then_inc(S["route_ok"], 1)
            link(dve.tensor_tensor(rrow[:, :, :], rpos[:, 0:NT, :], bc(ecol[:, :], NT), ALU.add))
            for j in range(1, MAXPASS):
                link(dve.tensor_scalar(rtmp[:, :, :], rpos[:, 0:NT, :], float(j * TW), float((NE - 1) * TW), ALU.is_ge, ALU.mult))
                link(dve.tensor_tensor(rrow[:, :, :], rrow[:, :, :], rtmp[:, :, :], ALU.add))
            link(dve.scalar_tensor_tensor(rtmp[:, :, :], rrow[:, :, :], -BIG, rmask[:, :, :], ALU.add, ALU.mult))
            link(dve.tensor_reduce(rr12[:, 0, :], rtmp[:, :, :], AX.X, ALU.min))
            link(dve.scalar_tensor_tensor(rtmp[:, :, :], rrow[:, :, :], 1.0, rmask[:, :, :], ALU.add, ALU.mult))
            link(dve.tensor_reduce(rr12[:, 1, :], rtmp[:, :, :], AX.X, ALU.max))
            link(dve.tensor_scalar(rr12[:, 0, :], rr12[:, 0, :], BIG, None, ALU.add))
            link(dve.tensor_scalar(rr12[:, 1, :], rr12[:, 1, :], -1.0, None, ALU.add))
            dve.tensor_copy(rows_u[:, 0, :], rr12[:, 0, :]).then_inc(S["route_ok"], 1)
            dve.tensor_copy(rows_u[:, 1, :], rr12[:, 1, :]).then_inc(S["route_ok"], 1)
            for c in range(2):
                link(dve.tensor_tensor(rtmp[:, :, :], rrow[:, :, :], rr12[:, c, :].unsqueeze(2).to_broadcast([P, NT, NE]), ALU.is_equal))
                link(dve.tensor_tensor(rtmp[:, :, :], rtmp[:, :, :], rgate[:, :, :], ALU.mult))
                link(dve.tensor_reduce(g12[:, c, :], rtmp[:, :, :], AX.X, ALU.add))

            def piece_lo(b, p):
                dve.wait_ge(S["eh_ok"], NPIECE * b + p + 1)
                dve.tensor_tensor(el[:, p, :], er[:, p, :], eh[:, p, :].bitcast(F32), ALU.subtract).then_inc(S["el_ok"], 1)

            def x_lo(b):
                for r in range(4):
                    dve.wait_ge(S["xTh_ok"], 4 * b + r + 1)
                    dve.tensor_tensor(xT2[:, 2 * r:2 * r + 2, 1, :], xb[r % 2].rearrange("p (d t) -> p d t", d=2),
                                      xT2[:, 2 * r:2 * r + 2, 0, :].bitcast(F32), ALU.subtract).then_inc(S["xTl_ok"], 1)

            def dve_block(b, nxt):
                for f in range(NF):
                    dve.wait_ge(S["cross_ok"], 4 * b + f + 1)
                    if f >= 2 or not first_block(b):
                        dve.wait_ge(S["h_ok"], 4 * b + f - 1)
                    dve.tensor_tensor(gu[:, f % 2, :, :], pz[f % 2][:, :].rearrange("p (w c) -> p w c", w=2)[:, :, 0:TW],
                                      cross[:, f % 2, :, :], ALU.add).then_inc(S["sum_ok"], 1)
                    if nxt:
                        piece_lo(b + 1, 2 * f)
                    dve.wait_ge(S["sil_ok"], 4 * b + f + 1)
                    dve.tensor_tensor(hf[:, f, :], sil[:, f % 2, :], gu[:, f % 2, 1, :], ALU.mult).then_inc(S["h_ok"], 1)
                    if nxt:
                        piece_lo(b + 1, 2 * f + 1)
                    dve.wait_ge(S["hh_ok"], 4 * b + f + 1)
                    dve.tensor_tensor(hl[:, f, :], hf[:, f, :], hh[:, f, :].bitcast(F32), ALU.subtract).then_inc(S["hl_ok"], 1)
                if nxt:
                    x_lo(b + 1)
                dve.wait_ge(S["rowsA_ps"], 2 * b + 1)
                if not first_block(b):
                    dve.wait_ge(S["y_out"], 32 * b)
                dve.tensor_copy(yA[:, 0:512], pp[0][:, :]).then_inc(S["yA0_ev"], 1)
                if nxt:
                    for p in range(2 * NF, NPIECE - 1):
                        piece_lo(b + 1, p)
                dve.wait_ge(S["piece_done"], NPIECE * b + NPIECE)
                dve.tensor_copy(yB[:, 0:512], pa_[0:TR, :]).then_inc(S["yB0_ev"], 1)
                if nxt:
                    piece_lo(b + 1, NPIECE - 1)

            def dve_pass(j):
                b0 = NE * j
                for p in range(NPIECE):
                    piece_lo(b0, p)
                    if p == 5:
                        x_lo(b0)
                experts_of(dve, j, dve_block)
            npass = passes_of(dve, dve_pass)

            for i in range(NT):
                s = i % 2
                if i == 0:
                    dve.wait_ge(S["y_out"], npass * (32 * NE))
                dve.wait_ge(S["c1_ok"], i + 1)
                dve.scalar_tensor_tensor(cy1[:, s, :], cy2[:, s, :], g12[:, 1, i:i + 1], cy1[:, s, :], ALU.mult, ALU.add).then_inc(S["c2_ok"], 1)
                dve.wait_ge(S["c2_ok"], i + 1)
                dve.wait_ge(S[f"cx_in{s}"], 16 * (i // 2 + 1))
                if i >= 2:
                    dve.wait_ge(S[f"out_st{s}"], 16 * (i // 2))
                dve.scalar_tensor_tensor(cr[:, s, :], cx[:, s, :], ALPHA, cy1[:, s, :], ALU.mult, ALU.add).then_inc(S["cres_ok"], 1)
                norm_stats(dve, cr, s, "cres_ok", i + 1, "cbn_ok", i, "clr_ok")
                dve.wait_ge(S["clr_ok"], 2 * i + 2)
                dve.tensor_scalar(cr[:, s, :], cr[:, s, :], bna[:, 0:1], rst[:, 1:2], ALU.subtract, ALU.mult).then_inc(S["cnorm_ok"], 1)
                if i == 0:
                    dve.wait_ge(S["lnq_in"], 32)
                dve.wait_ge(S["cnorm_ok"], i + 1)
                dve.tensor_tensor(cr[:, s, :], cr[:, s, :], lnq[:, 0, :], ALU.mult).then_inc(S["cout_ok"], 1)


_INS = ["x", "w_in", "conv_w", "conv_b", "gla_w_gate2", "gla_b_gate", "gla_norm_w", "w_out", "ln1_g", "ln1_b",
        "router_w", "router_bias", "w1", "w3", "w2", "ln2_g", "ln2_b"]


def kernel(**inputs):
    import numpy as np
    import concourse.bacc as bacc
    from concourse.bass_utils import run_bass_kernel_spmd

    nc = bacc.Bacc("TRN2", target_bir_lowering=False, num_devices=1)
    arrays, aps = {}, {}
    for name in _INS:
        a = np.ascontiguousarray(inputs[name])
        arrays[f"in_{name}_dram"] = a
        aps[name] = nc.dram_tensor(f"in_{name}_dram", a.shape, mybir.dt.from_np(a.dtype), kind="ExternalInput").ap()
    out = nc.dram_tensor("out_0_dram", (1, T, D), F32, kind="ExternalOutput").ap()
    build(nc, aps, out)
    r = run_bass_kernel_spmd(nc, [arrays], core_ids=[0])
    return r.results[0]["out_0_dram"]
```

```python
import math

import concourse.bass as bass
from concourse import mybir
from contextlib import ExitStack

F32, F32R, BF16 = mybir.dt.float32, mybir.dt.float32r, mybir.dt.bfloat16
I32, U32 = mybir.dt.int32, mybir.dt.uint32
ALU = mybir.AluOpType
ACT = mybir.ActivationFunctionType
AX = mybir.AxisListType

P = 128
D = 1024
T = 1024
NT = T // P
NK = D // P
CONV_W = D // 4
CONV_K = 3
SB_H, SB_D = 6, 64
SB_W = SB_H * SB_D
GLA_H, GLA_DV, GLA_DK, GLA_R, GLA_C = 4, 96, 48, 16, 64
GLA_W = GLA_H * GLA_DV
GLA_KW = GLA_H * GLA_DK
OFF = {}
_at = 0
for _n, _s in (("c_h", CONV_W), ("c_b", CONV_W), ("c_c", CONV_W), ("sb_q", SB_W), ("sb_k", SB_W), ("sb_v", SB_W),
               ("g_q", GLA_KW), ("g_k", GLA_KW), ("g_v", GLA_W), ("g_g", GLA_W), ("g_lr", GLA_R)):
    OFF[_n] = _at
    _at += _s
D_PROJ = _at
GATE_NORM = 16.0
CLAMP = 40.0
RMS_EPS = 1e-6
LN_EPS = 1e-5
ALPHA = 2 ** 0.25
NPAIR = SB_H // 2

T_FIRST = [("gq", 0), ("gk", 0), ("gq", 1), ("gk", 1), ("sq", 0), ("sk", 0)]
N_PIECES = ["g_v", "g_g", "sb_v"]
FILL = [("sq", 1), ("sk", 1), ("cc", 0), ("ch", 0), ("sq", 2), ("sk", 2), ("cb", 0), ("cc", 1), ("ch", 1), ("cb", 1)]
NCHUNK_T = len(T_FIRST)
CHUNK_N0 = NCHUNK_T
CHUNK_F0 = NCHUNK_T + 3 * len(N_PIECES)
NCHUNK = CHUNK_F0 + len(FILL)
SECOND = range(CHUNK_N0 + 3, CHUNK_N0 + 6)
FILL_T0 = 0
FILL_N0 = 2 * NCHUNK_T
FILL_F0 = FILL_N0 + NT * len(N_PIECES)
NFILL = FILL_F0 + 2 * len(FILL)
GG_FIRST, GG_LAST = FILL_N0 + NT, FILL_N0 + 2 * NT

UNITS = [(p, i, h) for p in range(NPAIR) for i in range(NT) for h in range(2)]
NU = len(UNITS)
HALVES = [0]
for _p, _i, _h in UNITS:
    HALVES.append(HALVES[-1] + (1 if _i < 4 else 2))
QUARTER = {}
_q = 0
for _u, (_p, _i, _h) in enumerate(UNITS):
    if _i < NT - 1 and _q < 4 * len(FILL):
        QUARTER[_u] = _q
        _q += 1
assert _q == 4 * len(FILL)
CONV_STEP = {}
for _j in range(2):
    for _n, _s0, _steps in (("ch", 0, 4), ("cb", 4, 1)):
        _u = max(_v for _v in QUARTER if QUARTER[_v] == 4 * FILL.index((_n, _j)) + 3)
        for _s in range(_steps):
            CONV_STEP[_u + 1 + _s] = (_j, _s0 + _s)
assert len(CONV_STEP) == 10 and max(CONV_STEP) < NU


def ev_before(f):
    return f - max(0, min(f, GG_LAST) - GG_FIRST)


def gg_before(f):
    return max(0, min(f, GG_LAST) - GG_FIRST)

NE, NGRP = 16, 4
EPG = NE // NGRP
DE = 512
NF = DE // P
TW = 160
TR = TW - P
MAXPASS = -(-T // TW)
NROW = MAXPASS * NE * TW
NPIECE = 3 * NF
BIG = float(1 << 20)


def build(nc, I, out):
    ctx = ExitStack()
    with ctx:
        base = 16512

        def at(name, offset, shape, dt=F32):
            return nc.alloc_sbuf_tensor_at(name, shape, dt, offset=base + offset)

        def sem(name):
            return ctx.enter_context(nc.semaphore(name))

        K = 1024
        xT_hi = at("xT_hi", 0, [P, NK, T], F32R)
        xT_lo = at("xT_lo", 32 * K, [P, NK, T], F32R)
        w_raw = at("w_raw", 64 * K, [P, 2, D])
        w_hi = at("w_hi", 72 * K, [P, 3, D], F32R)
        w_lo = at("w_lo", 84 * K, [P, 3, D], F32R)
        mix = at("mix", 96 * K, [P, NK, T])
        kin = at("kin", 96 * K, [P, 2, T])
        tA = at("tA", 104 * K, [P, T])
        tB = at("tB", 108 * K, [P, T])
        tC = at("tC", 112 * K, [P, T])
        sv = at("sv", 128 * K, [P, NT, SB_W])
        qk0 = at("qk0", 140 * K, [P, 2, T])
        x_row = at("x_row", 116 * K, [P, NT, D])
        w_hi2 = at("w_hi2", 116 * K, [P, 3, D], F32R)
        w_lo2 = at("w_lo2", 128 * K, [P, 3, D], F32R)
        R = 148 * K
        gq = at("gq", R, [P, 2, T])
        gk = at("gk", R + 8 * K, [P, 2, T])
        gv = at("gv", R + 16 * K, [P, NT, GLA_W])
        gg = at("gg", R + 28 * K, [P, NT, GLA_W])
        w_rawg = at("w_rawg", R + 16 * K, [P, 4, NK, P])
        S_st = at("S_st", R + 40 * K, [P, 2, 4, 2 * GLA_DV])
        kteN = at("kteN", R + 46 * K, [P, 2, P])
        sT = at("sT", R + 47 * K, [P, 2, 2, P])
        gy = at("gy", R + 49 * K, [P, GLA_W])
        gsq = at("gsq", R + 50 * K + 512, [P, GLA_W])
        gms = at("gms", R + 52 * K, [P, 8])
        E = at("E", R, [P, 2, T])
        SP = at("SP", R + 8 * K, [P, 2, T])
        aT = at("aT", R + 16 * K, [P, 2, NT, P])
        conv_in = at("conv_in", R + 24 * K, [P, 3, T])
        qk1 = at("qk1", R + 36 * K, [P, 2, T])
        C0 = R + 53 * K
        ident = at("ident", C0, [P, P])
        trimask = at("trimask", C0 + 512, [P, P])
        wg2 = at("wg2", C0 + 1024, [64, 4, 64])
        nw = at("nw", C0 + 2048, [P, GLA_DV])
        cw = at("cw", C0 + 2432, [P, CONV_K, 2])
        cb = at("cb", C0 + 2464, [P, 2])
        bg = at("bg", C0 + 2496, [P, 2])
        dec = at("dec", C0 + 2528, [P, 2, T // GLA_C])
        zb = at("zb", C0 + 2656, [P, GLA_W], BF16)
        zeros = at("zeros", C0 + 3424, [P, GLA_C])

        pp = [ctx.enter_context(nc.psum_tensor(f"bank{i}", [P, 512], F32)) for i in range(2)]
        pz = [ctx.enter_context(nc.psum_tensor(f"pz{i}", [P, 1024], F32)) for i in range(2)]
        pa_ = ctx.enter_context(nc.psum_tensor("bank6", [P, 512], F32))
        po = ctx.enter_context(nc.psum_tensor("bank7", [P, 512], F32))
        xt_bank = [pp[0][:, :], pp[1][:, :], pz[0][:, 0:512], pz[0][:, 512:1024]]
        gate_bank = [pz[0][:, 0:512], pz[0][:, 512:1024], pz[1][:, 0:512], pz[1][:, 512:1024]]
        sc_banks = pz[0][:, :].rearrange("p (b x) -> p b x", b=2)[:, :, 0:2 * P].rearrange("p b (j t) -> p b j t", j=2)
        kt_bank = pz[1][:, 0:2 * P]
        kv_bank = [pz[1][:, 0:384], pz[1][:, 512:512 + 384]]

        wo_hi = at("wo_hi", 0, [P, NK, D], F32R)
        wo_lo = at("wo_lo", 32 * K, [P, NK, D], F32R)
        wo_raw = at("wo_raw", 64 * K, [P, 2, D])
        mixh = at("mixh", 72 * K, [P, 2, NK, P], F32R)
        mixl = at("mixl", 80 * K, [P, 2, NK, P], F32R)
        xres = at("xres", 88 * K, [P, 2, D])
        x1 = at("x1", 128 * K, [P, 2, D])
        x1T = at("x1T", 136 * K, [P, NK, P])
        lnp = at("lnp", 140 * K, [P, 2, D])
        SMALL = {F32: 4, U32: 4, I32: 4, BF16: 2}
        place = [R + 48 * K]

        def small(name, shape, dt=F32):
            place[0] += -place[0] % 32
            t = at(name, place[0], shape, dt)
            place[0] += math.prod(shape[1:]) * SMALL[dt]
            return t

        rw = small("rw", [P, NK, NE])
        rb = small("rb", [P, NE])
        rank0 = small("rank0", [P, EPG])
        ecol = small("ecol", [P, NE])
        tok = small("tok", [P, NT], U32)
        rows_u = small("rows_u", [P, 2, NT], U32)
        g12 = small("g12", [P, 2, NT])
        npi = small("npi", [P, 1], I32)
        bns = small("bns", [P, 2, 6])
        bna = small("bna", [P, 2])
        rst = small("rst", [P, 2])
        passes = small("passes", [P, MAXPASS - 1])
        pcmp = small("pcmp", [P, MAXPASS - 1])
        zidl = small("zidl", [P, NROW // P], U32)
        trib = small("trib", [P, P], BF16)
        oneb = small("oneb", [P, P], BF16)
        idxA = small("idxA", [P, 1], U32)
        idxB = small("idxB", [TR, 1], U32)
        cstat = small("cstat", [P, NT, 2, 6])
        cmv = small("cmv", [P, NT, 2])
        crs = small("crs", [P, NT, 2])
        M = 96 * K
        assert place[0] <= R + 53 * K
        rt = lambda n, o, s, dt=F32: at(n, M + o, s, dt)
        place[0] = M
        rs = small("rs", [P, NT, NE])
        rsel = small("rsel", [P, NT * NGRP, EPG])
        rpair = small("rpair", [P, NT * NGRP, 6])
        rgs = small("rgs", [P, NT, NGRP])
        rgk = small("rgk", [P, NT, NGRP])
        rge = small("rge", [P, NT * NGRP, 3])
        rek = small("rek", [P, NT * NGRP, EPG])
        rmask = small("rmask", [P, NT, NE])
        rgate = small("rgate", [P, NT, NE])
        rden = small("rden", [P, NT])
        rmb = small("rmb", [P, NT, NE], BF16)
        rpos = small("rpos", [P, NT + 1, NE])
        rrow = small("rrow", [P, NT, NE])
        rtmp = small("rtmp", [P, NT, NE])
        rr12 = small("rr12", [P, 2, NT])
        rmax = small("rmax", [P, 1])
        rnp = small("rnp", [P, 1])
        er = at("er", R, [P, NPIECE, D])
        eh = at("eh", 0, [P, NPIECE, D], F32R)
        el = at("el", 48 * K, [P, NPIECE, D], F32R)
        xgA = rt("xgA", 6 * K, [P, D])
        xgB = rt("xgB", 10 * K, [TR, D])
        xT2 = rt("xT2", 14 * K, [P, NK, 2, TW], F32R)
        cross = rt("cross", 24 * K, [P, 2, 2, TW])
        gu = rt("gu", 24 * K + 2560, [P, 2, 2, TW])
        sil = rt("sil", 24 * K + 5120, [P, 2, TW])
        hf = rt("hf", 24 * K + 6400, [P, NF, TW])
        h2 = rt("h2", 24 * K + 8960, [P, NF, 2 * TW], F32R)
        yA = rt("yA", 38 * K, [P, D])
        yB = rt("yB", 42 * K, [TR, D])
        yBl = rt("yBl", 46 * K, [TR, D])
        cy1 = at("cy1", 0, [P, NT, D])
        cy2 = at("cy2", 32 * K, [P, NT, D])
        cx = at("cx", R, [P, NT, D])
        lnq = at("lnq", R + 32 * K, [P, 2, D])
        x1_dram = nc.dram_tensor("x1_scratch", [T, D], F32).ap()
        y_dram = nc.dram_tensor("y_scratch", [NROW, D], F32).ap()
        idl_dram = nc.dram_tensor("slot_tokens", [NROW, 1], U32).ap()
        ob = [[pp[0][:, :], pp[1][:, :]], [pz[0][:, 0:512], pz[0][:, 512:1024]]]
        xb = [pa_[:, 0:2 * TW], po[:, 0:2 * TW]]
        names = ("xt_ps xt_hi xt_lo w_in0 w_in1 wg_in w_hi_ok w_lo_ok proj_ps proj_ev gg_ev "
                 "const_in const_ok gate_ps n_ok m_ok ge_ok gl_ok gsp_ok cs_ok gexp_ok gmul_ok dec_ok sc_ps kt_ps kteN_ok sT_ok "
                 "kv_ps st_ok o_ps gsq_ok gms_ok rstd_ok gy_ok gyT_ps gyT_ev gs_ok "
                 "z_ps zc_ok e_ok ln_ok sp_ok spm_ok sfx_ok arg_ok a_ok am_ok aT_ps aT_ev o_done o_ev conv_ok ggs_ok stored").split()
        names += [f"x_in{i}" for i in range(NT)]
        names += ("wo_in0 wo_in1 wo_hi_ok wo_lo_ok xr_in0 xr_in1 lnp_in mixh_ok mixl_ok ob_ps res_ok bn_ok lrs_ok x1_ok x1_st0 x1_st1 "
                  "x1t_ps x1t_ev lg_ps rexp_ok route_step mask_ok pos_ps route_ok tokc_ok idl_z idl_st0 idl_st1 idx_in pool_go zrow_ok y_zero xg_in "
                  "piece_done eh_ok el_ok cross_ok sum_ok sil_ok h_ok hh_ok hl_ok xtr_ps xTh_ok xTl_ok rowsA_ps yA0_ev yA1_ev yBl_ok yB_ev y_out "
                  "lnq_in c1_ok c2_ok cres_ok cbn_ok clr_ok cnb_ok cnorm_ok cout_ok cgain_ok clast_ok cfin_ok out_st").split()
        names += [f"e_in{p}" for p in range(NPIECE)]
        names += [f"{n}{i}" for n in ("cx_in", "cg_in") for i in range(NT)]
        S = {n: sem(n) for n in names}

        block = ctx.enter_context(nc.Block())
        hs = [0, 64]

        def w_cols(n):
            if n < CHUNK_F0:
                m = n - CHUNK_N0
                return OFF[N_PIECES[m // 3]] + P * (m % 3)
            kind, j = FILL[n - CHUNK_F0]
            return OFF[{"sq": "sb_q", "sk": "sb_k", "cc": "c_c", "ch": "c_h", "cb": "c_b"}[kind]] + P * j

        def slot_of(n):
            return (w_hi2, w_lo2, n - SECOND[0]) if n in SECOND else (w_hi, w_lo, n % 3)

        def raw_chunk(n):
            return w_rawg[:, n, :, :].rearrange("p k c -> p (k c)") if n < 4 else w_raw[:, n % 2, :]

        w_k = I["w_in"][0].rearrange("(k p) n -> p k n", p=P)

        w1v = I["w1"][0].rearrange("e (k p) f -> p e k f", p=P)
        w3v = I["w3"][0].rearrange("e (k p) f -> p e k f", p=P)
        w2v = I["w2"][0].rearrange("e (f p) d -> p e f d", p=P)

        def load_expert(sp, j, e, first=False):
            b = NE * j + e
            for p in range(NPIECE):
                if not first:
                    sp.wait_ge(S["el_ok"], NPIECE * b - NPIECE + p + 1)
                if p < 2 * NF:
                    src = (w1v, w3v)[p % 2][:, bass.ds(e, 1), :, (p // 2) * P:(p // 2 + 1) * P]
                    dst = er[:, p:p + 1, :].rearrange("p e (k f) -> p e k f", k=NK)
                else:
                    src = w2v[:, bass.ds(e, 1), p - 2 * NF, :]
                    dst = er[:, p:p + 1, :]
                sp.dma_start(dst, src).then_inc(S[f"e_in{p}"], 16)

        def passes_of(eng, one_pass):
            one_pass(0)
            eng.wait_ge(S["route_ok"], 3)
            n = eng.value_load(npi[0:1, 0:1], min_val=1, max_val=MAXPASS)
            with eng.If(n > 1):
                with eng.Fori(1, n) as j:
                    one_pass(j)
            return n

        def experts_of(eng, j, block):
            block(NE * j, True)
            with eng.Fori(1, NE - 1) as e:
                block(NE * j + e, True)
            block(NE * j + NE - 1, False)

        def first_block(b):
            return isinstance(b, int) and b == 0

        def norm_stats(dve, buf, s, src, n, done, i, read):
            dve.wait_ge(S[src], n)
            for h in range(2):
                dve.bn_stats(bns[:, h, :], buf[:, s, h * 512:h * 512 + 512]).then_inc(S[done], 1)
            dve.wait_ge(S[done], 4 * i + 2)
            dve.bn_aggr(bna[:, :], bns[:, :, :].rearrange("p a b -> p (a b)")).then_inc(S[done], 1)
            dve.wait_ge(S[done], 4 * i + 3)
            dve.tensor_scalar(rst[:, 0:1], bna[:, 1:2], LN_EPS, None, ALU.add).then_inc(S[done], 1)

        POOL_GAIN = [i for i in range(NT - 1) if i % 3 != 2]

        def gain_and_bias(pool, i):
            pool.wait_ge(S["lnq_in"], 32)
            if i in POOL_GAIN:
                pool.wait_ge(S["cnorm_ok"], i + 1)
                pool.tensor_tensor(cx[:, i, :], cx[:, i, :], lnq[:, 0, :], ALU.mult).then_inc(S["cgain_ok"], 1)
                pool.wait_ge(S["cgain_ok"], POOL_GAIN.index(i) + 1)
            else:
                pool.wait_ge(S["cout_ok"], i + 1 - sum(j <= i for j in POOL_GAIN))
            pool.tensor_tensor(cx[:, i, :], cx[:, i, :], lnq[:, 1, :], ALU.add).then_inc(S["cfin_ok"], 1)

        @block.sync
        def _(sp):
            for i in range(NT):
                sp.dma_start(x_row[:, i, :], I["x"][0, i * P:(i + 1) * P, :]).then_inc(S[f"x_in{i}"], 16)
            sp.wait_ge(S["const_ok"], 5)
            for n in range(4):
                kind, hp = T_FIRST[n]
                src = OFF["g_q"] if kind == "gq" else OFF["g_k"]
                for h in range(2):
                    c0 = src + (2 * hp + h) * GLA_DK
                    sp.dma_start(w_rawg[:, n, :, hs[h]:hs[h] + GLA_DK], w_k[:, :, c0:c0 + GLA_DK]).then_inc(S["wg_in"], 16)
            sp.dma_start(w_rawg[:, 1, :, GLA_DK:64], w_k[:, :, OFF["g_lr"]:OFF["g_lr"] + GLA_R]).then_inc(S["wg_in"], 16)
            for n in range(4, NCHUNK):
                if n >= 6:
                    sp.wait_ge(S["w_lo_ok"], n - 1)
                if n < 6:
                    kind, j = T_FIRST[n]
                    c0 = OFF["sb_q" if kind == "sq" else "sb_k"] + P * j
                else:
                    c0 = w_cols(n)
                sp.dma_start(w_raw[:, n % 2, :].rearrange("p (k c) -> p k c", k=NK), w_k[:, :, c0:c0 + P])\
                    .then_inc(S[f"w_in{n % 2}"], 16)
            w_o = I["w_out"][0].rearrange("(k p) n -> p k n", p=P)
            for k in range(NK):
                if k < 2:
                    sp.wait_ge(S["w_lo_ok"], NCHUNK)
                else:
                    sp.wait_ge(S["wo_lo_ok"], k - 1)
                sp.dma_start(wo_raw[:, k % 2, :], w_o[:, k, :]).then_inc(S[f"wo_in{k % 2}"], 16)
            sp.wait_ge(S["proj_ps"], NFILL)
            for i in range(NT):
                if i >= 2:
                    sp.wait_ge(S["res_ok"], 2 * (i - 1))
                sp.dma_start(xres[:, i % 2, :], I["x"][0, i * P:(i + 1) * P, :]).then_inc(S[f"xr_in{i % 2}"], 16)
                if i == 1:
                    sp.wait_ge(S["o_ev"], NPAIR * NT)
                    sp.wait_ge(S["arg_ok"], NU)
                    sp.wait_ge(S["aT_ev"], HALVES[NU])
                    sp.wait_ge(S["conv_ok"], 10)
                    load_expert(sp, 0, 0, first=True)
                if i >= 1:
                    sp.wait_ge(S["x1_ok"], 3 * i)
                    sp.dma_start(x1_dram[(i - 1) * P:i * P, :], x1[:, (i - 1) % 2, :]).then_inc(S[f"x1_st{(i - 1) % 2}"], 16)
            sp.wait_ge(S["x1_ok"], 3 * NT)
            sp.dma_start(x1_dram[(NT - 1) * P:NT * P, :], x1[:, (NT - 1) % 2, :]).then_inc(S[f"x1_st{(NT - 1) % 2}"], 16)
            with sp.Fori(1, NE) as e:
                load_expert(sp, 0, e)
            sp.wait_ge(S["route_ok"], 3)
            npass = sp.value_load(npi[0:1, 0:1], min_val=1, max_val=MAXPASS)
            with sp.If(npass > 1):
                with sp.Fori(1, npass) as j:
                    with sp.Fori(0, NE) as e:
                        load_expert(sp, j, e)
            sp.wait_ge(S["el_ok"], npass * (NPIECE * NE))
            for i in range(NT):
                sp.dma_start(cx[:, i, :], x1_dram[i * P:(i + 1) * P, :]).then_inc(S[f"cx_in{i}"], 16)
            for a, name in enumerate(("ln2_g", "ln2_b")):
                sp.dma_start(lnq[:, a, :], I[name][0].partition_broadcast(P)).then_inc(S["lnq_in"], 16)
            for i in range(NT):
                if i < NT - 1:
                    sp.wait_ge(S["cfin_ok"], i + 1)
                else:
                    sp.wait_ge(S["clast_ok"], 1)
                sp.dma_start(out[0, i * P:(i + 1) * P, :], cx[:, i, :]).then_inc(S["out_st"], 16)
            sp.wait_ge(S["out_st"], 16 * NT)

        @block.gpsimd
        def _(pool):
            pool.memset(ident[:, :], 0.0).then_inc(S["const_ok"], 1)
            pool.wait_ge(S["const_ok"], 1)
            pool.affine_select(ident[:, :], ident[:, :], [[-1, P]], ALU.not_equal, 1.0, base=0, channel_multiplier=1)\
                .then_inc(S["const_ok"], 1)
            pool.memset(w_rawg[:, :, :, :], 0.0).then_inc(S["const_ok"], 1)
            pool.memset(wg2[:, :, :], 0.0).then_inc(S["const_ok"], 1)
            pool.memset(bg[:, :], 0.0).then_inc(S["const_ok"], 1)
            pool.memset(trimask[:, :], 1.0).then_inc(S["const_ok"], 1)
            pool.memset(zb[:, :], 0.0).then_inc(S["const_ok"], 1)
            pool.memset(zeros[:, :], 0.0).then_inc(S["const_ok"], 1)
            pool.memset(S_st[:, :, :, :], 0.0).then_inc(S["const_ok"], 1)
            pool.wait_ge(S["const_ok"], 9)
            pool.affine_select(trimask[:, :], trimask[:, :], [[1, P]], ALU.is_ge, 0.0, base=0, channel_multiplier=-1)\
                .then_inc(S["const_ok"], 1)
            pool.wait_ge(S["const_ok"], 10)
            pool.memset(trimask[0:64, 64:P], 0.0).then_inc(S["const_ok"], 1)
            for u, (p, i, h) in enumerate(UNITS):
                own = slice(i * P, (i + 1) * P)
                pool.wait_ge(S["sp_ok"], u + 1)
                pool.affine_select(SP[:, u % 2, own], SP[:, u % 2, own], [[-1, P]], ALU.is_gt, 0.0,
                                   base=0, channel_multiplier=1).then_inc(S["spm_ok"], 1)
                pool.wait_ge(S["a_ok"], u + 1)
                pool.affine_select(SP[:, u % 2, own], SP[:, u % 2, own], [[-1, P]], ALU.is_gt, 0.0,
                                   base=0, channel_multiplier=1).then_inc(S["am_ok"], 1)

            pool.wait_ge(S["aT_ev"], HALVES[NU])
            pool.memset(zidl[:, :], 0).then_inc(S["tokc_ok"], 1)
            pool.memset(trib[:, :], 1.0).then_inc(S["tokc_ok"], 1)
            pool.memset(oneb[:, :], 1.0).then_inc(S["tokc_ok"], 1)
            pool.iota(tok[:, :], [[P, NT]], base=0, channel_multiplier=1).then_inc(S["tokc_ok"], 1)
            pool.iota(ecol[:, :], [[TW, NE]], base=0, channel_multiplier=0, allow_small_or_imprecise_dtypes=True).then_inc(S["tokc_ok"], 1)
            pool.iota(rank0[:, :], [[-1, EPG]], base=EPG - 1, channel_multiplier=0, allow_small_or_imprecise_dtypes=True).then_inc(S["tokc_ok"], 1)
            pool.iota(passes[:, :], [[TW, MAXPASS - 1]], base=TW, channel_multiplier=0, allow_small_or_imprecise_dtypes=True).then_inc(S["tokc_ok"], 1)
            pool.wait_ge(S["tokc_ok"], 7)
            pool.affine_select(trib[:, :], trib[:, :], [[1, P]], ALU.is_gt, 0.0, base=0, channel_multiplier=-1).then_inc(S["tokc_ok"], 1)
            pool.dma_start(idl_dram.rearrange("(p c) o -> p (c o)", p=P), zidl[:, :]).then_inc(S["idl_z"], 16)
            pool.wait_ge(S["idl_z"], 16)
            def scatter(c):
                pool.wait_ge(S["route_ok"], 2 + c)
                for i in range(NT):
                    pool.indirect_dma_start(idl_dram, bass.IndirectOffsetOnAxis(rows_u[:, c, i:i + 1], 0), tok[:, i:i + 1], None,
                                            bounds_check=NROW - 1, oob_is_err=True).then_inc(S[f"idl_st{c}"], 16)

            scatter(0)
            for s in range(2):
                pool.wait_ge(S[f"x1_st{s}"], 16 * (NT // 2))
            pool.wait_ge(S["idl_st0"], 16 * NT)

            def gather(b):
                pool.dma_start(idxA[:, :], idl_dram[bass.ds(b * TW, P), :]).then_inc(S["idx_in"], 16)
                pool.dma_start(idxB[:, :], idl_dram[bass.ds(b * TW + P, TR), :]).then_inc(S["idx_in"], 16)
                pool.wait_ge(S["idx_in"], 32 * b + 32)
                pool.wait_ge(S["xtr_ps"], NF * b)
                pool.sem_inc(S["pool_go"], 1)
                pool.indirect_dma_start(xgA[:, :], None, x1_dram, bass.IndirectOffsetOnAxis(idxA[:, 0:1], 0)).then_inc(S["xg_in"], 16)
                pool.indirect_dma_start(xgB[:, :], None, x1_dram, bass.IndirectOffsetOnAxis(idxB[:, 0:1], 0)).then_inc(S["xg_in"], 16)
                pool.wait_ge(S["xg_in"], 32 * b + 32)
                pool.sem_inc(S["pool_go"], 1)

            def store(b):
                pool.wait_ge(S["yA0_ev"], b + 1)
                pool.wait_ge(S["yA1_ev"], b + 1)
                pool.dma_start(y_dram[bass.ds(b * TW, P), :], yA[:, :]).then_inc(S["y_out"], 16)
                pool.wait_ge(S["yB_ev"], 2 * b + 2)
                pool.dma_start(y_dram[bass.ds(b * TW + P, TR), :], yB[:, :]).then_inc(S["y_out"], 16)

            def pool_pass(j):
                gather(NE * j)
                if isinstance(j, int):
                    scatter(1)
                    pool.wait_ge(S["idl_st1"], 16 * NT)
                gather(NE * j + 1)
                with pool.Fori(2, NE) as e:
                    gather(NE * j + e)
                    store(NE * j + e - 2)
                store(NE * j + NE - 2)
                store(NE * j + NE - 1)
            pool_pass(0)
            npass = pool.value_load(npi[0:1, 0:1], min_val=1, max_val=MAXPASS)
            with pool.If(npass > 1):
                pool.memset(xgA[:, :], 0.0).then_inc(S["zrow_ok"], 1)
                pool.wait_ge(S["zrow_ok"], 1)
                with pool.Fori(NE * TW // P, NROW // P) as r:
                    pool.dma_start(y_dram[bass.ds(r * P, P), :], xgA[:, :]).then_inc(S["y_zero"], 16)
                pool.wait_ge(S["y_zero"], 16 * ((NROW - NE * TW) // P))
                with pool.Fori(1, npass) as j:
                    pool_pass(j)

            def token_rows(src):
                for i in range(NT):
                    for c, buf in ((0, cy1), (1, cy2)):
                        pool.indirect_dma_start(buf[:, i, :], None, src, bass.IndirectOffsetOnAxis(rows_u[:, c, i:i + 1], 0))\
                            .then_inc(S[f"cg_in{i}"], 16)
            pool.wait_ge(S["y_out"], npass * (32 * NE))
            pool.sem_inc(S["pool_go"], 1)
            with pool.If(npass < 2):
                token_rows(y_dram[0:NE * TW, :])
            with pool.If(npass > 1):
                token_rows(y_dram)
            for i in range(NT - 1):
                gain_and_bias(pool, i)

        def mm3(pe, dst, k_first, k_last, lhs, rhs, ks):
            for k in ks:
                lh, ll = lhs(k)
                rh, rl = rhs(k)
                pe.matmul(dst, lh, rh, start=(k == k_first), stop=False)
                pe.matmul(dst, lh, rl, start=False, stop=False)
                last = pe.matmul(dst, ll, rh, start=False, stop=(k == k_last))
            return last

        def qk_of(p):
            return qk0 if p % 2 == 0 else qk1

        @block.tensor
        def _(pe):
            def wait_bank(f):
                if f >= 2:
                    if GG_FIRST <= f - 2 < GG_LAST:
                        pe.wait_ge(S["gg_ev"], gg_before(f - 1))
                    else:
                        pe.wait_ge(S["proj_ev"], ev_before(f - 1))

            def t_fill(n, f, half, ks):
                hi, lo, s = slot_of(n)
                ns = slice(half * 512, half * 512 + 512)
                if ks[0] == 0:
                    wait_bank(f)
                    if half == 0:
                        pe.wait_ge(S["w_lo_ok"], n + 1)
                last = mm3(pe, pp[f % 2][:, :], 0, NK - 1,
                           lambda k: (hi[:, s, k * P:(k + 1) * P], lo[:, s, k * P:(k + 1) * P]),
                           lambda k: (xT_hi[:, k, ns], xT_lo[:, k, ns]), ks)
                return last

            def t_piece(n, f0):
                for half in range(2):
                    last = t_fill(n, f0 + half, half, range(NK))
                    last.then_inc(S["proj_ps"], 1)

            def n_tile(m, t):
                f = FILL_N0 + NT * m + t
                wait_bank(f)
                if t == 0:
                    pe.wait_ge(S["w_lo_ok"], CHUNK_N0 + 3 * m + 3)
                ts = slice(t * P, (t + 1) * P)
                hi, lo, _ = slot_of(CHUNK_N0 + 3 * m)
                mm3(pe, pp[f % 2][:, 0:GLA_W], 0, NK - 1,
                    lambda k: (xT_hi[:, k, ts], xT_lo[:, k, ts]),
                    lambda k: (hi[:, :, k * P:(k + 1) * P], lo[:, :, k * P:(k + 1) * P]),
                    range(NK)).then_inc(S["proj_ps"], 1)

            pe.wait_ge(S["const_ok"], 2)
            for i in range(NT):
                pe.wait_ge(S[f"x_in{i}"], 16)
                for half in range(2):
                    c = 2 * i + half
                    if c >= 4:
                        pe.wait_ge(S["xt_lo"], c - 3)
                    for j in range(4):
                        k = 4 * half + j
                        last = pe.transpose(xt_bank[c % 4][:, j * P:(j + 1) * P], x_row[:, i, k * P:(k + 1) * P], ident[:, :])
                    last.then_inc(S["xt_ps"], 1)
            pe.wait_ge(S["xt_lo"], 2 * NT)
            pe.wait_ge(S["const_ok"], 11)
            for n in range(NCHUNK_T):
                t_piece(n, 2 * n)
                if n == 1 or n == 3:
                    hp = n // 2
                    pe.wait_ge(S["const_in"], 16 * (CONV_K + 3 + GLA_H))
                    pe.wait_ge(S["proj_ev"], 2 * 2)
                    for half in range(2):
                        pe.matmul(gate_bank[2 * hp + half], wg2[:, 2 * hp:2 * hp + 2, :], gk[0:64, 0, half * 512:half * 512 + 512],
                                  start=True, stop=True).then_inc(S["gate_ps"], 1)
            for m in range(2):
                for t in range(NT):
                    n_tile(m, t)
            for t in range(NT + 2):
                if t < NT:
                    ts = slice(t * P, (t + 1) * P)
                    if t == 0:
                        pe.wait_ge(S["gmul_ok"], 6)
                    if t >= 1:
                        pe.wait_ge(S["sT_ok"], t)
                    for h in range(GLA_H):
                        r = slice(hs[h % 2], hs[h % 2] + GLA_DK)
                        last = pe.matmul(sc_banks[:, h % 2, h // 2, :], kin[r, h // 2, ts], gq[r, h // 2, ts], start=True, stop=True)
                    last.then_inc(S["sc_ps"], 1)
                    if t >= 1:
                        pe.wait_ge(S["st_ok"], 8 * t)
                    for hp in range(2):
                        last = pe.transpose(kt_bank[:, hp * P:(hp + 1) * P], gk[:, hp, ts], ident[:, :])
                    last.then_inc(S["kt_ps"], 1)
                if 1 <= t <= NT:
                    c = t - 1
                    ts = slice(c * P, (c + 1) * P)
                    pe.wait_ge(S["sT_ok"], c + 1)
                    if c >= 1:
                        pe.wait_ge(S["gs_ok"], c)
                        pe.wait_ge(S["st_ok"], 8 * (c - 1) + 8)
                    pe.matmul(pa_[:, 0:GLA_W], zb[:, 0:P], zb[:, :], start=True, stop=False, skip_group_check=True)
                    for h in range(GLA_H):
                        pe.matmul(pa_[:, h * GLA_DV:(h + 1) * GLA_DV], sT[:, h % 2, h // 2, :], gv[:, c, h * GLA_DV:(h + 1) * GLA_DV],
                                  start=False, stop=False, skip_group_check=True)
                    for cc in range(2):
                        ch = 2 * c + cc
                        if cc == 1:
                            pe.wait_ge(S["st_ok"], 8 * c + 4)
                        for hp in range(2):
                            last = pe.matmul(pa_[64 * cc:64 * cc + 64, hp * 192:hp * 192 + 192],
                                             gq[:, hp, ch * GLA_C:(ch + 1) * GLA_C], S_st[:, hp, ch % 4, :],
                                             start=False, stop=(hp == 1), skip_group_check=True)
                    last.then_inc(S["o_ps"], 1)
                if t >= 2:
                    c = t - 2
                    pe.wait_ge(S["gy_ok"], c + 1)
                    if c >= 1:
                        pe.wait_ge(S["gyT_ev"], c)
                    for j in range(3):
                        last = pe.transpose(po[:, j * P:(j + 1) * P], gy[:, j * P:(j + 1) * P], ident[:, :])
                    last.then_inc(S["gyT_ps"], 1)
                if t < NT:
                    n_tile(2, t)
                    pe.wait_ge(S["kteN_ok"], t + 1)
                    for cc in range(2):
                        for hp in range(2):
                            last = pe.matmul(kv_bank[cc][:, hp * 192:hp * 192 + 192], kteN[64 * cc:64 * cc + 64, hp, :],
                                             gv[64 * cc:64 * cc + 64, t, hp * 192:hp * 192 + 192], start=True, stop=True)
                    last.then_inc(S["kv_ps"], 1)

            def z_of(u):
                p, i, h = UNITS[u]
                q, r = qk_of(p), slice(64 * h, 64 * h + 64)
                if u == 0:
                    pe.wait_ge(S["gyT_ev"], NT)
                    pe.wait_ge(S["st_ok"], 8 * NT - 4)
                    pe.wait_ge(S["gs_ok"], NT)
                    pe.wait_ge(S["proj_ev"], ev_before(FILL_F0))
                if (i, h) == (0, 0) and p >= 1:
                    pe.wait_ge(S["proj_ev"], ev_before(FILL_F0 + 2 * (FILL.index(("sk", p)) + 1)))
                if u >= 2:
                    pe.wait_ge(S["arg_ok"], u - 1)
                W = (i + 1) * P
                for c in range(0, W, 512):
                    e = min(W, c + 512)
                    last = pe.matmul(pz[u % 2][:, c:e], q[r, 0, i * P:(i + 1) * P], q[r, 1, c:e], start=True, stop=True)
                last.then_inc(S["z_ps"], 1)

            def pv_of(u):
                p, i, h = UNITS[u]
                pe.wait_ge(S["aT_ev"], HALVES[u + 1])
                if h == 0 and u >= 2:
                    pe.wait_ge(S["o_ev"], (u // 2))
                for j in range(i + 1):
                    last = pe.matmul(po[64 * h:64 * h + 64, 0:P], sv[:, j, (2 * p + h) * SB_D:(2 * p + h + 1) * SB_D],
                                     aT[:, u % 2, j, :], start=(j == 0), stop=(j == i))
                last.then_inc(S["o_done"], 1)

            def t_of(u, half):
                p, i, h = UNITS[u]
                g = HALVES[u] + half
                if g >= 1:
                    pe.wait_ge(S["aT_ev"], g)
                if half == 0:
                    pe.wait_ge(S["am_ok"], u + 1)
                js = range(4 * half, min(i + 1, 4 * half + 4))
                for j in js:
                    last = pe.transpose(pa_[:, (j % 4) * P:(j % 4 + 1) * P], SP[:, u % 2, j * P:(j + 1) * P], ident[:, :])
                last.then_inc(S["aT_ps"], 1)

            z_of(0)
            z_of(1)
            for u, (p, i, h) in enumerate(UNITS):
                if u + 2 < NU:
                    z_of(u + 2)
                if u >= 1:
                    pv_of(u - 1)
                t_of(u, 0)
                if u in QUARTER:
                    q = QUARTER[u]
                    fi, half, kq = q // 4, (q // 2) % 2, q % 2
                    last = t_fill(CHUNK_F0 + fi, FILL_F0 + 2 * fi + half, half, range(4 * kq, 4 * kq + 4))
                    if kq == 1:
                        last.then_inc(S["proj_ps"], 1)
                if i >= 4:
                    t_of(u, 1)
            pv_of(NU - 1)
            pe.wait_ge(S["aT_ev"], HALVES[NU])
            pe.wait_ge(S["proj_ev"], ev_before(NFILL))
            pe.wait_ge(S["arg_ok"], NU)
            for i in range(NT + 2):
                if i >= 2:
                    c = i - 2
                    pe.wait_ge(S["x1_ok"], 3 * c + 3)
                    if c >= 1:
                        pe.wait_ge(S["x1t_ev"], c)
                    for k in range(NK):
                        last = pe.transpose(pz[1][:, k * P:(k + 1) * P], x1[:, c % 2, k * P:(k + 1) * P], ident[:, :])
                    last.then_inc(S["x1t_ps"], 1)
                if i < NT:
                    pe.wait_ge(S["mixl_ok"], i + 1)
                    for half in range(2):
                        if i >= 2:
                            pe.wait_ge(S["res_ok"], 2 * (i - 2) + half + 1)
                        ns = slice(half * 512, half * 512 + 512)
                        for k in range(NK):
                            if i == 0 and half == 0:
                                pe.wait_ge(S["wo_lo_ok"], k + 1)
                            last = mm3(pe, ob[i % 2][half], 0, NK - 1,
                                       lambda k: (mixh[:, i % 2, k, :], mixl[:, i % 2, k, :]),
                                       lambda k: (wo_hi[:, k, ns], wo_lo[:, k, ns]), [k])
                        last.then_inc(S["ob_ps"], 1)
                if i >= 2:
                    c = i - 2
                    if c == 0:
                        pe.wait_ge(S["lnp_in"], 16 * 4)
                    pe.wait_ge(S["x1t_ev"], c + 1)
                    for k in range(NK):
                        last = pe.matmul(pa_[:, c * NE:(c + 1) * NE], x1T[:, k, :], rw[:, k, :], start=(k == 0), stop=(k == NK - 1))
                    last.then_inc(S["lg_ps"], 1)
            pe.wait_ge(S["tokc_ok"], 8)
            pe.wait_ge(S["mask_ok"], 1)
            rk = po[:, 0:(NT + 1) * NE]
            pe.matmul(rk, zb[:, 0:P], zb[:, 0:(NT + 1) * NE], start=True, stop=False, skip_group_check=True)
            pe.matmul(po[:, 0:NT * NE], trib[:, :], rmb[:, :, :], start=False, stop=False, skip_group_check=True)
            for j in range(NT):
                last = pe.matmul(po[:, (j + 1) * NE:(NT + 1) * NE], oneb[:, :], rmb[:, j:j + 1, :].to_broadcast([P, NT - j, NE]),
                                 start=False, stop=(j == NT - 1), skip_group_check=True)
            last.then_inc(S["pos_ps"], 1)

            def x_transposes(b, rounds):
                pe.wait_ge(S["xg_in"], 32 * b + 32)
                for r in rounds:
                    if r >= 2:
                        pe.wait_ge(S["xTl_ok"], 4 * b + r - 1)
                    for dd in range(2):
                        d = 2 * r + dd
                        pe.transpose(xb[r % 2][:, dd * TW:dd * TW + P], xgA[:, d * P:(d + 1) * P], ident[:, :])
                        last = pe.transpose(xb[r % 2][:, dd * TW + P:(dd + 1) * TW], xgB[:, d * P:(d + 1) * P], ident[0:TR, 0:TR])
                    last.then_inc(S["xtr_ps"], 1)

            def pe_block(b, nxt):
                pe.wait_ge(S["xTl_ok"], 4 * b + 4)
                for f in range(NF):
                    if f >= 2 or not first_block(b):
                        pe.wait_ge(S["sum_ok"], 4 * b + f - 1)
                    if f == 1 and not first_block(b):
                        pe.wait_ge(S["yB_ev"], 2 * b)
                    for w in range(2):
                        p = 2 * f + w
                        bank = pz[f % 2][:, w * 512:w * 512 + 2 * TW]
                        pe.wait_ge(S["el_ok"], NPIECE * b + p + 1)
                        for k in range(NK):
                            ks = slice(k * P, (k + 1) * P)
                            pe.matmul(bank, eh[:, p, ks], xT2[:, k, :, :].rearrange("p a t -> p (a t)"),
                                      start=(k == 0), stop=False, skip_group_check=True)
                            last = pe.matmul(bank[:, 0:TW], el[:, p, ks], xT2[:, k, 0, :], start=False, stop=(k == NK - 1),
                                             skip_group_check=True)
                        last.then_inc(S["piece_done"], 1)
                if nxt:
                    x_transposes(b + 1, (0, 1))
                if not first_block(b):
                    pe.wait_ge(S["yA0_ev"], b)
                    pe.wait_ge(S["yA1_ev"], b)
                for f in range(NF):
                    pe.wait_ge(S["hl_ok"], 4 * b + f + 1)
                    pe.wait_ge(S["el_ok"], NPIECE * b + 2 * NF + f + 1)
                    for half in range(2):
                        w = slice(half * 512, half * 512 + 512)
                        last = mm3(pe, pp[half][:, :], 0, NF - 1, lambda f: (h2[:, f, 0:P], h2[:, f, TW + TR:]),
                                   lambda f: (eh[:, 2 * NF + f, w], el[:, 2 * NF + f, w]), [f])
                        if f == NF - 1:
                            last.then_inc(S["rowsA_ps"], 1)
                if nxt:
                    x_transposes(b + 1, (2, 3))
                for f in range(NF):
                    for half in range(2):
                        w = slice(half * 512, half * 512 + 512)
                        pe.matmul(pz[1][0:2 * TR, w], h2[:, f, P:TW + TR], eh[:, 2 * NF + f, w],
                                  start=(f == 0), stop=False, skip_group_check=True)
                        last = pe.matmul(pz[1][0:TR, w], h2[:, f, P:TW], el[:, 2 * NF + f, w], start=False, stop=(f == NF - 1),
                                         skip_group_check=True)
                    last.then_inc(S["piece_done"], 1)

            def pe_pass(j):
                x_transposes(NE * j, range(4))
                experts_of(pe, j, pe_block)
            passes_of(pe, pe_pass)

        def last_fill(n):
            if n < CHUNK_N0:
                return 2 * n + 2
            if n < CHUNK_F0:
                return FILL_N0 + NT * ((n - CHUNK_N0) // 3 + 1)
            return FILL_F0 + 2 * (n - CHUNK_F0) + 2

        def wait_raw(eng, n):
            if n < 4:
                eng.wait_ge(S["wg_in"], 16 * 9)
            else:
                eng.wait_ge(S[f"w_in{n % 2}"], 16 * ((n - 4) // 2 + 1))

        @block.scalar
        def _(act):
            act.preload_act_table_set("natural_log_exp_and_others")
            with nc.allow_non_contiguous_dma(reason="a few hundred parameters"):
                for i in range(CONV_K):
                    act.dma_start(cw[:, i, :], I["conv_w"][0, i, :].rearrange("(c p) -> p c", p=P)).then_inc(S["const_in"], 16)
                act.dma_start(cb[:, :], I["conv_b"][0].rearrange("(c p) -> p c", p=P)).then_inc(S["const_in"], 16)
                act.dma_start(nw[:, :], I["gla_norm_w"][0].partition_broadcast(P))\
                    .then_inc(S["const_in"], 16)
                act.wait_ge(S["const_ok"], 5)
                act.dma_start(wg2[GLA_DK:64, :, 0:GLA_DK], I["gla_w_gate2"][0].rearrange("r (h d) -> r h d", h=GLA_H))\
                    .then_inc(S["const_in"], 16)
                for h in range(GLA_H):
                    act.dma_start(bg[hs[h % 2]:hs[h % 2] + GLA_DK, h // 2:h // 2 + 1],
                                  I["gla_b_gate"][0, h * GLA_DK:(h + 1) * GLA_DK].rearrange("(d o) -> d o", o=1))\
                        .then_inc(S["const_in"], 16)

            def split_hi(n):
                wait_raw(act, n)
                before = n - 6 if CHUNK_N0 + 6 <= n < CHUNK_N0 + 9 else n - 3
                if n >= 3 and n not in SECOND:
                    act.wait_ge(S["proj_ps"], last_fill(before))
                hi, _, s = slot_of(n)
                act.activation(hi[:, s, :], raw_chunk(n), ACT.Copy).then_inc(S["w_hi_ok"], 1)

            def evac(f, dst, scale=1.0, cols=512):
                act.wait_ge(S["proj_ps"], f + 1)
                act.activation(dst, pp[f % 2][:, 0:cols], ACT.Copy, scale=scale).then_inc(S["proj_ev"], 1)

            for c in range(2 * NT):
                i, half = c // 2, c % 2
                act.wait_ge(S["xt_ps"], c + 1)
                act.activation(xT_hi[:, 4 * half:4 * half + 4, i * P:(i + 1) * P],
                               xt_bank[c % 4].rearrange("p (k t) -> p k t", k=4), ACT.Copy).then_inc(S["xt_hi"], 1)
            split_hi(0)
            split_hi(1)
            for n in range(NCHUNK_T):
                split_hi(n + 2)
                kind, j = T_FIRST[n]
                for half in range(2):
                    hsl = slice(half * 512, half * 512 + 512)
                    dst = {"gq": gq[:, j, hsl], "gk": gk[:, j, hsl], "sq": qk0[:, 0, hsl], "sk": qk0[:, 1, hsl]}[kind]
                    evac(2 * n + half, dst, {"gq": GLA_DK ** -0.5, "sq": SB_D ** -0.5}.get(kind, 1.0))
            split_hi(NCHUNK_T + 2)

            def gate_steps(hp):
                act.wait_ge(S["m_ok"], hp + 1)
                act.activation(tB[:, :], tB[:, :], ACT.Exp).then_inc(S["ge_ok"], 1)
                act.wait_ge(S["ge_ok"], hp + 1)
                act.activation(tB[:, :], tB[:, :], ACT.Ln, bias=1.0).then_inc(S["gl_ok"], 1)
                yield
                act.wait_ge(S["cs_ok"], 17 * hp + 16)
                act.activation(tB[:, :], tA[:, :], ACT.Exp, scale=-1.0 / GATE_NORM).then_inc(S["gexp_ok"], 1)
                act.activation(tC[:, :], tA[:, :], ACT.Exp, scale=1.0 / GATE_NORM).then_inc(S["gexp_ok"], 1)
                yield
                act.wait_ge(S["cs_ok"], 17 * hp + 17)
                act.activation(tB[:, :], tB[:, :], ACT.Exp, scale=1.0 / GATE_NORM).then_inc(S["gexp_ok"], 1)
                act.activation(dec[:, hp, :], tA[:, :].rearrange("p (c t) -> p c t", t=GLA_C)[:, :, GLA_C - 1],
                               ACT.Exp, scale=-1.0 / GATE_NORM).then_inc(S["dec_ok"], 1)
                yield

            steps = [s for hp in range(2) for s in [gate_steps(hp)] * 3]
            for t in range(NT):
                evac(FILL_N0 + t, gv[:, t, :], cols=GLA_W)
                if t < 6:
                    next(steps[t])
                if t % 2 == 1 and t < 6:
                    split_hi(CHUNK_N0 + 3 + t // 2)
            for t in range(NT):
                f = FILL_N0 + NT + t
                act.wait_ge(S["proj_ps"], f + 1)
                act.activation(gg[:, t, :], pp[f % 2][:, 0:GLA_W], ACT.Silu).then_inc(S["gg_ev"], 1)
                if t in (1, 3, 5):
                    split_hi(CHUNK_N0 + 6 + t // 2)
            act.preload_act_table_set("natural_log_exp_and_others")
            for t in range(NT + 2):
                if t < NT:
                    act.wait_ge(S["kt_ps"], t + 1)
                    if t >= 1:
                        act.wait_ge(S["kv_ps"], t)
                    act.activation(kteN[:, :, :], kt_bank.rearrange("p (h c) -> p h c", h=2), ACT.Copy).then_inc(S["kteN_ok"], 1)
                if 1 <= t <= NT:
                    act.wait_ge(S["o_ps"], t)
                    if t >= 2:
                        act.wait_ge(S["gms_ok"], 2 * (t - 1))
                    act.activation(gsq[:, :], pa_[:, 0:GLA_W], ACT.Square).then_inc(S["gsq_ok"], 1)
                if t >= 2:
                    act.wait_ge(S["gyT_ps"], t - 1)
                    act.activation(mix[:, 5:8, (t - 2) * P:(t - 1) * P], po[:, 0:3 * P].rearrange("p (j t) -> p j t", j=3),
                                   ACT.Copy).then_inc(S["gyT_ev"], 1)
                if 1 <= t <= NT:
                    act.wait_ge(S["gms_ok"], 2 * t)
                    act.activation(gms[:, 0:4], gms[:, 0:4], ACT.Ln).then_inc(S["rstd_ok"], 1)
                    act.wait_ge(S["rstd_ok"], 2 * t - 1)
                    act.activation(gms[:, 4:8], gms[:, 0:4], ACT.Exp, scale=-0.5).then_inc(S["rstd_ok"], 1)
                if t < NT:
                    evac(FILL_N0 + 2 * NT + t, sv[:, t, :], cols=SB_W)
            split_hi(CHUNK_F0)

            def softplus_of(u):
                W = (UNITS[u][1] + 1) * P
                act.wait_ge(S["zc_ok"], u + 1)
                act.activation(E[:, u % 2, 0:W], E[:, u % 2, 0:W], ACT.Exp).then_inc(S["e_ok"], 1)
                act.wait_ge(S["e_ok"], u + 1)
                act.activation(E[:, u % 2, 0:W], E[:, u % 2, 0:W], ACT.Ln, bias=1.0).then_inc(S["ln_ok"], 1)

            def weights_of(u):
                W = (UNITS[u][1] + 1) * P
                act.wait_ge(S["arg_ok"], u + 1)
                act.activation(SP[:, u % 2, 0:W], SP[:, u % 2, 0:W], ACT.Exp).then_inc(S["a_ok"], 1)

            def weights_out(u, half):
                i = UNITS[u][1]
                lo, hi = 4 * half, min(i + 1, 4 * half + 4)
                act.wait_ge(S["aT_ps"], HALVES[u] + half + 1)
                if half == 0 and u >= 2:
                    act.wait_ge(S["o_done"], u - 1)
                act.activation(aT[:, u % 2, lo:hi, :], pa_[:, 0:(hi - lo) * P].rearrange("p (j t) -> p j t", t=P),
                               ACT.Copy).then_inc(S["aT_ev"], 1)

            def evac_fill(f):
                kind, j = FILL[f // 2]
                hsl = slice((f % 2) * 512, (f % 2) * 512 + 512)
                if kind in ("sq", "sk"):
                    dst = qk_of(j)[:, 0 if kind == "sq" else 1, hsl]
                    if j == 2:
                        act.wait_ge(S["z_ps"], 2 * NT)
                else:
                    dst = conv_in[:, {"cc": 0, "ch": 1, "cb": 2}[kind], hsl]
                    if j == 1:
                        act.wait_ge(S["conv_ok"], 5 if kind == "cb" else 4)
                evac(FILL_F0 + f, dst, SB_D ** -0.5 if kind == "sq" else 1.0)

            def split_wo_hi(k):
                if k == 0:
                    act.wait_ge(S["proj_ps"], NFILL)
                act.wait_ge(S[f"wo_in{k % 2}"], 16 * (k // 2 + 1))
                act.activation(wo_hi[:, k, :], wo_raw[:, k % 2, :], ACT.Copy).then_inc(S["wo_hi_ok"], 1)

            softplus_of(0)
            softplus_of(1)
            weights_of(0)
            for u, (p, i, h) in enumerate(UNITS):
                weights_out(u, 0)
                if u + 2 < NU:
                    softplus_of(u + 2)
                if u >= 1 and QUARTER.get(u - 1, 0) % 2 == 1:
                    evac_fill(QUARTER[u - 1] // 2)
                if h == 0 and u >= 2:
                    pp_, ii = UNITS[u - 1][0], UNITS[u - 1][1]
                    act.wait_ge(S["o_done"], u)
                    act.activation(mix[:, 2 + pp_, ii * P:(ii + 1) * P], po[:, 0:P], ACT.Copy).then_inc(S["o_ev"], 1)
                if u + 1 < NU:
                    weights_of(u + 1)
                if i >= 4:
                    weights_out(u, 1)
                q = QUARTER.get(u, 1)
                if q % 4 == 0 and q // 4 + 1 < len(FILL):
                    split_hi(CHUNK_F0 + q // 4 + 1)
                if u >= NU - 4:
                    split_wo_hi(2 * (u - NU + 4))
                    split_wo_hi(2 * (u - NU + 4) + 1)

            def mix_hi(i):
                if i == 0:
                    act.wait_ge(S["conv_ok"], 10)
                    act.wait_ge(S["gyT_ev"], NT)
                act.wait_ge(S["o_ev"], 2 * NT + i + 1)
                if i >= 2:
                    act.wait_ge(S["ob_ps"], 2 * (i - 1))
                act.activation(mixh[:, i % 2, :, :], mix[:, :, i * P:(i + 1) * P], ACT.Copy).then_inc(S["mixh_ok"], 1)
            mix_hi(0)
            act.wait_ge(S["o_done"], NU)
            act.activation(mix[:, 2 + NPAIR - 1, (NT - 1) * P:NT * P], po[:, 0:P], ACT.Copy).then_inc(S["o_ev"], 1)
            act.wait_ge(S["am_ok"], NU)
            act.dma_start(lnp[:, 0, :], I["ln1_g"][0].partition_broadcast(P)).then_inc(S["lnp_in"], 16)
            act.dma_start(lnp[:, 1, :], I["ln1_b"][0].partition_broadcast(P)).then_inc(S["lnp_in"], 16)
            act.dma_start(rw[:, :, :], I["router_w"].rearrange("(k p) e -> p k e", p=P)).then_inc(S["lnp_in"], 16)
            act.dma_start(rb[:, :], I["router_bias"].partition_broadcast(P)).then_inc(S["lnp_in"], 16)
            for i in range(NT + 2):
                if i + 1 < NT:
                    mix_hi(i + 1)
                if i >= 2:
                    act.wait_ge(S["x1t_ps"], i - 1)
                    if i >= 3:
                        act.wait_ge(S["lg_ps"], i - 2)
                    act.activation(x1T[:, :, :], pz[1][:, :].rearrange("p (k t) -> p k t", k=NK), ACT.Copy).then_inc(S["x1t_ev"], 1)
                if i < NT:
                    act.wait_ge(S["bn_ok"], 4 * i + 4)
                    act.activation(rst[:, 0:1], rst[:, 0:1], ACT.Ln).then_inc(S["lrs_ok"], 1)
                    act.wait_ge(S["lrs_ok"], 2 * i + 1)
                    act.activation(rst[:, 1:2], rst[:, 0:1], ACT.Exp, scale=-0.5).then_inc(S["lrs_ok"], 1)
            act.wait_ge(S["lg_ps"], NT)
            act.activation(rs[:, :, :], pa_[:, 0:NT * NE].rearrange("p (i e) -> p i e", e=NE), ACT.Exp, scale=-1.0).then_inc(S["rexp_ok"], 1)

            def piece_hi(b, p):
                act.wait_ge(S[f"e_in{p}"], 16 * b + 16)
                if not (isinstance(b, int) and b == 0):
                    act.wait_ge(S["piece_done"], NPIECE * b - NPIECE + p + 1)
                act.activation(eh[:, p, :], er[:, p, :], ACT.Copy).then_inc(S["eh_ok"], 1)

            def x_hi(b, rounds=range(4)):
                for r in rounds:
                    act.wait_ge(S["xtr_ps"], 4 * b + r + 1)
                    act.activation(xT2[:, 2 * r:2 * r + 2, 0, :], xb[r % 2].rearrange("p (d t) -> p d t", d=2), ACT.Copy).then_inc(S["xTh_ok"], 1)

            def act_block(b, nxt):
                for f in range(NF):
                    act.wait_ge(S["piece_done"], NPIECE * b + 2 * f + 2)
                    act.activation(cross[:, f % 2, :, :], pz[f % 2][:, :].rearrange("p (w c) -> p w c", w=2)[:, :, TW:2 * TW],
                                   ACT.Copy).then_inc(S["cross_ok"], 1)
                    if nxt and f < NF - 1:
                        piece_hi(b + 1, 2 * f)
                    act.wait_ge(S["sum_ok"], 4 * b + f + 1)
                    act.activation(sil[:, f % 2, :], gu[:, f % 2, 0, :], ACT.Silu).then_inc(S["sil_ok"], 1)
                    if nxt and f < NF - 1:
                        piece_hi(b + 1, 2 * f + 1)
                    act.wait_ge(S["h_ok"], 4 * b + f + 1)
                    act.activation(h2[:, f, 0:TW], hf[:, f, :], ACT.Copy).then_inc(S["hh_ok"], 1)
                if nxt:
                    x_hi(b + 1, (0, 1))
                    piece_hi(b + 1, 2 * NF - 2)
                    piece_hi(b + 1, 2 * NF - 1)
                    x_hi(b + 1, (2, 3))
                act.wait_ge(S["rowsA_ps"], 2 * b + 2)
                if not first_block(b):
                    act.wait_ge(S["y_out"], 32 * b)
                act.activation(yA[:, 512:], pp[1][:, :], ACT.Copy).then_inc(S["yA1_ev"], 1)
                if nxt:
                    for p in range(2 * NF, NPIECE - 1):
                        piece_hi(b + 1, p)
                act.wait_ge(S["piece_done"], NPIECE * b + NPIECE)
                if not first_block(b):
                    act.wait_ge(S["yB_ev"], 2 * b)
                for half in range(2):
                    act.activation(yBl[:, half * 512:half * 512 + 512], pz[1][TR:2 * TR, half * 512:half * 512 + 512], ACT.Copy)\
                        .then_inc(S["yBl_ok"], 1)
                if nxt:
                    piece_hi(b + 1, NPIECE - 1)

            def act_pass(j):
                b0 = NE * j
                if isinstance(j, int):
                    act.wait_ge(S["ob_ps"], 2 * NT)
                    act.wait_ge(S["res_ok"], 2 * NT)
                for p in range(NPIECE):
                    piece_hi(b0, p)
                    if p == 5:
                        x_hi(b0)
                experts_of(act, j, act_block)
            passes_of(act, act_pass)

            act.preload_act_table_set("natural_log_exp_and_others")
            for i in range(NT + 1):
                if i < NT:
                    act.wait_ge(S[f"cg_in{i}"], 32)
                    act.activation(cy1[:, i, :], cy1[:, i, :], ACT.Copy, scale=g12[:, 0, i:i + 1]).then_inc(S["c1_ok"], 1)
                if i >= 1:
                    c = i - 1
                    act.wait_ge(S["cbn_ok"], 4 * c + 4)
                    act.activation(crs[:, c, 1:2], cmv[:, c, 1:2], ACT.Ln).then_inc(S["clr_ok"], 1)
                    act.wait_ge(S["clr_ok"], 2 * c + 1)
                    act.activation(crs[:, c, 0:1], crs[:, c, 1:2], ACT.Exp, scale=-0.5).then_inc(S["clr_ok"], 1)
                    act.wait_ge(S["cnb_ok"], c + 1)
                    act.activation(cx[:, c, :], cx[:, c, :], ACT.Identity, bias=crs[:, c, 1:2], scale=crs[:, c, 0:1])\
                        .then_inc(S["cnorm_ok"], 1)

        @block.vector
        def _(dve):
            def split_lo(n):
                dve.wait_ge(S["w_hi_ok"], n + 1)
                hi, lo, s = slot_of(n)
                dve.tensor_tensor(lo[:, s, :], raw_chunk(n), hi[:, s, :].bitcast(F32), ALU.subtract)\
                    .then_inc(S["w_lo_ok"], 1)

            for c in range(2 * NT):
                i, half = c // 2, c % 2
                dve.wait_ge(S["xt_hi"], c + 1)
                ts = slice(i * P, (i + 1) * P)
                dve.tensor_tensor(xT_lo[:, 4 * half:4 * half + 4, ts], xt_bank[c % 4].rearrange("p (k t) -> p k t", k=4),
                                  xT_hi[:, 4 * half:4 * half + 4, ts].bitcast(F32), ALU.subtract).then_inc(S["xt_lo"], 1)
            for n in range(CHUNK_N0 + 3):
                split_lo(n)

            dve.wait_ge(S["const_in"], 16 * (CONV_K + 3 + GLA_H))
            for hp in range(2):
                if hp == 1:
                    dve.wait_ge(S["dec_ok"], 1)
                for half in range(2):
                    dve.wait_ge(S["gate_ps"], 2 * hp + half + 1)
                    dve.tensor_scalar(tA[:, half * 512:half * 512 + 512], gate_bank[2 * hp + half], bg[:, hp:hp + 1], -1.0,
                                      ALU.add, ALU.mult).then_inc(S["n_ok"], 1)
                dve.wait_ge(S["n_ok"], 2 * hp + 2)
                dve.tensor_scalar(tB[:, :], tA[:, :], CLAMP, None, ALU.min).then_inc(S["m_ok"], 1)
                dve.wait_ge(S["gl_ok"], hp + 1)
                dve.tensor_tensor(tB[:, :], tB[:, :], tA[:, :], ALU.max).then_inc(S["gsp_ok"], 1)
                dve.wait_ge(S["gsp_ok"], hp + 1)
                for c in range(T // GLA_C):
                    cs = slice(c * GLA_C, (c + 1) * GLA_C)
                    dve.tensor_tensor_scan(tA[:, cs], tB[:, cs], zeros[:, :], 0.0, ALU.add, ALU.add).then_inc(S["cs_ok"], 1)
                dve.wait_ge(S["gate_ps"], 4)
                dve.wait_ge(S["gexp_ok"], 3 * hp + 1)
                dve.tensor_tensor(gq[:, hp, :], gq[:, hp, :], tB[:, :], ALU.mult).then_inc(S["gmul_ok"], 1)
                dve.wait_ge(S["gexp_ok"], 3 * hp + 2)
                dve.tensor_tensor(kin[:, hp, :], gk[:, hp, :], tC[:, :], ALU.mult).then_inc(S["gmul_ok"], 1)
                csv = tA[:, :].rearrange("p (c t) -> p c t", t=GLA_C)
                dve.wait_ge(S["gmul_ok"], 3 * hp + 1)
                dve.tensor_tensor(tB[:, :].rearrange("p (c t) -> p c t", t=GLA_C), csv,
                                  csv[:, :, GLA_C - 1:GLA_C].to_broadcast([P, T // GLA_C, GLA_C]), ALU.subtract)\
                    .then_inc(S["cs_ok"], 1)
                if hp == 0:
                    split_lo(CHUNK_N0 + 3)
                dve.wait_ge(S["gexp_ok"], 3 * hp + 3)
                dve.tensor_tensor(gk[:, hp, :], gk[:, hp, :], tB[:, :], ALU.mult).then_inc(S["gmul_ok"], 1)

            split_lo(CHUNK_N0 + 4)
            split_lo(CHUNK_N0 + 5)
            for t in range(NT):
                dve.wait_ge(S["gg_ev"], t + 1)
                dve.tensor_tensor(gg[:, t, :].rearrange("p (h d) -> p h d", h=GLA_H), gg[:, t, :].rearrange("p (h d) -> p h d", h=GLA_H),
                                  nw[:, :].unsqueeze(1).to_broadcast([P, GLA_H, GLA_DV]), ALU.mult).then_inc(S["ggs_ok"], 1)
                if t in (1, 3, 5):
                    split_lo(CHUNK_N0 + 6 + t // 2)

            for t in range(NT + 1):
                if t < NT:
                    dve.wait_ge(S["sc_ps"], t + 1)
                    if t >= 1:
                        dve.wait_ge(S["o_ps"], t)
                    dve.tensor_tensor(sT[:, :, :, :], sc_banks,
                                      trimask[:, :].unsqueeze(1).unsqueeze(1).to_broadcast([P, 2, 2, P]), ALU.mult).then_inc(S["sT_ok"], 1)
                if t >= 1:
                    c = t - 1
                    dve.wait_ge(S["gsq_ok"], c + 1)
                    dve.tensor_reduce(gms[:, 0:4], gsq[:, :].rearrange("p (h d) -> p h d", h=GLA_H), AX.X, ALU.add)\
                        .then_inc(S["gms_ok"], 1)
                    dve.wait_ge(S["gms_ok"], 2 * c + 1)
                    dve.tensor_scalar(gms[:, 0:4], gms[:, 0:4], 1.0 / GLA_DV, RMS_EPS, ALU.mult, ALU.add).then_inc(S["gms_ok"], 1)
                    dve.wait_ge(S["rstd_ok"], 2 * c + 2)
                    if c >= 1:
                        dve.wait_ge(S["gyT_ps"], c)
                    dve.tensor_tensor(gy[:, :].rearrange("p (h d) -> p h d", h=GLA_H), pa_[:, 0:GLA_W].rearrange("p (h d) -> p h d", h=GLA_H),
                                      gms[:, 4:8].unsqueeze(2).to_broadcast([P, GLA_H, GLA_DV]), ALU.mult).then_inc(S["gs_ok"], 1)
                    dve.wait_ge(S["gs_ok"], c + 1)
                    dve.wait_ge(S["ggs_ok"], c + 1)
                    dve.tensor_tensor(gy[:, :], gy[:, :], gg[:, c, :], ALU.mult).then_inc(S["gy_ok"], 1)
                if t < NT:
                    dve.wait_ge(S["kv_ps"], t + 1)
                    for cc in range(2):
                        ch = 2 * t + cc
                        if ch == T // GLA_C - 1:
                            continue
                        if ch >= 3:
                            dve.wait_ge(S["o_ps"], (ch - 3) // 2 + 1)
                        if ch >= 1:
                            dve.wait_ge(S["st_ok"], 4 * ch)
                        for hp in range(2):
                            for h in range(2):
                                r = slice(hs[h], hs[h] + 64)
                                c_ = slice(h * GLA_DV, (h + 1) * GLA_DV)
                                dve.scalar_tensor_tensor(S_st[r, hp, (ch + 1) % 4, c_], S_st[r, hp, ch % 4, c_],
                                                         dec[r, hp, ch:ch + 1],
                                                         kv_bank[cc][r, hp * 192 + h * GLA_DV:hp * 192 + (h + 1) * GLA_DV],
                                                         ALU.mult, ALU.add).then_inc(S["st_ok"], 1)
            split_lo(CHUNK_F0)

            def clamp_of(u):
                W = (UNITS[u][1] + 1) * P
                dve.wait_ge(S["z_ps"], u + 1)
                dve.tensor_scalar(E[:, u % 2, 0:W], pz[u % 2][:, 0:W], CLAMP, None, ALU.min).then_inc(S["zc_ok"], 1)

            def conv_step(ct, k):
                y = mix[:, ct, :]
                u_ = conv_in[:, 0, :]
                if k in (0, 4):
                    what = ("ch" if k == 0 else "cb", ct)
                    dve.wait_ge(S["proj_ev"], ev_before(FILL_F0 + 2 * (FILL.index(what) + 1)))
                if k:
                    dve.wait_ge(S["conv_ok"], 5 * ct + k)
                if k == 0:
                    ins = dve.tensor_tensor(u_, u_, conv_in[:, 1, :], ALU.mult)
                elif k == 1:
                    ins = dve.tensor_scalar(y, u_, cw[:, 0, ct:ct + 1], cb[:, ct:ct + 1], ALU.mult, ALU.add)
                elif k < 4:
                    i = k - 1
                    ins = dve.scalar_tensor_tensor(y[:, i:], u_[:, :T - i], cw[:, i, ct:ct + 1], y[:, i:], ALU.mult, ALU.add)
                else:
                    ins = dve.tensor_tensor(y, y, conv_in[:, 2, :], ALU.mult)
                ins.then_inc(S["conv_ok"], 1)

            def softplus_max(u):
                W = (UNITS[u][1] + 1) * P
                dve.wait_ge(S["ln_ok"], u + 1)
                if u >= 2:
                    dve.wait_ge(S["aT_ps"], HALVES[u - 1])
                dve.tensor_tensor(SP[:, u % 2, 0:W], pz[u % 2][:, 0:W], E[:, u % 2, 0:W], ALU.max).then_inc(S["sp_ok"], 1)

            def arg_of(u):
                W = (UNITS[u][1] + 1) * P
                dve.wait_ge(S["spm_ok"], u + 1)
                dve.tensor_tensor_scan(E[:, u % 2, 0:W][:, ::-1], SP[:, u % 2, 0:W][:, ::-1], SP[:, u % 2, 0:W][:, ::-1], 0.0,
                                       ALU.add, ALU.max).then_inc(S["sfx_ok"], 1)
                dve.wait_ge(S["sfx_ok"], u + 1)
                dve.tensor_tensor(SP[:, u % 2, 0:W], pz[u % 2][:, 0:W], E[:, u % 2, 0:W], ALU.subtract).then_inc(S["arg_ok"], 1)

            def split_wo_lo(k):
                dve.wait_ge(S["wo_hi_ok"], k + 1)
                dve.tensor_tensor(wo_lo[:, k, :], wo_raw[:, k % 2, :], wo_hi[:, k, :].bitcast(F32), ALU.subtract).then_inc(S["wo_lo_ok"], 1)

            clamp_of(0)
            clamp_of(1)
            softplus_max(0)
            arg_of(0)
            for u, (p, i, h) in enumerate(UNITS):
                if u + 1 < NU:
                    softplus_max(u + 1)
                if u + 2 < NU:
                    clamp_of(u + 2)
                if u + 1 < NU:
                    arg_of(u + 1)
                q = QUARTER.get(u - 1, 1)
                if q % 4 == 0 and q // 4 + 1 < len(FILL):
                    split_lo(CHUNK_F0 + q // 4 + 1)
                if u in CONV_STEP:
                    conv_step(*CONV_STEP[u])
                if u >= NU - 4:
                    split_wo_lo(2 * (u - NU + 4))
                    split_wo_lo(2 * (u - NU + 4) + 1)
            def mix_lo(i):
                dve.wait_ge(S["mixh_ok"], i + 1)
                dve.tensor_tensor(mixl[:, i % 2, :, :], mix[:, :, i * P:(i + 1) * P], mixh[:, i % 2, :, :].bitcast(F32), ALU.subtract)\
                    .then_inc(S["mixl_ok"], 1)
            mix_lo(0)
            for i in range(NT):
                if i + 1 < NT:
                    mix_lo(i + 1)
                s = i % 2
                dve.wait_ge(S[f"xr_in{s}"], 16 * (i // 2 + 1))
                if i >= 2:
                    dve.wait_ge(S[f"x1_st{s}"], 16 * (i // 2))
                    dve.wait_ge(S["x1t_ps"], i - 1)
                for half in range(2):
                    hsl = slice(half * 512, half * 512 + 512)
                    dve.wait_ge(S["ob_ps"], 2 * i + half + 1)
                    dve.scalar_tensor_tensor(x1[:, s, hsl], xres[:, s, hsl], ALPHA, ob[s][half], ALU.mult, ALU.add).then_inc(S["res_ok"], 1)
                norm_stats(dve, x1, s, "res_ok", 2 * i + 2, "bn_ok", i, "lrs_ok")
                dve.wait_ge(S["lrs_ok"], 2 * i + 2)
                dve.tensor_scalar(x1[:, s, :], x1[:, s, :], bna[:, 0:1], rst[:, 1:2], ALU.subtract, ALU.mult).then_inc(S["x1_ok"], 1)
                if i == 0:
                    dve.wait_ge(S["lnp_in"], 16 * 4)
                for a, op in ((0, ALU.mult), (1, ALU.add)):
                    dve.wait_ge(S["x1_ok"], 3 * i + a + 1)
                    dve.tensor_tensor(x1[:, s, :], x1[:, s, :], lnp[:, a, :], op).then_inc(S["x1_ok"], 1)

            step = [0]

            def link(ins):
                step[0] += 1
                ins.then_inc(S["route_step"], 1)
                dve.wait_ge(S["route_step"], step[0])

            def grp(t_):
                return t_[:, :, :].rearrange("p i (g j) -> p (i g) j", j=EPG)

            bc = lambda t_, n: t_.unsqueeze(1).to_broadcast([P, n, t_.shape[-1]])
            dve.wait_ge(S["rexp_ok"], 1)
            dve.wait_ge(S["tokc_ok"], 8)
            dve.wait_ge(S["mixl_ok"], NT)
            link(dve.tensor_scalar(rs[:, :, :], rs[:, :, :], 1.0, None, ALU.add))
            link(dve.reciprocal(rs[:, :, :], rs[:, :, :]))
            link(dve.tensor_tensor(rsel[:, :, :].rearrange("p (i g) j -> p i (g j)", g=NGRP), rs[:, :, :], bc(rb[:, :], NT), ALU.add))
            dve.tensor_tensor(rpair[:, :, 0:3], rsel[:, :, 0:3], rsel[:, :, 1:4], ALU.add).then_inc(S["route_step"], 1)
            dve.tensor_tensor(rpair[:, :, 3:5], rsel[:, :, 0:2], rsel[:, :, 2:4], ALU.add).then_inc(S["route_step"], 1)
            step[0] += 2
            link(dve.tensor_tensor(rpair[:, :, 5:6], rsel[:, :, 0:1], rsel[:, :, 3:4], ALU.add))
            link(dve.tensor_reduce(rgs[:, :, :].rearrange("p i g -> p (i g)"), rpair[:, :, :], AX.X, ALU.max))

            def ranks(v, r, n):
                link(dve.tensor_copy(r, bc(rank0[:, :], n)))
                for d in range(1, EPG):
                    m = EPG - d
                    ge = rge[:, 0:n, 0:m]
                    link(dve.tensor_tensor(ge, v[:, :, 0:m], v[:, :, d:EPG], ALU.is_ge))
                    link(dve.tensor_tensor(r[:, :, d:EPG], r[:, :, d:EPG], ge, ALU.add))
                    link(dve.tensor_tensor(r[:, :, 0:m], r[:, :, 0:m], ge, ALU.subtract))
            ranks(rgs[:, :, :], rgk[:, :, :], NT)
            ranks(rsel[:, :, :], rek[:, :, :], NT * NGRP)
            link(dve.tensor_scalar(rgk[:, :, :], rgk[:, :, :], 0.0, None, ALU.is_equal))
            link(dve.scalar_tensor_tensor(grp(rmask), rek[:, :, :], 2.0,
                                          rgk[:, :, :].rearrange("p i g -> p (i g)").unsqueeze(2).to_broadcast([P, NT * NGRP, EPG]),
                                          ALU.is_lt, ALU.mult))
            dve.tensor_copy(rmb[:, :, :], rmask[:, :, :]).then_inc(S["mask_ok"], 1)
            link(dve.tensor_tensor(rgate[:, :, :], rs[:, :, :], rmask[:, :, :], ALU.mult))
            link(dve.tensor_reduce(rden[:, :], rgate[:, :, :], AX.X, ALU.add))
            link(dve.reciprocal(rden[:, :], rden[:, :]))
            link(dve.tensor_tensor(rgate[:, :, :], rgate[:, :, :], rden[:, :].unsqueeze(2).to_broadcast([P, NT, NE]), ALU.mult))
            dve.wait_ge(S["pos_ps"], 1)
            link(dve.tensor_copy(rpos[:, :, :], po[:, 0:(NT + 1) * NE].rearrange("p (i e) -> p i e", e=NE)))
            link(dve.tensor_reduce(rmax[:, :], rpos[:, NT, :], AX.X, ALU.max))
            link(dve.tensor_scalar(pcmp[:, :], passes[:, :], rmax[:, 0:1], None, ALU.is_lt))
            link(dve.tensor_reduce(rnp[:, :], pcmp[:, :], AX.X, ALU.add))
            dve.tensor_scalar(npi[:, :], rnp[:, :], 1.0, None, ALU.add).then_inc(S["route_ok"], 1)
            link(dve.tensor_scalar(rtmp[:, :, :], rpos[:, 0:NT, :], float(TW), None, ALU.is_ge))
            for j in range(2, MAXPASS):
                link(dve.scalar_tensor_tensor(rtmp[:, :, :], rpos[:, 0:NT, :], float(j * TW), rtmp[:, :, :], ALU.is_ge, ALU.add))
            link(dve.tensor_tensor(rrow[:, :, :], rpos[:, 0:NT, :], bc(ecol[:, :], NT), ALU.add))
            link(dve.scalar_tensor_tensor(rrow[:, :, :], rtmp[:, :, :], float((NE - 1) * TW), rrow[:, :, :], ALU.mult, ALU.add))
            link(dve.scalar_tensor_tensor(rtmp[:, :, :], rrow[:, :, :], -BIG, rmask[:, :, :], ALU.add, ALU.mult))
            link(dve.tensor_reduce(rr12[:, 0, :], rtmp[:, :, :], AX.X, ALU.min))
            link(dve.tensor_scalar(rr12[:, 0, :], rr12[:, 0, :], BIG, None, ALU.add))
            dve.tensor_copy(rows_u[:, 0, :], rr12[:, 0, :]).then_inc(S["route_ok"], 1)
            link(dve.scalar_tensor_tensor(rtmp[:, :, :], rrow[:, :, :], 1.0, rmask[:, :, :], ALU.add, ALU.mult))
            link(dve.tensor_reduce(rr12[:, 1, :], rtmp[:, :, :], AX.X, ALU.max))
            link(dve.tensor_scalar(rr12[:, 1, :], rr12[:, 1, :], -1.0, None, ALU.add))
            dve.tensor_copy(rows_u[:, 1, :], rr12[:, 1, :]).then_inc(S["route_ok"], 1)
            for c in range(2):
                link(dve.tensor_tensor(rtmp[:, :, :], rrow[:, :, :], rr12[:, c, :].unsqueeze(2).to_broadcast([P, NT, NE]), ALU.is_equal))
                link(dve.tensor_tensor(rtmp[:, :, :], rtmp[:, :, :], rgate[:, :, :], ALU.mult))
                link(dve.tensor_reduce(g12[:, c, :], rtmp[:, :, :], AX.X, ALU.add))

            def piece_lo(b, p):
                dve.wait_ge(S["eh_ok"], NPIECE * b + p + 1)
                dve.tensor_tensor(el[:, p, :], er[:, p, :], eh[:, p, :].bitcast(F32), ALU.subtract).then_inc(S["el_ok"], 1)

            def x_lo(b, rounds=range(4)):
                for r in rounds:
                    dve.wait_ge(S["xTh_ok"], 4 * b + r + 1)
                    dve.tensor_tensor(xT2[:, 2 * r:2 * r + 2, 1, :], xb[r % 2].rearrange("p (d t) -> p d t", d=2),
                                      xT2[:, 2 * r:2 * r + 2, 0, :].bitcast(F32), ALU.subtract).then_inc(S["xTl_ok"], 1)

            def dve_block(b, nxt):
                for f in range(NF):
                    dve.wait_ge(S["cross_ok"], 4 * b + f + 1)
                    if f >= 2 or not first_block(b):
                        dve.wait_ge(S["h_ok"], 4 * b + f - 1)
                    dve.tensor_tensor(gu[:, f % 2, :, :], pz[f % 2][:, :].rearrange("p (w c) -> p w c", w=2)[:, :, 0:TW],
                                      cross[:, f % 2, :, :], ALU.add).then_inc(S["sum_ok"], 1)
                    if nxt and f < NF - 1:
                        piece_lo(b + 1, 2 * f)
                    dve.wait_ge(S["sil_ok"], 4 * b + f + 1)
                    dve.tensor_tensor(hf[:, f, :], sil[:, f % 2, :], gu[:, f % 2, 1, :], ALU.mult).then_inc(S["h_ok"], 1)
                    if nxt and f < NF - 1:
                        piece_lo(b + 1, 2 * f + 1)
                    dve.wait_ge(S["hh_ok"], 4 * b + f + 1)
                    dve.tensor_tensor(h2[:, f, TW + TR:], hf[:, f, 0:P], h2[:, f, 0:P].bitcast(F32), ALU.subtract)
                    dve.tensor_tensor(h2[:, f, TW:TW + TR], hf[:, f, P:], h2[:, f, P:TW].bitcast(F32), ALU.subtract).then_inc(S["hl_ok"], 1)
                if nxt:
                    x_lo(b + 1, (0, 1))
                    piece_lo(b + 1, 2 * NF - 2)
                    piece_lo(b + 1, 2 * NF - 1)
                    x_lo(b + 1, (2, 3))
                dve.wait_ge(S["rowsA_ps"], 2 * b + 1)
                if not first_block(b):
                    dve.wait_ge(S["y_out"], 32 * b)
                dve.tensor_copy(yA[:, 0:512], pp[0][:, :]).then_inc(S["yA0_ev"], 1)
                if nxt:
                    for p in range(2 * NF, NPIECE - 1):
                        piece_lo(b + 1, p)
                for half in range(2):
                    dve.wait_ge(S["yBl_ok"], 2 * b + half + 1)
                    dve.tensor_tensor(yB[:, half * 512:half * 512 + 512], pz[1][0:TR, half * 512:half * 512 + 512],
                                      yBl[:, half * 512:half * 512 + 512], ALU.add).then_inc(S["yB_ev"], 1)
                if nxt:
                    piece_lo(b + 1, NPIECE - 1)

            def dve_pass(j):
                b0 = NE * j
                for p in range(NPIECE):
                    piece_lo(b0, p)
                    if p == 5:
                        x_lo(b0)
                experts_of(dve, j, dve_block)
            passes_of(dve, dve_pass)

            for i in range(NT + 1):
                if i >= 1:
                    c = i - 1
                    dve.wait_ge(S["clr_ok"], 2 * c + 2)
                    dve.scalar_tensor_tensor(crs[:, c, 1:2], cmv[:, c, 0:1], -1.0, crs[:, c, 0:1], ALU.mult, ALU.mult).then_inc(S["cnb_ok"], 1)
                if i < NT:
                    dve.wait_ge(S["c1_ok"], i + 1)
                    dve.scalar_tensor_tensor(cy1[:, i, :], cy2[:, i, :], g12[:, 1, i:i + 1], cy1[:, i, :], ALU.mult, ALU.add).then_inc(S["c2_ok"], 1)
                    dve.wait_ge(S["c2_ok"], i + 1)
                    dve.wait_ge(S[f"cx_in{i}"], 16)
                    dve.scalar_tensor_tensor(cx[:, i, :], cx[:, i, :], ALPHA, cy1[:, i, :], ALU.mult, ALU.add).then_inc(S["cres_ok"], 1)
                    dve.wait_ge(S["cres_ok"], i + 1)
                    for h in range(2):
                        dve.bn_stats(cstat[:, i, h, :], cx[:, i, h * 512:h * 512 + 512]).then_inc(S["cbn_ok"], 1)
                if i >= 1:
                    if c == 0:
                        dve.wait_ge(S["lnq_in"], 32)
                    dve.wait_ge(S["cnorm_ok"], c + 1)
                    if c not in POOL_GAIN:
                        dve.tensor_tensor(cx[:, c, :], cx[:, c, :], lnq[:, 0, :], ALU.mult).then_inc(S["cout_ok"], 1)
                    if c == NT - 1:
                        dve.wait_ge(S["cout_ok"], NT - len(POOL_GAIN))
                        dve.tensor_tensor(cx[:, c, :], cx[:, c, :], lnq[:, 1, :], ALU.add).then_inc(S["clast_ok"], 1)
                if i < NT:
                    dve.wait_ge(S["cbn_ok"], 4 * i + 2)
                    dve.bn_aggr(cmv[:, i, :], cstat[:, i, :, :].rearrange("p a b -> p (a b)")).then_inc(S["cbn_ok"], 1)
                    dve.wait_ge(S["cbn_ok"], 4 * i + 3)
                    dve.tensor_scalar(cmv[:, i, 1:2], cmv[:, i, 1:2], LN_EPS, None, ALU.add).then_inc(S["cbn_ok"], 1)


_INS = ["x", "w_in", "conv_w", "conv_b", "gla_w_gate2", "gla_b_gate", "gla_norm_w", "w_out", "ln1_g", "ln1_b",
        "router_w", "router_bias", "w1", "w3", "w2", "ln2_g", "ln2_b"]


def kernel(**inputs):
    import numpy as np
    import concourse.bacc as bacc
    from concourse.bass_utils import run_bass_kernel_spmd

    nc = bacc.Bacc("TRN2", target_bir_lowering=False, num_devices=1)
    arrays, aps = {}, {}
    for name in _INS:
        a = np.ascontiguousarray(inputs[name])
        arrays[f"in_{name}_dram"] = a
        aps[name] = nc.dram_tensor(f"in_{name}_dram", a.shape, mybir.dt.from_np(a.dtype), kind="ExternalInput").ap()
    out = nc.dram_tensor("out_0_dram", (1, T, D), F32, kind="ExternalOutput").ap()
    build(nc, aps, out)
    r = run_bass_kernel_spmd(nc, [arrays], core_ids=[0])
    return r.results[0]["out_0_dram"]
```
